# Optimizing a Trainium2 kernel written in Bass

```python
import jax, jax.numpy as jnp
from jax import lax
import numpy as np
import math

D_MODEL = 1024
BATCH = 1
SEQ = 1024
DEPTH = 1

CHUNK = 64
Q_BLOCK = 128
SB_HEAD_DIM = 64
SB_HEADS = (D_MODEL // 2) // SB_HEAD_DIM
SB_WIDTH = SB_HEADS * SB_HEAD_DIM
GLA_HEADS = 4
GLA_DV = (D_MODEL // 2) // GLA_HEADS
GLA_DK = GLA_DV // 2
GLA_VWIDTH = GLA_HEADS * GLA_DV
GLA_KWIDTH = GLA_HEADS * GLA_DK
GLA_GATE_RANK = 16
GLA_TAU = 16.0
MIX_WIDTH = SB_WIDTH + GLA_VWIDTH
D_FF = 2816
CONV_WIDTH = 3
N_MOD = 6
EPS = 1e-6
IN_SPLITS = (SB_WIDTH, SB_WIDTH, SB_WIDTH,
             GLA_KWIDTH, GLA_KWIDTH, GLA_VWIDTH,
             GLA_VWIDTH, GLA_GATE_RANK)
IN_WIDTH = sum(IN_SPLITS)


def rms_norm(x, gain):
    xf = x.astype(jnp.float32)
    n = xf * lax.rsqrt(jnp.mean(xf * xf, axis=-1, keepdims=True) + EPS)
    return (n * gain.astype(jnp.float32)).astype(x.dtype)

def modulate(h, shift, scale):
    return h * (1 + scale[:, None, :]) + shift[:, None, :]

def stick_breaking_attention(q, k, v):
    B, S, H, d = q.shape
    q = q.transpose(0, 2, 1, 3)
    k = k.transpose(0, 2, 1, 3)
    v = v.transpose(0, 2, 1, 3)
    scale = d ** -0.5
    outs = []
    for i in range(S // Q_BLOCK):
        start = i * Q_BLOCK
        end = start + Q_BLOCK
        qb = q[:, :, start:end]
        kb = k[:, :, :end]
        vb = v[:, :, :end]
        z = jnp.einsum('bhqd,bhkd->bhqk', qb, kb).astype(jnp.float32) * scale
        t_pos = start + jnp.arange(Q_BLOCK)
        s_pos = jnp.arange(end)
        mask = s_pos[None, :] < t_pos[:, None]
        log_one_minus = jnp.where(mask, jax.nn.log_sigmoid(-z), 0.0)
        shifted = jnp.concatenate(
            [log_one_minus[..., 1:], jnp.zeros_like(log_one_minus[..., :1])], axis=-1)
        between = lax.cumsum(shifted, axis=3, reverse=True)
        weights = jnp.where(mask, jnp.exp(jax.nn.log_sigmoid(z) + between), 0.0)
        outs.append(jnp.einsum('bhqk,bhkd->bhqd', weights.astype(vb.dtype), vb))
    o = jnp.concatenate(outs, axis=2)
    return o.transpose(0, 2, 1, 3).reshape(B, S, H * d)

def gla_chunk_causal(q, k, v, log_alpha):
    B, S, H, dk = q.shape
    dv = v.shape[-1]
    nc = S // CHUNK
    qc = q.reshape(B, nc, CHUNK, H, dk).astype(jnp.float32) * (dk ** -0.5)
    kc = k.reshape(B, nc, CHUNK, H, dk).astype(jnp.float32)
    vc = v.reshape(B, nc, CHUNK, H, dv).astype(jnp.float32)
    la = log_alpha.reshape(B, nc, CHUNK, H, dk).astype(jnp.float32)
    cum = jnp.cumsum(la, axis=2)
    total = cum[:, :, -1]
    k_dec = kc * jnp.exp(total[:, :, None] - cum)
    chunk_kv = jnp.einsum('bnchk,bnchv->nbhkv', k_dec, vc)
    chunk_decay = jnp.exp(total).transpose(1, 0, 2, 3)

    def step(state, inp):
        decay, kv = inp
        state = decay[..., None] * state + kv
        return state, state

    s0 = jnp.zeros((B, H, dk, dv), jnp.float32)
    _, states = lax.scan(step, s0, (chunk_decay, chunk_kv))
    o = jnp.einsum('bnchk,nbhkv->bnchv', qc, states)
    return o.reshape(B, S, H * dv)

def causal_depthwise_conv(u, w, b):
    S = u.shape[1]
    up = jnp.pad(u, ((0, 0), (CONV_WIDTH - 1, 0), (0, 0)))
    out = b
    for j in range(CONV_WIDTH):
        out = out + w[j] * up[:, j:j + S]
    return out

def first_inputs(seed: int = 0) -> dict:
    key = jax.random.key(seed)
    ks = jax.random.split(key, 18)

    def nrm(k, shape, scale):
        return jax.random.normal(k, shape, jnp.float32) * scale

    L, D = DEPTH, D_MODEL
    return {
        "x": nrm(ks[0], (BATCH, SEQ, D), 1.0),
        "c": nrm(ks[1], (BATCH, D), 1.0),
        "w_ada": nrm(ks[2], (L, D, N_MOD * D), 0.5 * D ** -0.5),
        "b_ada": nrm(ks[3], (L, N_MOD * D), 0.01),
        "g_norm1": 1.0 + nrm(ks[4], (L, D), 0.02),
        "w_in": nrm(ks[5], (L, D, IN_WIDTH), D ** -0.5),
        "w_fg2": nrm(ks[6], (L, GLA_GATE_RANK, GLA_KWIDTH), GLA_GATE_RANK ** -0.5),
        "b_fg2": nrm(ks[7], (L, GLA_KWIDTH), 0.1),
        "g_gla_out": 1.0 + nrm(ks[8], (L, GLA_VWIDTH), 0.02),
        "w_out": nrm(ks[9], (L, MIX_WIDTH, D), MIX_WIDTH ** -0.5),
        "g_norm2": 1.0 + nrm(ks[10], (L, D), 0.02),
        "w_up": nrm(ks[11], (L, D, 2 * D_FF), D ** -0.5),
        "w_conv": nrm(ks[12], (L, CONV_WIDTH, 2 * D_FF), CONV_WIDTH ** -0.5),
        "b_conv": nrm(ks[13], (L, 2 * D_FF), 0.01),
        "w_down": nrm(ks[14], (L, D_FF, D), D_FF ** -0.5),
        "g_final": 1.0 + nrm(ks[15], (D,), 0.02),
    }

def first_block(x, c, w_ada, b_ada, g_norm1, w_in, w_fg2, b_fg2, g_gla_out, w_out,
              g_norm2, w_up, w_conv, b_conv, w_down, g_final):
    B, S, _ = x.shape
    offsets = np.cumsum(IN_SPLITS)[:-1].tolist()
    for l in range(DEPTH):
        mod = jax.nn.silu(c) @ w_ada[l] + b_ada[l]
        shift1, scale1, gate1, shift2, scale2, gate2 = jnp.split(mod, N_MOD, axis=-1)

        h = modulate(rms_norm(x, g_norm1[l]), shift1, scale1)
        proj = h @ w_in[l]
        sb_q, sb_k, sb_v, gq, gk, gv, gg, gf = jnp.split(proj, offsets, axis=-1)

        o_sb = stick_breaking_attention(
            sb_q.reshape(B, S, SB_HEADS, SB_HEAD_DIM),
            sb_k.reshape(B, S, SB_HEADS, SB_HEAD_DIM),
            sb_v.reshape(B, S, SB_HEADS, SB_HEAD_DIM))

        log_alpha = jax.nn.log_sigmoid(
            (gf @ w_fg2[l] + b_fg2[l]).astype(jnp.float32)) / GLA_TAU
        o_gla = gla_chunk_causal(
            gq.reshape(B, S, GLA_HEADS, GLA_DK),
            gk.reshape(B, S, GLA_HEADS, GLA_DK),
            gv.reshape(B, S, GLA_HEADS, GLA_DV),
            log_alpha.reshape(B, S, GLA_HEADS, GLA_DK))
        oh = o_gla.reshape(B, S, GLA_HEADS, GLA_DV)
        oh = oh * lax.rsqrt(jnp.mean(oh * oh, axis=-1, keepdims=True) + EPS)
        o_gla = (oh.reshape(B, S, GLA_VWIDTH) * g_gla_out[l].astype(jnp.float32)
                 ).astype(x.dtype) * jax.nn.silu(gg)

        mixed = jnp.concatenate([o_sb.astype(x.dtype), o_gla], axis=-1) @ w_out[l]
        x = x + (1 + gate1[:, None, :]) * mixed

        h2 = modulate(rms_norm(x, g_norm2[l]), shift2, scale2)
        u = causal_depthwise_conv(h2 @ w_up[l], w_conv[l], b_conv[l])
        val, gte = jnp.split(u, 2, axis=-1)
        x = x + (1 + gate2[:, None, :]) * ((val * jax.nn.silu(gte)) @ w_down[l])
    return rms_norm(x, g_final)


HEAD_DIM = 64
SWA_HEADS = 8
SWA_KV_HEADS = 2
SWA_WINDOW = 128
DSA_HEADS = 8
DSA_KV_RANK = 128
IDX_HEADS = 8
IDX_DIM = 64
IDX_TOPK_MAX = 256
DSA_QBLOCK = 128
REL_BUCKETS = 32
REL_MAX_DIST = 128
N_SELF_HEADS = SWA_HEADS + DSA_HEADS
MEM_LEN = 256
MEM_HEADS = 4
MEM_HEAD_DIM = D_MODEL // MEM_HEADS
D_FF_2 = 4 * D_MODEL
DN_ALPHA = (2.0 * DEPTH) ** 0.25
DN_BETA = (8.0 * DEPTH) ** -0.25
LN_EPS = 1e-5
NEG_INF = -1e30
IN_SPLITS_2 = (SWA_HEADS * HEAD_DIM,
             SWA_KV_HEADS * HEAD_DIM,
             SWA_KV_HEADS * HEAD_DIM,
             DSA_HEADS * HEAD_DIM,
             DSA_KV_RANK,
             IDX_HEADS * IDX_DIM,
             IDX_DIM,
             IDX_HEADS)
D_IN = sum(IN_SPLITS_2)
MIX_WIDTH_2 = (SWA_HEADS + DSA_HEADS) * HEAD_DIM


def layer_norm(x, g, b):
    xf = x.astype(jnp.float32)
    mu = jnp.mean(xf, axis=-1, keepdims=True)
    var = jnp.mean(jnp.square(xf - mu), axis=-1, keepdims=True)
    return ((xf - mu) * lax.rsqrt(var + LN_EPS) * g.astype(jnp.float32) + b.astype(jnp.float32)).astype(x.dtype)

def rms_norm_2(x, g):
    xf = x.astype(jnp.float32)
    ms = jnp.mean(jnp.square(xf), axis=-1, keepdims=True)
    return (xf * lax.rsqrt(ms + LN_EPS) * g.astype(jnp.float32)).astype(x.dtype)

def rel_bucket(dist):
    n = jnp.maximum(dist, 0)
    max_exact = REL_BUCKETS // 2
    nf = jnp.maximum(n, 1).astype(jnp.float32)
    large = max_exact + (jnp.log(nf / max_exact) / math.log(REL_MAX_DIST / max_exact)
                         * (REL_BUCKETS - max_exact)).astype(jnp.int32)
    large = jnp.minimum(large, REL_BUCKETS - 1)
    return jnp.where(n < max_exact, n, large)

def swa_sink_attention(q, k, v, sinks, rel_table):
    B, T, Hq, dh = q.shape
    W = SWA_WINDOW
    nb = T // W
    Hkv = SWA_KV_HEADS
    G = Hq // Hkv
    qb = q.reshape(B, nb, W, Hkv, G, dh)

    def band_blocks(z):
        zp = jnp.pad(z, ((0, 0), (W, 0), (0, 0), (0, 0)))
        prev = zp[:, :T].reshape(B, nb, W, Hkv, dh)
        cur = z.reshape(B, nb, W, Hkv, dh)
        return jnp.concatenate([prev, cur], axis=2)

    kb = band_blocks(k)
    vb = band_blocks(v)
    s = jnp.einsum('bnqkgd,bnskd->bnkgqs', qb, kb,
                   preferred_element_type=jnp.float32) * (dh ** -0.5)
    qi = jnp.arange(W)[:, None]
    si = jnp.arange(2 * W)[None, :]
    rel = qi + W - si
    band = (rel >= 0) & (rel < W)
    has_prev = (jnp.arange(nb) > 0)[:, None, None] | (si >= W)[None]
    valid = band[None] & has_prev
    bias = rel_table[rel_bucket(rel)].astype(jnp.float32)
    bias = jnp.transpose(bias, (2, 0, 1)).reshape(Hkv, G, W, 2 * W)
    logits = jnp.where(valid[None, :, None, None, :, :], s + bias, NEG_INF)
    sink = sinks.astype(jnp.float32).reshape(Hkv, G)[:, :, None, None]
    m = jnp.maximum(jnp.max(logits, axis=-1, keepdims=True), sink)
    p = jnp.exp(logits - m)
    denom = jnp.sum(p, axis=-1, keepdims=True) + jnp.exp(sink - m)
    o = jnp.einsum('bnkgqs,bnskd->bnqkgd', (p / denom).astype(v.dtype), vb)
    return o.reshape(B, T, Hq * dh)

def dsa_attention(q, c_kv, iq, ik, iw, w_uk, w_uv, rel_table):
    B, T, H, dh = q.shape
    topk = min(IDX_TOPK_MAX, T // 4)
    QB = DSA_QBLOCK
    nb = T // QB
    q_lat = jnp.einsum('bthd,hcd->bthc', q, w_uk) * (dh ** -0.5)
    key_pos = jnp.arange(T)

    def to_blocks(z):
        return jnp.moveaxis(z.reshape(B, nb, QB, *z.shape[2:]), 1, 0)

    def block(args):
        ql, iqb, iwb, n = args
        t = n * QB + jnp.arange(QB)
        dots = jnp.einsum('bqhd,bsd->bqhs', iqb, ik,
                          preferred_element_type=jnp.float32) * (IDX_DIM ** -0.5)
        score = jnp.einsum('bqh,bqhs->bqs', iwb.astype(jnp.float32), jax.nn.relu(dots))
        causal = key_pos[None, :] <= t[:, None]
        score = jnp.where(causal[None], score, NEG_INF)
        _, idx = lax.top_k(score, topk)
        ok = idx <= t[None, :, None]
        sel = jax.vmap(lambda c, i: c[i])(c_kv, idx)
        logits = jnp.einsum('bqhc,bqkc->bhqk', ql, sel, preferred_element_type=jnp.float32)
        bias = rel_table[rel_bucket(t[None, :, None] - idx)].astype(jnp.float32)
        logits = jnp.where(ok[:, None], logits + jnp.moveaxis(bias, 3, 1), NEG_INF)
        p = jax.nn.softmax(logits, axis=-1).astype(sel.dtype)
        o_lat = jnp.einsum('bhqk,bqkc->bqhc', p, sel)
        return jnp.einsum('bqhc,hcd->bqhd', o_lat, w_uv)

    out = lax.map(block, (to_blocks(q_lat), to_blocks(iq), to_blocks(iw), jnp.arange(nb)))
    return jnp.moveaxis(out, 0, 1).reshape(B, T, H * dh)

def memory_cross_attention(x, mem, wq, bq, wkv, bkv, wo, bo):
    B, T, _ = x.shape
    M = mem.shape[1]
    q = (x @ wq + bq).reshape(B, T, MEM_HEADS, MEM_HEAD_DIM)
    kv = mem @ wkv + bkv
    k, v = jnp.split(kv, 2, axis=-1)
    k = k.reshape(B, M, MEM_HEADS, MEM_HEAD_DIM)
    v = v.reshape(B, M, MEM_HEADS, MEM_HEAD_DIM)
    s = jnp.einsum('bthd,bmhd->bhtm', q, k, preferred_element_type=jnp.float32) * (MEM_HEAD_DIM ** -0.5)
    p = jax.nn.softmax(s, axis=-1).astype(v.dtype)
    o = jnp.einsum('bhtm,bmhd->bthd', p, v).reshape(B, T, D_MODEL)
    return o @ wo + bo

def second_inputs(seed: int = 0) -> dict:
    key = jax.random.key(seed)
    ks = jax.random.split(key, 40)
    f32 = jnp.float32

    def w(k, shape, fan_in, scale=1.0):
        return jax.random.normal(k, shape, f32) * (fan_in ** -0.5) * scale

    def gain(k, shape):
        return 1.0 + 0.05 * jax.random.normal(k, shape, f32)

    def small(k, shape):
        return 0.01 * jax.random.normal(k, shape, f32)

    L = DEPTH
    return {
        "x": jax.random.normal(ks[0], (BATCH, SEQ, D_MODEL), f32),
        "mem": jax.random.normal(ks[1], (BATCH, MEM_LEN, D_MODEL), f32),
        "ln_emb_g": gain(ks[2], (D_MODEL,)),
        "ln_emb_b": small(ks[3], (D_MODEL,)),
        "w_in": w(ks[4], (L, D_MODEL, D_IN), D_MODEL),
        "b_in": small(ks[5], (L, D_IN)),
        "swa_sinks": 0.5 * jax.random.normal(ks[6], (L, SWA_HEADS), f32),
        "dsa_kv_norm_g": gain(ks[7], (L, DSA_KV_RANK)),
        "dsa_w_uk": w(ks[8], (L, DSA_HEADS, DSA_KV_RANK, HEAD_DIM), DSA_KV_RANK),
        "dsa_w_uv": w(ks[9], (L, DSA_HEADS, DSA_KV_RANK, HEAD_DIM), DSA_KV_RANK),
        "idx_k_ln_g": gain(ks[10], (L, IDX_DIM)),
        "idx_k_ln_b": small(ks[11], (L, IDX_DIM)),
        "rel_bias": 0.5 * jax.random.normal(ks[12], (REL_BUCKETS, N_SELF_HEADS), f32),
        "w_o": w(ks[13], (L, MIX_WIDTH_2, D_MODEL), MIX_WIDTH_2, DN_BETA),
        "b_o": small(ks[14], (L, D_MODEL)),
        "ln1_g": gain(ks[15], (L, D_MODEL)),
        "ln1_b": small(ks[16], (L, D_MODEL)),
        "xa_wq": w(ks[17], (L, D_MODEL, D_MODEL), D_MODEL),
        "xa_bq": small(ks[18], (L, D_MODEL)),
        "xa_wkv": w(ks[19], (L, D_MODEL, 2 * D_MODEL), D_MODEL),
        "xa_bkv": small(ks[20], (L, 2 * D_MODEL)),
        "xa_wo": w(ks[21], (L, D_MODEL, D_MODEL), D_MODEL, DN_BETA),
        "xa_bo": small(ks[22], (L, D_MODEL)),
        "ln2_g": gain(ks[23], (L, D_MODEL)),
        "ln2_b": small(ks[24], (L, D_MODEL)),
        "w_up": w(ks[25], (L, D_MODEL, D_FF_2), D_MODEL),
        "b_up": small(ks[26], (L, D_FF_2)),
        "w_down": w(ks[27], (L, D_FF_2, D_MODEL), D_FF_2, DN_BETA),
        "b_down": small(ks[28], (L, D_MODEL)),
        "ln3_g": gain(ks[29], (L, D_MODEL)),
        "ln3_b": small(ks[30], (L, D_MODEL)),
    }

def second_block(x, mem, ln_emb_g, ln_emb_b, w_in, b_in, swa_sinks, dsa_kv_norm_g, dsa_w_uk, dsa_w_uv,
              idx_k_ln_g, idx_k_ln_b, rel_bias, w_o, b_o, ln1_g, ln1_b, xa_wq, xa_bq, xa_wkv, xa_bkv,
              xa_wo, xa_bo, ln2_g, ln2_b, w_up, b_up, w_down, b_down, ln3_g, ln3_b):
    B, T, _ = x.shape
    offsets = [int(o) for o in np.cumsum(IN_SPLITS_2)[:-1]]
    rel_a = rel_bias[:, :SWA_HEADS]
    rel_b = rel_bias[:, SWA_HEADS:]
    x = layer_norm(x, ln_emb_g, ln_emb_b)
    for l in range(DEPTH):
        h = x @ w_in[l] + b_in[l]
        qa, ka, va, qb, cb, iq, ik, iw = jnp.split(h, offsets, axis=-1)
        qa = qa.reshape(B, T, SWA_HEADS, HEAD_DIM)
        ka = ka.reshape(B, T, SWA_KV_HEADS, HEAD_DIM)
        va = va.reshape(B, T, SWA_KV_HEADS, HEAD_DIM)
        out_a = swa_sink_attention(qa, ka, va, swa_sinks[l], rel_a)
        qb = qb.reshape(B, T, DSA_HEADS, HEAD_DIM)
        cb = rms_norm_2(cb, dsa_kv_norm_g[l])
        iq = iq.reshape(B, T, IDX_HEADS, IDX_DIM)
        ik = layer_norm(ik, idx_k_ln_g[l], idx_k_ln_b[l])
        iw = iw * (IDX_HEADS ** -0.5)
        out_b = dsa_attention(qb, cb, iq, ik, iw, dsa_w_uk[l], dsa_w_uv[l], rel_b)
        mix = jnp.concatenate([out_a, out_b], axis=-1) @ w_o[l] + b_o[l]
        x = layer_norm(DN_ALPHA * x + mix, ln1_g[l], ln1_b[l])
        ca = memory_cross_attention(x, mem, xa_wq[l], xa_bq[l], xa_wkv[l], xa_bkv[l], xa_wo[l], xa_bo[l])
        x = layer_norm(DN_ALPHA * x + ca, ln2_g[l], ln2_b[l])
        f = jnp.square(jax.nn.relu(x @ w_up[l] + b_up[l])) @ w_down[l] + b_down[l]
        x = layer_norm(DN_ALPHA * x + f, ln3_g[l], ln3_b[l])
    return x


def setup_inputs(seed=0):
    out = dict(first_inputs(seed))
    for name, value in second_inputs(seed + 1).items():
        if name != "x":
            out[name + "_2"] = value
    return out


def reference(
    x, c, w_ada, b_ada, g_norm1, w_in, w_fg2, b_fg2, g_gla_out, w_out, g_norm2, w_up, w_conv,
    b_conv, w_down, g_final, mem_2, ln_emb_g_2, ln_emb_b_2, w_in_2, b_in_2, swa_sinks_2,
    dsa_kv_norm_g_2, dsa_w_uk_2, dsa_w_uv_2, idx_k_ln_g_2, idx_k_ln_b_2, rel_bias_2, w_o_2,
    b_o_2, ln1_g_2, ln1_b_2, xa_wq_2, xa_bq_2, xa_wkv_2, xa_bkv_2, xa_wo_2, xa_bo_2, ln2_g_2,
    ln2_b_2, w_up_2, b_up_2, w_down_2, b_down_2, ln3_g_2, ln3_b_2,
):
    x = first_block(
        x, c, w_ada, b_ada, g_norm1, w_in, w_fg2, b_fg2, g_gla_out, w_out, g_norm2, w_up,
        w_conv, b_conv, w_down, g_final,
    )
    return second_block(
        x, mem_2, ln_emb_g_2, ln_emb_b_2, w_in_2, b_in_2, swa_sinks_2, dsa_kv_norm_g_2,
        dsa_w_uk_2, dsa_w_uv_2, idx_k_ln_g_2, idx_k_ln_b_2, rel_bias_2, w_o_2, b_o_2, ln1_g_2,
        ln1_b_2, xa_wq_2, xa_bq_2, xa_wkv_2, xa_bkv_2, xa_wo_2, xa_bo_2, ln2_g_2, ln2_b_2,
        w_up_2, b_up_2, w_down_2, b_down_2, ln3_g_2, ln3_b_2,
    )


_drawn_inputs = setup_inputs


def setup_inputs(seed=0):
    import zlib

    import numpy as np

    out = dict(_drawn_inputs(seed))
    spreads = {}
    factors = {'g_gla_out': 6.221,
     'g_norm2': 3.825,
     'b_conv': 7.446,
     'ln_emb_b_2': 4.741,
     'b_in_2': 8.0,
     'swa_sinks_2': 59.432,
     'dsa_kv_norm_g_2': 8.0,
     'idx_k_ln_g_2': 8.0,
     'idx_k_ln_b_2': 8.0,
     'b_o_2': 6.518,
     'ln1_b_2': 5.226,
     'xa_bq_2': 64.0,
     'xa_bkv_2': 8.0,
     'xa_bo_2': 6.676,
     'ln2_b_2': 5.478,
     'b_up_2': 8.0,
     'b_down_2': 8.0,
     'ln3_b_2': 5.589}
    for name, (base, spread) in spreads.items():
        noise = np.random.default_rng([zlib.crc32(name.encode()), seed]).standard_normal(out[name].shape)
        drawn = base * np.exp(spread * noise) if base else spread * noise
        out[name] = __import__('jax').numpy.asarray(drawn.astype(out[name].dtype))
    for name, factor in factors.items():
        out[name] = (out[name] * factor).astype(out[name].dtype)
    return out
```

```python
from contextlib import ExitStack

import numpy as np
import concourse.bass as bass
from concourse import mybir
from concourse.alu_op_type import AluOpType as ALU

F = mybir.dt.float32
R = mybir.dt.float32r
U32 = mybir.dt.uint32
I32 = mybir.dt.int32
ACT = mybir.ActivationFunctionType
AX = mybir.AxisListType.X
ds = bass.ds

P = 128
S = 1024
D = 1024
NT = S // P
KT = D // P
CW = 256
NEG = -1e30
EPS = 1e-6
LN_EPS = 1e-5
ALPHA = 2.0 ** 0.25

SB_HEADS, HD = 8, 64
GLA_HEADS, DK, DV, CHUNK = 4, 64, 128, 64
RANK = 16
GATE_TAU = 16.0
NF1 = 2816 // P
F2C = 4096 // CW
SWA_HEADS, SWA_GROUP = 8, 4
DSA_HEADS, DC = 8, 128
TOPK = 256
BUCKETS, MAX_DIST = 32, 128
MEM, MEM_HEADS, MEM_HD = 256, 4, 256
BAND = 384


class Kernel:

    def __init__(self, nc, ctx, dram):
        self.nc, self.ctx, self.dram = nc, ctx, dram
        self.named, self.used_sems = {}, []
        self.psum = ctx.enter_context(nc.psum_tensor("psum", [P, 8 * 512], F))
        self.bank = [self.psum[:, 512 * b:512 * b + 512] for b in range(8)]
        self.x = self.sb(ctx, "residual", [P, NT, D])
        self.ident = self.sb(ctx, "ident", [P, P])
        self.w_raw = [self.sb(ctx, f"w_raw{s}", [P, KT * CW]) for s in range(2)]
        self.w_hi = [self.sb(ctx, f"w_hi{s}", [P, KT * CW], R) for s in range(2)]
        self.w_lo = [self.sb(ctx, f"w_lo{s}", [P, KT * CW], R) for s in range(2)]
        names = ("w_loaded", "w_hi_done", "w_ready", "lin_mm", "lin_evac", "lin_stored")
        self.wsem = {n: [self.sem(f"{n}{s}") for s in range(2)] for n in names}
        self.wbase = {n: [0, 0] for n in names}
        self.used_sems = []

    def sb(self, ctx, name, shape, dt=F):
        self.named[name] = self.named.get(name, 0) + 1
        if self.named[name] > 1:
            name = f"{name}_{self.named[name]}"
        return ctx.enter_context(self.nc.sbuf_tensor(name, shape, dt))

    def sem(self, name):
        handle = self.nc.alloc_semaphore(name=name)
        self.used_sems.append(handle)
        return handle

    def free_sems(self):
        self.nc.clear_and_free_semaphores(self.used_sems)
        self.nc.all_engine_barrier()
        self.used_sems = []

    def is_dram(self, ap):
        return len(ap.shape) == 1

    def scratch(self, name, shape):
        return self.nc.dram_tensor(name, shape, F, kind="Internal").ap()


def rows(ap, n=P):
    return ap.rearrange("(a n) -> a n", a=1).broadcast_to([n, ap.shape[0]])


def looped(e, n, body):
    if n == 1:
        body(0)
    elif n > 1:
        with e.Fori(0, n) as i:
            body(i)



def setup(k):
    nc = k.nc
    made = k.sem("ident_made")
    with nc.Block() as block:
        @block.gpsimd
        def _(pool):
            pool.memset(k.ident[:, :], 0.0).then_inc(made, 1)
            pool.wait_ge(made, 1)
            pool.affine_select(out=k.ident[:, :], in_=k.ident[:, :], compare_op=ALU.not_equal,
                               fill=1.0, base=0, pattern=[[-1, P]], channel_multiplier=1).then_inc(made, 1)
            pool.wait_ge(made, 2)


def load_x(k):
    nc = k.nc
    x_in = k.sem("x_in")
    with nc.Block() as block:
        @block.sync
        def _(sp):
            for i in range(NT):
                sp.dma_start(k.x[:, i, :], k.dram["x"][i * P:(i + 1) * P, :]).then_inc(x_in, 16)
            sp.wait_ge(x_in, 16 * NT)



def modulation(k, mod):
    nc, d = k.nc, k.dram
    n = 6 * D // CW
    with ExitStack() as c:
        NS = 3
        w = [k.sb(c, f"ada_w{s}", [P, KT * CW]) for s in range(NS)]
        ccol = k.sb(c, "ada_c", [P, KT])
        csig = k.sb(c, "ada_csig", [P, KT])
        cb = k.sb(c, "ada_cb", [P, KT, P])
        ones = k.sb(c, "ada_ones", [P, P])
        c_in, b_in, silu, bc, ones_made = (k.sem("ada_" + x) for x in ("c_in", "b_in", "silu", "bcast", "ones"))
        loaded = [k.sem(f"ada_loaded{s}") for s in range(NS)]
        used = [k.sem(f"ada_used{s}") for s in range(NS)]
        evac = [k.sem(f"ada_evac{s}") for s in range(NS)]
        with nc.Block() as block:
            @block.sync
            def _(sp):
                sp.dma_start(ccol[:, :], d["c"]).then_inc(c_in, 16)
                sp.dma_start(mod[:, :], rows(d["b_ada"])).then_inc(b_in, 16)

                def body(i):
                    for s in range(NS):
                        sp.wait_ge(used[s], i)
                        sp.dma_start(w[s][:, :], d["w_ada"][i * NS + s, :, :]).then_inc(loaded[s], 16)
                looped(sp, n // NS, body)

            @block.gpsimd
            def _(pool):
                pool.memset(ones[:, :], 1.0).then_inc(ones_made, 1)

            @block.scalar
            def _(act):
                act.wait_ge(c_in, 16)
                act.activation(csig[:, :], ccol[:, :], ACT.Silu).then_inc(silu, 1)

            @block.tensor
            def _(pe):
                pe.wait_ge(bc, KT)

                def body(i):
                    for s in range(NS):
                        pe.wait_ge(loaded[s], i * 16 + 16)
                        pe.wait_ge(evac[s], i)
                        for t in range(KT):
                            mm = pe.matmul(k.bank[s][:, 0:CW], cb[:, t, :], w[s][:, t * CW:(t + 1) * CW],
                                           start=t == 0, stop=t == KT - 1)
                        mm.then_inc(used[s], 1)
                looped(pe, n // NS, body)

            @block.vector
            def _(dve):
                dve.wait_ge(silu, 1)
                dve.wait_ge(ones_made, 1)
                for t in range(KT):
                    dve.tensor_scalar(cb[:, t, :], ones[:, :], csig[:, t:t + 1], None, ALU.mult).then_inc(bc, 1)
                dve.wait_ge(b_in, 16)

                def body(i):
                    for s in range(NS):
                        dve.wait_ge(used[s], i + 1)
                        m = mod[:, ds((i * NS + s) * CW, CW)]
                        dve.tensor_tensor(m, k.bank[s][:, 0:CW], m, ALU.add).then_inc(evac[s], 1)
                looped(dve, n // NS, body)
                for s in range(NS):
                    dve.wait_ge(evac[s], n // NS)
                for j in (1, 2, 4, 5):
                    dve.tensor_scalar(mod[:, j * D:(j + 1) * D], mod[:, j * D:(j + 1) * D], 1.0, None,
                                      ALU.add).then_inc(bc, 1)
                dve.wait_ge(bc, KT + 4)



def turn(k, name, src, hh, hl, n_tiles=NT):
    nc = k.nc
    NB = 4
    with ExitStack() as c:
        y = [k.sb(c, f"{name}_y{s}", [P, D]) for s in range(NB)]
        loaded = [k.sem(f"{name}_loaded{s}") for s in range(NB)]
        turned, hi, lo = (k.sem(f"{name}_{x}") for x in ("turned", "hi", "lo"))
        with nc.Block() as block:
            @block.sync
            def _(sp):
                for i in range(n_tiles):
                    if i >= NB:
                        sp.wait_ge(turned, 2 * (i - NB + 1))
                    sp.dma_start(y[i % NB][:, :], src[i * P:(i + 1) * P, :]).then_inc(loaded[i % NB], 16)

            @block.tensor
            def _(pe):
                for n in range(2 * n_tiles):
                    i, half = n // 2, n % 2
                    pe.wait_ge(loaded[i % NB], 16 * (i // NB + 1))
                    if n >= 8:
                        pe.wait_ge(lo, n - 7)
                    for j in range(4):
                        t = half * 4 + j
                        mm = pe.transpose(k.bank[n % 8][:, j * P:(j + 1) * P], y[i % NB][:, t * P:(t + 1) * P],
                                          k.ident[:, :])
                    mm.then_inc(turned, 1)

            @block.scalar
            def _(act):
                for n in range(2 * n_tiles):
                    i, half = n // 2, n % 2
                    act.wait_ge(turned, n + 1)
                    act.activation(hh[:, half * 4:half * 4 + 4, i * P:(i + 1) * P],
                                   k.bank[n % 8][:, :].rearrange("p (a b) -> p a b", a=4), ACT.Copy).then_inc(hi, 1)

            @block.vector
            def _(dve):
                for n in range(2 * n_tiles):
                    i, half = n // 2, n % 2
                    dst = (slice(None), slice(half * 4, half * 4 + 4), slice(i * P, (i + 1) * P))
                    dve.wait_ge(hi, n + 1)
                    dve.tensor_tensor(hl[dst], k.bank[n % 8][:, :].rearrange("p (a b) -> p a b", a=4),
                                      hh[dst].bitcast(F), ALU.subtract).then_inc(lo, 1)
                dve.wait_ge(lo, 2 * n_tiles)


def norm(k, name, kind, gain, shift, hh=None, hl=None, out=None):
    nc = k.nc
    into_x = out is None and not (hh is not None and kind == "rms")
    with ExitStack() as c:
        NB = 2
        y = [k.sb(c, f"{name}_y{s}", [P, D]) for s in range(NB)]
        st = k.sb(c, f"{name}_stats", [P, NT, 12])
        mv = k.sb(c, f"{name}_mv", [P, NT, 2])
        std = k.sb(c, f"{name}_std", [P, NT])
        rstd = k.sb(c, f"{name}_rstd", [P, NT])
        eps = k.sb(c, f"{name}_eps", [P, 1])
        sem = lambda x: k.sem(f"{name}_{x}")
        rows_in, eps_made, stats_raw, aggr, stats, std_done, rstd_done, scaled, ready = (
            sem(x) for x in ("rows_in", "eps_made", "stats_raw", "aggr", "stats", "std_done", "rstd_done",
                             "scaled", "ready"))
        g_rows = gain
        s_rows = shift
        n_rows = 0
        if k.is_dram(gain):
            g_rows = k.sb(c, f"{name}_g", [P, D])[:, :]
            n_rows += 1
        if shift is not None and k.is_dram(shift):
            s_rows = k.sb(c, f"{name}_s", [P, D])[:, :]
            n_rows += 1
        stored = [sem(f"stored{s}") for s in range(NB)] if out is not None else None
        turned, hi, lo = (sem(x) for x in ("turned", "hi", "lo")) if hh is not None else (None,) * 3
        target = lambda i: k.x[:, i, :] if into_x else y[i % NB][:, :]

        with nc.Block() as block:
            @block.sync
            def _(sp):
                if k.is_dram(gain):
                    sp.dma_start(g_rows, rows(gain)).then_inc(rows_in, 16)
                if shift is not None and k.is_dram(shift):
                    sp.dma_start(s_rows, rows(shift)).then_inc(rows_in, 16)
                if out is not None:
                    for i in range(NT):
                        sp.wait_ge(ready, i + 1)
                        sp.dma_start(out[i * P:(i + 1) * P, :], y[i % NB][:, :]).then_inc(stored[i % NB], 16)
                    for s in range(NB):
                        sp.wait_ge(stored[s], 16 * (NT // NB))

            @block.gpsimd
            def _(pool):
                pool.memset(eps[:, :], EPS if kind == "rms" else LN_EPS).then_inc(eps_made, 1)
                if shift is not None:
                    pool.wait_ge(rows_in, 16 * n_rows)
                    for i in range(NT):
                        pool.wait_ge(scaled, i + 1)
                        pool.tensor_tensor(target(i), target(i), s_rows, ALU.add).then_inc(ready, 1)

            @block.scalar
            def _(act):
                act.wait_ge(eps_made, 1)
                act.wait_ge(stats, NT if kind == "ln" else 1)
                act.activation(std[:, :], mv[:, :, 1], ACT.Sqrt, bias=eps[:, 0:1]).then_inc(std_done, 1)
                if hh is not None:
                    for n in range(2 * NT):
                        i, half = n // 2, n % 2
                        act.wait_ge(turned, n + 1)
                        act.activation(hh[:, half * 4:half * 4 + 4, i * P:(i + 1) * P],
                                       k.bank[n % 8][:, :].rearrange("p (a b) -> p a b", a=4),
                                       ACT.Copy).then_inc(hi, 1)

            @block.vector
            def _(dve):
                for i in range(NT):
                    for j in range(2):
                        dve.bn_stats(st[:, i, 6 * j:6 * j + 6], k.x[:, i, 512 * j:512 * j + 512]).then_inc(stats_raw, 1)
                for i in range(NT):
                    dve.wait_ge(stats_raw, 2 * (i + 1))
                    a = dve.bn_aggr(mv[:, i, :], st[:, i, :])
                    a.then_inc(stats if kind == "ln" else aggr, 1)
                if kind == "rms":
                    dve.wait_ge(aggr, NT)
                    dve.tensor_tensor(std[:, :], mv[:, :, 0], mv[:, :, 0], ALU.mult).then_inc(aggr, 1)
                    dve.wait_ge(aggr, NT + 1)
                    dve.tensor_tensor(mv[:, :, 1], mv[:, :, 1], std[:, :], ALU.add).then_inc(stats, 1)
                dve.wait_ge(std_done, 1)
                dve.reciprocal(rstd[:, :], std[:, :]).then_inc(rstd_done, 1)
                dve.wait_ge(rstd_done, 1)
                dve.wait_ge(rows_in, 16 * n_rows)

                def scale(i):
                    if not into_x and i >= NB:
                        if hh is not None:
                            dve.wait_ge(turned, 2 * (i - NB + 1))
                        else:
                            dve.wait_ge(stored[i % NB], 16 * (i // NB))
                    done = scaled if shift is not None else ready
                    if kind == "rms":
                        dve.scalar_tensor_tensor(out=target(i), in0=k.x[:, i, :], scalar=rstd[:, i:i + 1],
                                                 in1=g_rows, op0=ALU.mult, op1=ALU.mult).then_inc(done, 1)
                    else:
                        dve.tensor_scalar(target(i), k.x[:, i, :], mv[:, i, 0:1], rstd[:, i:i + 1],
                                          ALU.subtract, ALU.mult).then_inc(rstd_done, 1)
                        dve.wait_ge(rstd_done, i + 2)
                        dve.tensor_tensor(target(i), target(i), g_rows, ALU.mult).then_inc(done, 1)

                def lows(n):
                    i, half = n // 2, n % 2
                    dst = (slice(None), slice(half * 4, half * 4 + 4), slice(i * P, (i + 1) * P))
                    dve.wait_ge(hi, n + 1)
                    dve.tensor_tensor(hl[dst], k.bank[n % 8][:, :].rearrange("p (a b) -> p a b", a=4),
                                      hh[dst].bitcast(F), ALU.subtract).then_inc(lo, 1)

                scale(0)
                for i in range(NT):
                    if i + 1 < NT:
                        scale(i + 1)
                    if hh is not None:
                        lows(2 * i)
                        lows(2 * i + 1)
                if hh is not None:
                    dve.wait_ge(lo, 2 * NT)
                if out is None:
                    dve.wait_ge(ready, NT)

            if hh is not None:
                @block.tensor
                def _(pe):
                    for n in range(2 * NT):
                        i, half = n // 2, n % 2
                        pe.wait_ge(ready, i + 1)
                        if n >= 8:
                            pe.wait_ge(lo, n - 7)
                        for j in range(4):
                            t = half * 4 + j
                            mm = pe.transpose(k.bank[n % 8][:, j * P:(j + 1) * P],
                                              target(i)[:, t * P:(t + 1) * P], k.ident[:, :])
                        mm.then_inc(turned, 1)



class Linear:

    def __init__(self, k, w, n, kind, hh, hl, width=CW, tokens=S):
        self.k, self.w, self.n, self.kind, self.hh, self.hl = k, w, n, kind, hh, hl
        self.width, self.tokens = width, tokens
        self.banks = (2 * tokens // S if tokens == S else 0) * 2 if kind == "T" else tokens // (2 * P)
        if tokens < S:
            self.banks = 1
        self.base = {name: list(v) for name, v in k.wbase.items()}
        for s in range(2):
            uses = (n + 1 - s) // 2
            for name, step in (("w_loaded", 16), ("w_hi_done", 1), ("w_ready", 1), ("lin_mm", self.banks),
                               ("lin_evac", self.banks)):
                k.wbase[name][s] += step * uses

    def at(self, name, s, count):
        return self.k.wsem[name][s], self.base[name][s] + count

    def chunks(self, e, step):
        def pair(i):
            for s in range(2):
                step(2 * i + s, i, s)
        looped(e, self.n // 2, pair)
        if self.n % 2:
            step(self.n - 1, self.n // 2, 0)

    def load(self, sp, c, i, s):
        sp.wait_ge(*self.at("w_ready", s, i))
        sp.dma_start(self.k.w_raw[s][:, 0:KT * self.width], self.w[c, :, :]).then_inc(self.k.wsem["w_loaded"][s], 16)

    def split_hi(self, act):
        def step(c, i, s):
            act.wait_ge(*self.at("w_loaded", s, 16 * i + 16))
            act.wait_ge(*self.at("lin_mm", s, self.banks * i))
            n = KT * self.width
            act.activation(self.k.w_hi[s][:, 0:n], self.k.w_raw[s][:, 0:n], ACT.Copy)\
               .then_inc(self.k.wsem["w_hi_done"][s], 1)
        self.chunks(act, step)

    def split_lo(self, pool):
        def step(c, i, s):
            pool.wait_ge(*self.at("w_hi_done", s, i + 1))
            n = KT * self.width
            pool.tensor_tensor(self.k.w_lo[s][:, 0:n], self.k.w_raw[s][:, 0:n],
                               self.k.w_hi[s][:, 0:n].bitcast(F), ALU.subtract)\
                .then_inc(self.k.wsem["w_ready"][s], 1)
        self.chunks(pool, step)

    def out(self, s, b):
        return self.k.bank[4 * s + b]

    def products(self, pe):
        k, W, T = self.k, self.width, self.tokens

        def step(c, i, s):
            pe.wait_ge(*self.at("w_ready", s, i + 1))
            pe.wait_ge(*self.at("lin_evac", s, self.banks * i))
            wh, wl = k.w_hi[s], k.w_lo[s]
            for b in range(self.banks):
                if self.kind == "T" and T == S:
                    f, half = b // 2, b % 2
                    groups = [(k.bank[4 * s + b][:, :], f, half * 512, 512)]
                elif self.kind == "T":
                    groups = [(k.bank[4 * s][:, f * T:(f + 1) * T], f, 0, T) for f in range(2)]
                else:
                    groups = [(k.bank[4 * s + b][:, j * W:(j + 1) * W], 2 * b + j, 0, 0) for j in range(2)]
                for out, tile, t0, tn in groups:
                    for t in range(KT):
                        for p in range(3):
                            w = (wh, wl, wh)[p]
                            h = (self.hh, self.hh, self.hl)[p]
                            if self.kind == "T":
                                lhs = w[:, t * W + tile * P:t * W + tile * P + P]
                                rhs = h[:, t, t0:t0 + tn]
                            else:
                                lhs = h[:, t, tile * P:(tile + 1) * P]
                                rhs = w[:, t * W:(t + 1) * W]
                            mm = pe.matmul(out, lhs, rhs, start=t == 0 and p == 0, stop=t == KT - 1 and p == 2)
                mm.then_inc(k.wsem["lin_mm"][s], 1)
        self.chunks(pe, step)


def project(k, name, w, n, kind, hh, hl, dst, bias=None, width=CW):
    nc = k.nc
    lin = Linear(k, w, n, kind, hh, hl, width)
    with ExitStack() as c:
        stage = [k.sb(c, f"{name}_stage{s}", [P, 8 * width]) for s in range(2)]
        bias_in = k.sem(f"{name}_bias_in")
        stored = [k.sem(f"{name}_stored{s}") for s in range(2)]
        if bias is not None:
            bt = k.sb(c, f"{name}_bias", [P, 2 * n] if kind == "T" else [P, n * width])
        with nc.Block() as block:
            @block.sync
            def _(sp):
                if bias is not None:
                    sp.dma_start(bt[:, :], bias if kind == "T" else rows(bias)).then_inc(bias_in, 16)

                def store(c, i, s):
                    sp.wait_ge(*lin.at("lin_evac", s, 4 * i + 4))
                    if kind == "T":
                        sp.dma_start(dst[ds(c * CW, CW), :].rearrange("(f p) t -> p f t", p=P),
                                     stage[s][:, :].rearrange("p (f t) -> p f t", f=2)).then_inc(stored[s], 16)
                    else:
                        sp.dma_start(dst[:, ds(c * width, width)].rearrange("(i p) n -> p i n", p=P),
                                     stage[s][:, :].rearrange("p (i n) -> p i n", i=NT)).then_inc(stored[s], 16)

                pairs = n // 2
                if pairs:
                    lin.load(sp, 0, 0, 0)
                    lin.load(sp, 1, 0, 1)

                    def ahead(j):
                        i = j + 1
                        for s in range(2):
                            lin.load(sp, 2 * i + s, i, s)
                            store(2 * i + s - 2, i - 1, s)
                    looped(sp, pairs - 1, ahead)
                if n % 2:
                    lin.load(sp, n - 1, n // 2, 0)
                for s in range(2 if pairs else 0):
                    store(2 * pairs - 2 + s, pairs - 1, s)
                if n % 2:
                    store(n - 1, n // 2, 0)
                for s in range(2):
                    sp.wait_ge(stored[s], 16 * ((n + 1 - s) // 2))

            @block.scalar
            def _(act):
                lin.split_hi(act)

            @block.gpsimd
            def _(pool):
                lin.split_lo(pool)

            @block.tensor
            def _(pe):
                lin.products(pe)

            @block.vector
            def _(dve):
                if bias is not None:
                    dve.wait_ge(bias_in, 16)

                def step(c, i, s):
                    dve.wait_ge(stored[s], 16 * i)
                    for b in range(4):
                        dve.wait_ge(*lin.at("lin_mm", s, 4 * i + b + 1))
                        if kind == "T":
                            dst_, src = stage[s][:, 512 * b:512 * b + 512], lin.out(s, b)[:, :]
                            if bias is None:
                                e = dve.tensor_copy(dst_, src)
                            else:
                                e = dve.tensor_scalar(dst_, src, bt[:, ds(c * 2 + b // 2, 1)], None, ALU.add)
                            e.then_inc(k.wsem["lin_evac"][s], 1)
                        elif bias is None:
                            dve.tensor_copy(stage[s][:, 2 * b * width:2 * (b + 1) * width],
                                            lin.out(s, b)[:, 0:2 * width]).then_inc(k.wsem["lin_evac"][s], 1)
                        else:
                            for j in range(2):
                                e = dve.tensor_tensor(stage[s][:, (2 * b + j) * width:(2 * b + j + 1) * width],
                                                      lin.out(s, b)[:, j * width:(j + 1) * width],
                                                      bt[:, ds(c * width, width)], ALU.add)
                            e.then_inc(k.wsem["lin_evac"][s], 1)
                lin.chunks(dve, step)


def scaled_residual(k, dve, brow, done):
    for i in range(NT):
        dve.scalar_tensor_tensor(out=k.x[:, i, :], in0=k.x[:, i, :], scalar=ALPHA, in1=brow,
                                 op0=ALU.mult, op1=ALU.add).then_inc(done, 1)
    dve.wait_ge(done, NT)


def project_residual(k, name, w, hh, hl, gate=None, bias=None):
    nc, n = k.nc, D // CW
    lin = Linear(k, w, n, "N", hh, hl)
    with ExitStack() as c:
        scaled, bias_in, gated = (k.sem(f"{name}_{x}") for x in ("scaled", "bias_in", "gated"))
        brow = k.sb(c, f"{name}_bias", [P, D]) if bias is not None else None
        tmp = k.sb(c, f"{name}_gated", [P, 2, CW])
        with nc.Block() as block:
            @block.sync
            def _(sp):
                if bias is not None:
                    sp.dma_start(brow[:, :], rows(bias)).then_inc(bias_in, 16)
                lin.chunks(sp, lambda c, i, s: lin.load(sp, c, i, s))

            @block.scalar
            def _(act):
                lin.split_hi(act)

            @block.gpsimd
            def _(pool):
                lin.split_lo(pool)

            @block.tensor
            def _(pe):
                lin.products(pe)

            @block.vector
            def _(dve):
                if bias is not None:
                    dve.wait_ge(bias_in, 16)
                    scaled_residual(k, dve, brow[:, :], scaled)

                def step(c, i, s):
                    for b in range(4):
                        dve.wait_ge(*lin.at("lin_mm", s, 4 * i + b + 1))
                        for j in range(2):
                            src = lin.out(s, b)[:, j * CW:(j + 1) * CW]
                            xt = k.x[:, 2 * b + j, ds(c * CW, CW)]
                            if gate is not None:
                                m = dve.tensor_tensor(tmp[:, j, :], src, gate[:, ds(c * CW, CW)], ALU.mult)
                                m.then_inc(gated, 1)
                                dve.wait_ge(gated, c * 8 + (2 * b + j + 1))
                                src = tmp[:, j, :]
                            e = dve.tensor_tensor(xt, xt, src, ALU.add)
                        e.then_inc(k.wsem["lin_evac"][s], 1)
                lin.chunks(dve, step)
                for s in range(2):
                    dve.wait_ge(*lin.at("lin_evac", s, 4 * (n // 2)))



class Slots:

    def __init__(self, k, uses):
        self.k, self.uses = k, uses
        self.base = {name: list(v) for name, v in k.wbase.items()}
        for s in range(2):
            k.wbase["w_loaded"][s] += 16 * uses[s]
            k.wbase["w_hi_done"][s] += uses[s]
            k.wbase["w_ready"][s] += uses[s]

    def at(self, name, s, count):
        return self.k.wsem[name][s], self.base[name][s] + count

    def load(self, sp, s, use, src):
        sp.wait_ge(*self.at("w_ready", s, use))
        sp.dma_start(self.k.w_raw[s][:, :], src).then_inc(self.k.wsem["w_loaded"][s], 16)

    def split_hi(self, act, s, use):
        act.wait_ge(*self.at("w_loaded", s, 16 * use + 16))
        act.activation(self.k.w_hi[s][:, :], self.k.w_raw[s][:, :], ACT.Copy)\
           .then_inc(self.k.wsem["w_hi_done"][s], 1)

    def split_lo(self, pool, s, use):
        pool.wait_ge(*self.at("w_hi_done", s, use + 1))
        pool.tensor_tensor(self.k.w_lo[s][:, :], self.k.w_raw[s][:, :], self.k.w_hi[s][:, :].bitcast(F),
                           ALU.subtract).then_inc(self.k.wsem["w_ready"][s], 1)


def up_products(k, pe, hh, hl, mm):
    for f in range(2):
        for half in range(2):
            b = 2 * f + half
            for t in range(KT):
                for w, h in ((k.w_hi[0], hh), (k.w_lo[0], hh), (k.w_hi[0], hl)):
                    m = pe.matmul(k.bank[b][:, :], w[:, t * CW + f * P:t * CW + (f + 1) * P],
                                  h[:, t, half * 512:half * 512 + 512],
                                  start=t == 0 and w is k.w_hi[0] and h is hh,
                                  stop=t == KT - 1 and h is hl)
            m.then_inc(mm, 1)


def down_products(k, pe, a_hi, a_lo, out, mm, waits):
    tile, half = out // 2, out % 2
    waits()
    for f in range(2):
        for n, (w, a) in enumerate(((k.w_hi[1], a_hi), (k.w_lo[1], a_hi), (k.w_hi[1], a_lo))):
            m = pe.matmul(k.bank[4 + out % 4][:, :], a[:, f, tile * P:(tile + 1) * P],
                          w[:, f * D + half * 512:f * D + half * 512 + 512],
                          start=f == 0 and n == 0, stop=f == 1 and n == 2)
    m.then_inc(mm, 1)


def ffn_conv(k, w_up, w_down, conv, hh, hl, gate):
    nc = k.nc
    G = NF1 // 2
    wt = Slots(k, (2 * G, G))
    PAD = 2
    with ExitStack() as c:
        sem = lambda n: k.sem("ffn1_" + n)
        raw = [k.sb(c, f"ffn1_raw{s}", [P, 2, PAD + S]) for s in range(2)]
        u = [k.sb(c, f"ffn1_u{s}", [P, 2, S]) for s in range(2)]
        a_hi = k.sb(c, "ffn1_a_hi", [P, 2, S], R)
        a_lo = k.sb(c, "ffn1_a_lo", [P, 2, S], R)
        cw = k.sb(c, "ffn1_conv", [P, NF1, 2, 4])
        tmp = k.sb(c, "ffn1_gated", [P, 2, 512])
        conv_in, padded, up_mm, up_out, conved, silued, prod, mult, a_hi_done, a_lo_done, dn_mm, dn_out, gated = (
            sem(n) for n in ("conv_in", "padded", "up_mm", "up_out", "conved", "silued", "prod", "mult",
                             "a_hi", "a_lo", "dn_mm", "dn_out", "gated"))
        with nc.Block() as block:
            @block.sync
            def _(sp):
                sp.dma_start(cw[:, :, :, :], conv).then_inc(conv_in, 16)
                wt.load(sp, 0, 0, w_up[0, :, :])
                wt.load(sp, 0, 1, w_up[1, :, :])
                wt.load(sp, 1, 0, w_down[0, :, :])

                def body(j):
                    g = j + 1
                    wt.load(sp, 0, 2 * g, w_up[2 * g, :, :])
                    wt.load(sp, 0, 2 * g + 1, w_up[2 * g + 1, :, :])
                    wt.load(sp, 1, g, w_down[g, :, :])
                looped(sp, G - 1, body)

            @block.tensor
            def _(pe):
                def up(n):
                    pe.wait_ge(*wt.at("w_ready", 0, n + 1))
                    pe.wait_ge(up_out, 4 * n)
                    up_products(k, pe, hh, hl, up_mm)

                def down(g, outs):
                    pe.wait_ge(*wt.at("w_ready", 1, g + 1))
                    pe.wait_ge(a_lo_done, 2 * g + 2)
                    for o in outs:
                        free = 16 * g + o - 3
                        down_products(k, pe, a_hi, a_lo, o, dn_mm,
                                      (lambda: pe.wait_ge(dn_out, free)) if not isinstance(g, int) or free > 0
                                      else (lambda: None))
                up(0)
                up(1)
                up(2)
                down(0, range(8))
                up(3)
                down(0, range(8, 16))

                def body(j):
                    g = j + 2
                    up(2 * g)
                    down(g - 1, range(8))
                    up(2 * g + 1)
                    down(g - 1, range(8, 16))
                looped(pe, G - 2, body)
                down(G - 1, range(16))

            @block.scalar
            def _(act):
                def evac(n, s):
                    for b in range(4):
                        act.wait_ge(up_mm, 4 * n + b + 1)
                        if b == 0:
                            act.wait_ge(conved, 2 * (n - 1) if isinstance(n, int) and n < 2 else 2 * (n - 1))
                        act.activation(raw[s][:, b // 2, PAD + (b % 2) * 512:PAD + (b % 2) * 512 + 512],
                                       k.bank[b][:, :], ACT.Copy).then_inc(up_out, 1)

                def evac_first(n, s):
                    for b in range(4):
                        act.wait_ge(up_mm, 4 * n + b + 1)
                        act.activation(raw[s][:, b // 2, PAD + (b % 2) * 512:PAD + (b % 2) * 512 + 512],
                                       k.bank[b][:, :], ACT.Copy).then_inc(up_out, 1)

                def w_up_hi(n):
                    act.wait_ge(up_mm, 4 * n)
                    wt.split_hi(act, 0, n)

                def w_down_hi(g):
                    act.wait_ge(dn_mm, 16 * g)
                    wt.split_hi(act, 1, g)

                def silu(n, s):
                    act.wait_ge(conved, 2 * n + 2)
                    act.activation(u[s][:, 1, :], u[s][:, 1, :], ACT.Silu).then_inc(silued, 1)

                def a_part(n, s):
                    act.wait_ge(mult, n + 1)
                    act.activation(a_hi[:, s, :], u[s][:, 0, :], ACT.Copy).then_inc(a_hi_done, 1)

                w_up_hi(0)
                evac_first(0, 0)
                w_up_hi(1)
                silu(0, 0)
                evac_first(1, 1)
                w_up_hi(2)
                w_down_hi(0)
                a_part(0, 0)
                silu(1, 1)
                a_part(1, 1)

                def body(j):
                    g = j + 1
                    evac(2 * g, 0)
                    w_up_hi(2 * g + 1)
                    silu(2 * g, 0)
                    evac(2 * g + 1, 1)
                    w_up_hi(2 * g + 2)
                    w_down_hi(g)
                    a_part(2 * g, 0)
                    silu(2 * g + 1, 1)
                    a_part(2 * g + 1, 1)
                looped(act, G - 2, body)
                g = G - 1
                evac(2 * g, 0)
                w_up_hi(2 * g + 1)
                silu(2 * g, 0)
                evac(2 * g + 1, 1)
                w_down_hi(g)
                a_part(2 * g, 0)
                silu(2 * g + 1, 1)
                a_part(2 * g + 1, 1)

            @block.gpsimd
            def _(pool):
                for s in range(2):
                    pool.memset(raw[s][:, :, 0:PAD], 0.0).then_inc(padded, 1)

                def a_part(n, s):
                    pool.wait_ge(a_hi_done, n + 1)
                    pool.tensor_tensor(a_lo[:, s, :], u[s][:, 0, :], a_hi[:, s, :].bitcast(F),
                                       ALU.subtract).then_inc(a_lo_done, 1)

                def group(g, more):
                    wt.split_lo(pool, 0, 2 * g + 1)
                    if more:
                        wt.split_lo(pool, 0, 2 * g + 2)
                    wt.split_lo(pool, 1, g)
                    a_part(2 * g, 0)
                    a_part(2 * g + 1, 1)
                wt.split_lo(pool, 0, 0)
                looped(pool, G - 1, lambda g: group(g, True))
                group(G - 1, False)

            @block.vector
            def _(dve):
                dve.wait_ge(conv_in, 16)
                dve.wait_ge(padded, 2)

                def conv_steps(n, s, first):
                    dve.wait_ge(up_out, 4 * n + 4)
                    if not first:
                        dve.wait_ge(a_lo_done, n - 1)
                    for v in range(2):
                        co = lambda j: cw[:, n, v, j:j + 1] if isinstance(n, int) else cw[:, ds(n, 1), v, j]
                        dve.tensor_scalar(u[s][:, v, :], raw[s][:, v, 2:2 + S], co(2), co(3),
                                          ALU.mult, ALU.add).then_inc(prod, 1)
                    for j in (1, 0):
                        for v in range(2):
                            co = cw[:, n, v, j:j + 1] if isinstance(n, int) else cw[:, ds(n, 1), v, j]
                            dve.wait_ge(prod, n * 4 + (1 - j) * 2 + v + 1)
                            dve.scalar_tensor_tensor(out=u[s][:, v, :], in0=raw[s][:, v, j:j + S], scalar=co,
                                                     in1=u[s][:, v, :], op0=ALU.mult, op1=ALU.add)\
                               .then_inc(prod if j else conved, 1)
                    dve.wait_ge(silued, n + 1)
                    dve.tensor_tensor(u[s][:, 0, :], u[s][:, 0, :], u[s][:, 1, :], ALU.mult).then_inc(mult, 1)

                def add_down(g, outs):
                    for o in outs:
                        tile, half = o // 2, o % 2
                        cols = slice(half * 512, half * 512 + 512)
                        dve.wait_ge(dn_mm, 16 * g + o + 1)
                        dve.tensor_tensor(tmp[:, o % 2, :], k.bank[4 + o % 4][:, :], gate[:, cols], ALU.mult)\
                           .then_inc(gated, 1)
                        dve.wait_ge(gated, 16 * g + o + 1)
                        dve.tensor_tensor(k.x[:, tile, cols], k.x[:, tile, cols], tmp[:, o % 2, :], ALU.add)\
                           .then_inc(dn_out, 1)

                conv_steps(0, 0, True)
                conv_steps(1, 1, True)

                def body(j):
                    g = j + 1
                    add_down(g - 1, range(8))
                    conv_steps(2 * g, 0, False)
                    add_down(g - 1, range(8, 16))
                    conv_steps(2 * g + 1, 1, False)
                looped(dve, G - 1, body)
                add_down(G - 1, range(16))
                dve.wait_ge(dn_out, 16 * G)


def ffn_squared_relu(k, w_up, w_down, b_up, b_down, hh, hl):
    nc = k.nc
    G = F2C
    wt = Slots(k, (G, G))
    with ExitStack() as c:
        sem = lambda n: k.sem("ffn2_" + n)
        r = k.sb(c, "ffn2_relu", [P, 2, S])
        a_hi = k.sb(c, "ffn2_a_hi", [P, 2, S], R)
        a_lo = k.sb(c, "ffn2_a_lo", [P, 2, S], R)
        bu = k.sb(c, "ffn2_b_up", [P, 2 * G])
        brow = k.sb(c, "ffn2_b_down", [P, D])
        bias_in, scaled, up_mm, up_out, squared, a_hi_done, a_lo_done, dn_mm, dn_out = (
            sem(n) for n in ("bias_in", "scaled", "up_mm", "up_out", "squared", "a_hi", "a_lo", "dn_mm", "dn_out"))
        with nc.Block() as block:
            @block.sync
            def _(sp):
                sp.dma_start(bu[:, :], b_up).then_inc(bias_in, 16)
                sp.dma_start(brow[:, :], rows(b_down)).then_inc(bias_in, 16)

                def body(g):
                    wt.load(sp, 0, g, w_up[g, :, :])
                    wt.load(sp, 1, g, w_down[g, :, :])
                looped(sp, G, body)

            @block.tensor
            def _(pe):
                def up(g):
                    pe.wait_ge(*wt.at("w_ready", 0, g + 1))
                    pe.wait_ge(up_out, 4 * g)
                    up_products(k, pe, hh, hl, up_mm)

                def down(g):
                    pe.wait_ge(*wt.at("w_ready", 1, g + 1))
                    pe.wait_ge(a_lo_done, g + 1)
                    for o in range(16):
                        free = 16 * g + o - 3
                        down_products(k, pe, a_hi, a_lo, o, dn_mm,
                                      (lambda: pe.wait_ge(dn_out, free)) if not isinstance(g, int) or free > 0
                                      else (lambda: None))
                up(0)
                up(1)
                down(0)

                def body(j):
                    up(j + 2)
                    down(j + 1)
                looped(pe, G - 2, body)
                down(G - 1)

            @block.scalar
            def _(act):
                def w_up_hi(g):
                    act.wait_ge(up_mm, 4 * g)
                    wt.split_hi(act, 0, g)

                def group(g, more):
                    if more:
                        w_up_hi(g + 1)
                    act.wait_ge(dn_mm, 16 * g)
                    wt.split_hi(act, 1, g)
                    act.wait_ge(squared, g + 1)
                    act.activation(a_hi[:, :, :], r[:, :, :], ACT.Copy).then_inc(a_hi_done, 1)
                w_up_hi(0)
                looped(act, G - 1, lambda g: group(g, True))
                group(G - 1, False)

            @block.gpsimd
            def _(pool):
                def group(g, more):
                    if more:
                        wt.split_lo(pool, 0, g + 1)
                    wt.split_lo(pool, 1, g)
                    pool.wait_ge(a_hi_done, g + 1)
                    pool.tensor_tensor(a_lo[:, :, :], r[:, :, :], a_hi[:, :, :].bitcast(F),
                                       ALU.subtract).then_inc(a_lo_done, 1)
                wt.split_lo(pool, 0, 0)
                looped(pool, G - 1, lambda g: group(g, True))
                group(G - 1, False)

            @block.vector
            def _(dve):
                dve.wait_ge(bias_in, 32)
                scaled_residual(k, dve, brow[:, :], scaled)

                def square(g):
                    dve.wait_ge(a_lo_done, g)
                    for b in range(4):
                        dve.wait_ge(up_mm, 4 * g + b + 1)
                        dve.tensor_scalar(r[:, b // 2, (b % 2) * 512:(b % 2) * 512 + 512], k.bank[b][:, :],
                                          bu[:, ds(2 * g + b // 2, 1)], 0.0, ALU.add, ALU.max).then_inc(up_out, 1)
                    dve.wait_ge(up_out, 4 * g + 4)
                    dve.tensor_tensor(r[:, :, :], r[:, :, :], r[:, :, :], ALU.mult).then_inc(squared, 1)

                def add_down(g):
                    for o in range(16):
                        xt = k.x[:, o // 2, (o % 2) * 512:(o % 2) * 512 + 512]
                        dve.wait_ge(dn_mm, 16 * g + o + 1)
                        dve.tensor_tensor(xt, xt, k.bank[4 + o % 4][:, :], ALU.add).then_inc(dn_out, 1)
                square(0)

                def body(j):
                    square(j + 1)
                    add_down(j)
                looped(dve, G - 1, body)
                add_down(G - 1)
                dve.wait_ge(dn_out, 16 * G)



def pipelined(e, bodies, per, stages):
    deepest = max(lag for lag, _ in stages)
    for m in range(per):
        for lag, stage in stages:
            if m >= lag:
                stage(m - lag, m - lag, 0)

    def body(b):
        for m in range(per):
            for lag, stage in stages:
                pos = (m - lag) % per
                stage((b + 1) * per + m - lag, pos, b + 1 if m >= lag else b)
    looped(e, bodies - 1, body)
    for m in range(deepest):
        for lag, stage in stages:
            if m < lag:
                stage(bodies * per + m - lag, (m - lag) % per, bodies - 1)


def reached(e, sem, value):
    if not isinstance(value, int) or value > 0:
        e.wait_ge(sem, value)


def stick_breaking(k, qkT, v, mix):
    nc = k.nc
    with ExitStack() as c:
        sem = lambda n: k.sem("sb_" + n)
        q = [k.sb(c, f"sb_q{s}", [HD, S]) for s in range(2)]
        kk = [k.sb(c, f"sb_k{s}", [HD, S]) for s in range(2)]
        vv = [k.sb(c, f"sb_v{s}", [P, NT, HD]) for s in range(2)]
        soft = [k.sb(c, f"sb_soft{s}", [P, S]) for s in range(2)]
        wgt = [k.sb(c, f"sb_wgt{s}", [P, S]) for s in range(2)]
        wT = [k.sb(c, f"sb_wT{s}", [P, NT, P]) for s in range(2)]
        o = [k.sb(c, f"sb_o{s}", [P, NT, HD]) for s in range(2)]
        keep = k.sb(c, "sb_keep", [P, P])
        limit = k.sb(c, "sb_limit", [P, P])
        eighth = k.sb(c, "sb_eighth", [HD, S])
        made = sem("keep_made")
        loaded = [sem(f"loaded{s}") for s in range(2)]
        scaled_q = [sem(f"scaled_q{s}") for s in range(2)]
        stored = [sem(f"stored{s}") for s in range(2)]
        z_done, step_a, soft_done, plus, masked, summed, diff, cut, w_done, turned, wT_done, pv, out = (
            sem(n) for n in ("z", "act_step", "soft", "plus", "masked", "summed", "diff", "cut", "w",
                             "turned", "wT", "pv", "out"))
        bodies, per = SB_HEADS // 2, 2 * NT
        zs = lambda n, lo, hi: k.psum[:, 1024 * (n % 2) + lo:1024 * (n % 2) + hi]
        par = lambda pos: pos % 2

        with nc.Block() as block:
            @block.sync
            def _(sp):
                def load(j, s):
                    h = 2 * j + s
                    reached(sp, out, NT * (h - 1))
                    sp.dma_start(q[s][:, :], qkT[ds(h * HD, HD), :]).then_inc(loaded[s], 16)
                    sp.dma_start(kk[s][:, :], qkT[ds(SB_HEADS * HD + h * HD, HD), :]).then_inc(loaded[s], 16)
                    sp.dma_start(vv[s][:, :, :], v[:, ds(h * HD, HD)].rearrange("(i p) d -> p i d", p=P))\
                      .then_inc(loaded[s], 16)

                def store(j, s):
                    sp.wait_ge(out, 8 * (2 * j + s + 1))
                    sp.dma_start(mix[:, ds((2 * j + s) * HD, HD)].rearrange("(i p) d -> p i d", p=P),
                                 o[s][:, :, :]).then_inc(stored[s], 16)
                load(0, 0)
                load(0, 1)

                def body(j):
                    for s in range(2):
                        load(j + 1, s)
                        store(j, s)
                looped(sp, bodies - 1, body)
                for s in range(2):
                    store(bodies - 1, s)
                for s in range(2):
                    sp.wait_ge(stored[s], 16 * bodies)

            @block.gpsimd
            def _(pool):
                pool.memset(keep[:, :], 1.0).then_inc(made, 1)
                pool.memset(limit[:, :], 0.0).then_inc(made, 1)
                pool.memset(eighth[:, :], HD ** -0.5).then_inc(made, 1)
                pool.wait_ge(made, 3)
                for tile, fill in ((keep, 0.0), (limit, NEG)):
                    pool.affine_select(out=tile[:, :], in_=tile[:, :], compare_op=ALU.is_gt, fill=fill, base=0,
                                       pattern=[[-1, P]], channel_multiplier=1).then_inc(made, 1)
                pool.wait_ge(made, 5)

                def scale_q(n, pos, j):
                    if pos % NT == 0:
                        s = pos // NT
                        pool.wait_ge(loaded[s], 48 * (j + 1))
                        pool.tensor_tensor(q[s][:, :], q[s][:, :], eighth[:, :], ALU.mult)\
                            .then_inc(scaled_q[s], 1)

                def cut_diagonal(n, pos, j):
                    i = pos % NT
                    blk = wgt[par(pos)][:, i * P:(i + 1) * P]
                    pool.wait_ge(diff, n + 1)
                    pool.tensor_tensor(blk, blk, limit[:, :], ALU.add).then_inc(cut, 1)
                pipelined(pool, bodies, per, [(0, scale_q), (1, cut_diagonal)])

            @block.tensor
            def _(pe):
                def scores(n, pos, j):
                    s, i = pos // NT, pos % NT
                    L = (i + 1) * P
                    if i == 0:
                        pe.wait_ge(scaled_q[s], j + 1)
                    reached(pe, diff, n - 1)
                    for a in range(0, L, 512):
                        b = min(L, a + 512)
                        mm = pe.matmul(zs(pos, a, b), q[s][:, i * P:(i + 1) * P], kk[s][:, a:b],
                                       start=True, stop=True)
                    mm.then_inc(z_done, 1)

                def turn_w(n, pos, j):
                    i = pos % NT
                    pe.wait_ge(w_done, n + 1)
                    reached(pe, wT_done, n)
                    for b in range(i + 1):
                        mm = pe.transpose(k.bank[4 + b // 4][:, (b % 4) * P:(b % 4 + 1) * P],
                                          wgt[par(pos)][:, b * P:(b + 1) * P], k.ident[:, :])
                    mm.then_inc(turned, 1)

                def values(n, pos, j):
                    s, i = pos // NT, pos % NT
                    pe.wait_ge(wT_done, n + 1)
                    reached(pe, out, n - 1)
                    for b in range(i + 1):
                        mm = pe.matmul(k.bank[6 + par(pos)][:, 0:HD], wT[par(pos)][:, b, :], vv[s][:, b, :],
                                       start=b == 0, stop=b == i)
                    mm.then_inc(pv, 1)
                pipelined(pe, bodies, per, [(0, scores), (2, turn_w), (3, values)])

            @block.scalar
            def _(act):
                act.preload_act_table_set("natural_log_exp_and_others")

                def softplus_part(n, pos, j):
                    L = (pos % NT + 1) * P
                    e = soft[par(pos)][:, 0:L]
                    act.wait_ge(z_done, n + 1)
                    reached(act, plus, n - 1)
                    act.activation(e, zs(pos, 0, L), ACT.Abs).then_inc(step_a, 1)
                    act.wait_ge(step_a, 2 * n + 1)
                    act.activation(e, e, ACT.Exp, scale=-1.0).then_inc(step_a, 1)
                    act.wait_ge(step_a, 2 * n + 2)
                    act.activation(e, e, ACT.Ln, bias=1.0).then_inc(soft_done, 1)

                def weights(n, pos, j):
                    L = (pos % NT + 1) * P
                    act.wait_ge(cut, n + 1)
                    act.activation(wgt[par(pos)][:, 0:L], wgt[par(pos)][:, 0:L], ACT.Exp).then_inc(w_done, 1)

                def copy_turned(n, pos, j):
                    i = pos % NT
                    act.wait_ge(turned, n + 1)
                    reached(act, pv, n - 1)
                    act.activation(wT[par(pos)][:, 0:i + 1, :],
                                   k.psum[:, 2048:2048 + (i + 1) * P].rearrange("p (a b) -> p a b", b=P),
                                   ACT.Copy).then_inc(wT_done, 1)
                pipelined(act, bodies, per, [(0, softplus_part), (1, weights), (2, copy_turned)])

            @block.vector
            def _(dve):
                dve.wait_ge(made, 5)

                def suffix(n, pos, j):
                    i = pos % NT
                    L = (i + 1) * P
                    w = wgt[par(pos)]
                    dve.wait_ge(soft_done, n + 1)
                    reached(dve, turned, n - 1)
                    dve.scalar_tensor_tensor(out=w[:, 0:L], in0=zs(pos, 0, L), scalar=0.0,
                                             in1=soft[par(pos)][:, 0:L], op0=ALU.max, op1=ALU.add)\
                       .then_inc(plus, 1)
                    dve.wait_ge(plus, n + 1)
                    dve.tensor_tensor(w[:, L - P:L], w[:, L - P:L], keep[:, :], ALU.mult).then_inc(masked, 1)
                    dve.wait_ge(masked, n + 1)
                    back = w[:, 0:L][:, ::-1]
                    dve.tensor_tensor_scan(back, back, back, 0.0, ALU.add, ALU.max).then_inc(summed, 1)
                    dve.wait_ge(summed, n + 1)
                    dve.tensor_tensor(w[:, 0:L], zs(pos, 0, L), w[:, 0:L], ALU.subtract).then_inc(diff, 1)

                def output(n, pos, j):
                    s, i = pos // NT, pos % NT
                    dve.wait_ge(pv, n + 1)
                    if i == 0:
                        dve.wait_ge(stored[s], 16 * j)
                    dve.tensor_copy(o[s][:, i, :], k.bank[6 + par(pos)][:, 0:HD]).then_inc(out, 1)
                pipelined(dve, bodies, per, [(0, suffix), (3, output)])


def gla(k, gqT, pn, gf, w_fg, b_fg, g_out, mix):
    nc = k.nc
    KW, VW = GLA_HEADS * DK, GLA_HEADS * DV
    NC = S // CHUNK
    with ExitStack() as c:
        sem = lambda n: k.sem("gla_" + n)
        qT = k.sb(c, "gla_qT", [P, 2, S])
        kd = k.sb(c, "gla_k", [P, NT, KW])
        v = k.sb(c, "gla_v", [P, NT, VW])
        gg = k.sb(c, "gla_gate", [P, NT, VW])
        f = k.sb(c, "gla_f", [P, NT, RANK])
        fT = k.sb(c, "gla_fT", [RANK + 1, S])
        wfg = k.sb(c, "gla_wfg", [RANK + 1, KW])
        grow = k.sb(c, "gla_g", [P, VW])
        la = [k.sb(c, f"gla_la{s}", [P, KW]) for s in range(2)]
        ex = [k.sb(c, f"gla_ex{s}", [P, KW]) for s in range(2)]
        dec = [k.sb(c, f"gla_dec{s}", [P, KW]) for s in range(2)]
        decay = k.sb(c, "gla_decay", [P, 2, NC])
        state = k.sb(c, "gla_state", [P, 2, NC, DV])
        later = k.sb(c, "gla_later", [P, P])
        inchunk = k.sb(c, "gla_inchunk", [P, 2])
        eps = k.sb(c, "gla_eps", [P, 1])
        junk = k.sb(c, "gla_junk", [P, DV])
        ss = k.sb(c, "gla_ss", [P, NT * GLA_HEADS])
        rs = k.sb(c, "gla_rs", [P, NT * GLA_HEADS])
        o = [k.sb(c, f"gla_o{s}", [P, VW]) for s in range(2)]
        (in_f, in_w, in_qkv, in_g, made, f_turned, f_copied, pre, abs_done, exp_done, ln_done, la_done,
         suffix, dec_done, kd_done, total, decay_done, silued, gated, kv, stated, outp, sq, std, rstd,
         scaled, o_done) = (sem(n) for n in (
             "in_f", "in_w", "in_qkv", "in_g", "made", "f_turned", "f_copied", "pre", "abs", "exp", "ln",
             "la", "suffix", "dec", "kd", "total", "decay", "silu", "gated", "kv", "state", "out", "sq",
             "std", "rstd", "scaled", "o"))
        stored = [sem(f"stored{s}") for s in range(2)]
        TURN, PRE, SUF, TOT = k.bank[0], k.bank[1], k.bank[2], k.bank[3]

        def head_out(i, h):
            return k.bank[2 * (i % 2) + h % 2][:, (h // 2) * DV:(h // 2 + 1) * DV]
        with nc.Block() as block:
            @block.sync
            def _(sp):
                sp.dma_start(f[:, :, :], gf.rearrange("(i p) n -> p i n", p=P)).then_inc(in_f, 16)
                sp.wait_ge(made, 2)
                sp.dma_start(wfg[0:RANK, :], w_fg).then_inc(in_w, 16)
                sp.dma_start(wfg[RANK:RANK + 1, :], b_fg.rearrange("(a n) -> a n", a=1)).then_inc(in_w, 16)
                sp.dma_start(kd[:, :, :], pn[:, 0:KW].rearrange("(i p) n -> p i n", p=P)).then_inc(in_qkv, 16)
                sp.dma_start(v[:, :, :], pn[:, KW:KW + VW].rearrange("(i p) n -> p i n", p=P)).then_inc(in_qkv, 16)
                sp.dma_start(qT[:, :, :], gqT.rearrange("(a p) t -> p a t", p=P)).then_inc(in_qkv, 16)
                sp.dma_start(gg[:, :, :], pn[:, KW + VW:KW + 2 * VW].rearrange("(i p) n -> p i n", p=P))\
                  .then_inc(in_g, 16)
                sp.dma_start(grow[:, :], rows(g_out)).then_inc(in_g, 16)
                for i in range(NT):
                    sp.wait_ge(o_done, 4 * (i + 1))
                    sp.dma_start(mix[i * P:(i + 1) * P, :], o[i % 2][:, :]).then_inc(stored[i % 2], 16)
                for s in range(2):
                    sp.wait_ge(stored[s], 16 * NT // 2)

            @block.gpsimd
            def _(pool):
                pool.memset(fT[:, :], 1.0).then_inc(made, 1)
                pool.memset(wfg[:, :], 0.0).then_inc(made, 1)
                pool.memset(eps[:, :], EPS).then_inc(made, 1)
                pool.memset(later[:, :], 1.0).then_inc(made, 1)
                pool.memset(inchunk[:, :], 0.0).then_inc(made, 1)
                pool.wait_ge(made, 5)
                for j in range(2):
                    pool.memset(inchunk[j * CHUNK:(j + 1) * CHUNK, j:j + 1], 1.0).then_inc(made, 1)
                    pool.wait_ge(made, 6 + j)
                pool.affine_select(out=later[:, :], in_=later[:, :], compare_op=ALU.is_gt, fill=0.0, base=0,
                                   pattern=[[-1, P]], channel_multiplier=1).then_inc(made, 1)
                pool.wait_ge(made, 8)
                pool.memset(later[CHUNK:P, 0:CHUNK], 0.0).then_inc(made, 1)
                pool.wait_ge(made, 9)
                for i in range(NT):
                    pool.wait_ge(in_g, 32)
                    pool.wait_ge(silued, i + 1)
                    pool.tensor_tensor(gg[:, i, :], gg[:, i, :], grow[:, :], ALU.mult).then_inc(gated, 1)

            @block.tensor
            def _(pe):
                pe.wait_ge(in_f, 16)
                for i in range(NT):
                    reached(pe, f_copied, i)
                    pe.transpose(TURN[0:RANK, 0:P], f[:, i, :], k.ident[:, :]).then_inc(f_turned, 1)
                pe.wait_ge(in_w, 32)
                pe.wait_ge(made, 9)
                for i in range(NT):
                    pe.wait_ge(f_copied, i + 1)
                    reached(pe, la_done, i)
                    pe.matmul(PRE[:, 0:KW], fT[:, i * P:(i + 1) * P], wfg[:, :], start=True, stop=True)\
                      .then_inc(pre, 1)
                    pe.wait_ge(la_done, i + 1)
                    reached(pe, dec_done, i)
                    pe.matmul(SUF[:, 0:KW], later[:, :], la[i % 2][:, :], start=True, stop=True)\
                      .then_inc(suffix, 1)
                    for pair in range(2):
                        mm = pe.matmul(TOT[:, 16 * pair + 2 * i:16 * pair + 2 * i + 2],
                                       la[i % 2][:, pair * P:(pair + 1) * P], inchunk[:, :], start=True, stop=True)
                    mm.then_inc(total, 1)
                for n in range(2 * NC):
                    ch, pair = n // 2, n % 2
                    i, r0 = ch // 2, (ch % 2) * CHUNK
                    pe.wait_ge(kd_done, i + 1)
                    reached(pe, stated, 2 * (n - 3))
                    pe.matmul(k.bank[4 + n % 4][:, 0:2 * DV], kd[r0:r0 + CHUNK, i, pair * P:(pair + 1) * P],
                              v[r0:r0 + CHUNK, i, pair * 2 * DV:(pair + 1) * 2 * DV],
                              start=True, stop=True).then_inc(kv, 1)
                for i in range(NT):
                    pe.wait_ge(stated, 4 * 2 * (i + 1))
                    reached(pe, o_done, 4 * (i - 1))
                    for h in range(GLA_HEADS):
                        pair, r0 = h // 2, (h % 2) * DK
                        for j in range(2):
                            mm = pe.matmul(head_out(i, h)[j * CHUNK:(j + 1) * CHUNK, :],
                                           qT[r0:r0 + DK, pair, i * P + j * CHUNK:i * P + (j + 1) * CHUNK],
                                           state[r0:r0 + DK, pair, 2 * i + j, :], start=True, stop=True)
                    mm.then_inc(outp, 1)

            @block.scalar
            def _(act):
                act.preload_act_table_set("natural_log_exp_and_others")
                for i in range(NT):
                    s = i % 2
                    act.wait_ge(pre, i + 1)
                    reached(act, la_done, i - 1)
                    act.activation(ex[s][:, :], PRE[:, 0:KW], ACT.Abs).then_inc(abs_done, 1)
                    act.wait_ge(abs_done, i + 1)
                    act.activation(ex[s][:, :], ex[s][:, :], ACT.Exp, scale=-1.0).then_inc(exp_done, 1)
                    act.wait_ge(exp_done, i + 1)
                    act.activation(ex[s][:, :], ex[s][:, :], ACT.Ln, bias=1.0).then_inc(ln_done, 1)
                    act.wait_ge(suffix, i + 1)
                    reached(act, kd_done, i - 1)
                    act.activation(dec[s][:, :], SUF[:, 0:KW], ACT.Exp, scale=1.0 / GATE_TAU).then_inc(dec_done, 1)
                act.wait_ge(total, NT)
                act.activation(decay[:, :, :], TOT[:, 0:2 * NC].rearrange("p (a b) -> p a b", a=2), ACT.Exp,
                               scale=1.0 / GATE_TAU).then_inc(decay_done, 1)
                act.wait_ge(in_g, 32)
                for i in range(NT):
                    act.activation(gg[:, i, :], gg[:, i, :], ACT.Silu).then_inc(silued, 1)
                for i in range(NT):
                    act.wait_ge(outp, i + 1)
                    for h in range(GLA_HEADS):
                        n = i * GLA_HEADS + h
                        reached(act, sq, n)
                        act.activation(junk[:, :], head_out(i, h), ACT.Square,
                                       scale=DK ** -0.5, accum_out=ss[:, n:n + 1]).then_inc(sq, 1)
                    act.wait_ge(sq, 4 * i + 4)
                    act.activation(rs[:, 4 * i:4 * i + 4], ss[:, 4 * i:4 * i + 4], ACT.Sqrt, bias=eps[:, 0:1],
                                   scale=1.0 / DV).then_inc(std, 1)

            @block.vector
            def _(dve):
                dve.wait_ge(made, 9)
                for i in range(NT):
                    dve.wait_ge(f_turned, i + 1)
                    dve.tensor_copy(fT[0:RANK, i * P:(i + 1) * P], TURN[0:RANK, 0:P]).then_inc(f_copied, 1)
                dve.wait_ge(in_qkv, 48)
                for i in range(NT):
                    s = i % 2
                    dve.wait_ge(ln_done, i + 1)
                    reached(dve, total, i - 1)
                    dve.scalar_tensor_tensor(out=la[s][:, :], in0=PRE[:, 0:KW], scalar=0.0, in1=ex[s][:, :],
                                             op0=ALU.min, op1=ALU.subtract).then_inc(la_done, 1)
                    dve.wait_ge(dec_done, i + 1)
                    dve.tensor_tensor(kd[:, i, :], kd[:, i, :], dec[s][:, :], ALU.mult).then_inc(kd_done, 1)
                dve.wait_ge(decay_done, 1)
                for n in range(2 * NC):
                    ch, pair = n // 2, n % 2
                    dve.wait_ge(kv, n + 1)
                    reached(dve, stated, 2 * (n - 1))
                    for r in range(2):
                        rows_ = slice(r * DK, (r + 1) * DK)
                        new = k.bank[4 + n % 4][rows_, r * DV:(r + 1) * DV]
                        if ch == 0:
                            dve.tensor_copy(state[rows_, pair, 0, :], new).then_inc(stated, 1)
                        else:
                            dve.scalar_tensor_tensor(out=state[rows_, pair, ch, :],
                                                     in0=state[rows_, pair, ch - 1, :],
                                                     scalar=decay[rows_, pair, ch:ch + 1], in1=new,
                                                     op0=ALU.mult, op1=ALU.add).then_inc(stated, 1)
                for i in range(NT):
                    r4 = rs[:, 4 * i:4 * i + 4]
                    dve.wait_ge(std, i + 1)
                    dve.reciprocal(r4, r4).then_inc(rstd, 1)
                    dve.wait_ge(rstd, i + 1)
                    dve.tensor_scalar(r4, r4, DK ** -0.5, None, ALU.mult).then_inc(scaled, 1)
                    dve.wait_ge(scaled, i + 1)
                    dve.wait_ge(gated, i + 1)
                    reached(dve, stored[i % 2], 16 * (i // 2))
                    for h in range(GLA_HEADS):
                        cols = slice(h * DV, (h + 1) * DV)
                        dve.scalar_tensor_tensor(out=o[i % 2][:, cols], in0=head_out(i, h),
                                                 scalar=rs[:, 4 * i + h:4 * i + h + 1], in1=gg[:, i, cols],
                                                 op0=ALU.mult, op1=ALU.mult).then_inc(o_done, 1)



def distance_buckets(window):
    exact = BUCKETS // 2
    hot = np.zeros((BUCKETS + 1, BAND), np.float32)
    for y in range(BAND):
        dist = 2 * P - 1 - y
        if dist < 0 or (window is not None and dist >= window):
            b = BUCKETS
        elif dist < exact:
            b = dist
        else:
            b = min(BUCKETS - 1, exact + int(np.log(dist / exact) / np.log(MAX_DIST / exact) * (BUCKETS - exact)))
        hot[b, y] = 1.0
    return hot


def bias_bands(k, scratch):
    nc, d = k.nc, k.dram
    H = SWA_HEADS + DSA_HEADS
    with ExitStack() as c:
        sem = lambda n: k.sem("bias_" + n)
        rel = k.sb(c, "bias_rel", [BUCKETS + 1, H])
        hot = k.sb(c, "bias_hot", [BUCKETS + 1, 2, BAND])
        wide = k.sb(c, "bias_wide", [BUCKETS + 1, H, P])
        ones = k.sb(c, "bias_ones", [BUCKETS + 1, P])
        row = [k.sb(c, f"bias_row{s}", [P, BAND]) for s in range(2)]
        made, loaded, widened, mm, out = (sem(n) for n in ("made", "loaded", "widened", "mm", "out"))
        stored = [sem(f"stored{s}") for s in range(2)]
        with nc.Block() as block:
            @block.gpsimd
            def _(pool):
                pool.memset(rel[:, :], NEG).then_inc(made, 1)
                pool.memset(ones[:, :], 1.0).then_inc(made, 1)

            @block.sync
            def _(sp):
                sp.wait_ge(made, 2)
                sp.dma_start(rel[0:BUCKETS, :], d["rel_bias"]).then_inc(loaded, 16)
                sp.dma_start(hot[:, :, :], d["buckets"].rearrange("a b y -> b a y")).then_inc(loaded, 16)
                for g in range(H):
                    sp.wait_ge(out, g + 1)
                    sp.dma_start(scratch[g, :, :], row[g % 2][:, :]).then_inc(stored[g % 2], 16)
                for s in range(2):
                    sp.wait_ge(stored[s], 16 * H // 2)

            @block.tensor
            def _(pe):
                for g in range(H):
                    pe.wait_ge(widened, g + 1)
                    reached(pe, out, g - 1)
                    pe.matmul(k.bank[g % 2][:, 0:BAND], wide[:, g, :], hot[:, g // SWA_HEADS, :],
                              start=True, stop=True).then_inc(mm, 1)

            @block.vector
            def _(dve):
                dve.wait_ge(loaded, 32)
                for g in range(H):
                    dve.tensor_scalar(wide[:, g, :], ones[:, :], rel[:, g:g + 1], None, ALU.mult).then_inc(widened, 1)
                for g in range(H):
                    dve.wait_ge(mm, g + 1)
                    reached(dve, stored[g % 2], 16 * (g // 2))
                    dve.tensor_copy(row[g % 2][:, :], k.bank[g % 2][:, 0:BAND]).then_inc(out, 1)


def band_of(scratch, g):
    flat = scratch[g, :, :].rearrange("p y -> (p y)")
    return flat[P - 1:P - 1 + P * (BAND - 1)].rearrange("(p y) -> p y", y=BAND - 1)[:, 0:2 * P]


def window_attention(k, pT, va, bands, sinks, mix):
    nc = k.nc
    with ExitStack() as c:
        sem = lambda n: k.sem("swa_" + n)
        q = [k.sb(c, f"swa_q{s}", [HD, S]) for s in range(2)]
        kk = [k.sb(c, f"swa_k{s}", [HD, S]) for s in range(2)]
        vv = k.sb(c, "swa_v", [P, NT, 2 * HD])
        band = [k.sb(c, f"swa_band{s}", [P, 2 * P]) for s in range(2)]
        sink = k.sb(c, "swa_sink", [P, SWA_HEADS])
        p = [k.sb(c, f"swa_p{s}", [P, 2 * P]) for s in range(2)]
        pT_ = [k.sb(c, f"swa_pT{s}", [P, 2, P]) for s in range(2)]
        st = {n: k.sb(c, "swa_" + n, [P, 2 * NT]) for n in ("max", "shift", "sinkd", "esink", "den", "rden")}
        o = [k.sb(c, f"swa_o{s}", [P, NT, HD]) for s in range(2)]
        const_in = sem("const_in")
        loaded = [sem(f"loaded{s}") for s in range(2)]
        stored = [sem(f"stored{s}") for s in range(2)]
        z_done, logit, maxed, shifted, p_done, e_done, added, rden, turned, pT_done, pv, out = (
            sem(n) for n in ("z", "logit", "max", "shift", "p", "esink", "added", "rden", "turned", "pT", "pv", "out"))
        bodies, per = SWA_GROUP, 2 * NT
        col = lambda name, pos: st[name][:, pos:pos + 1]
        keys = lambda i: ((i - 1) * P if i else 0, (i + 1) * P)
        with nc.Block() as block:
            @block.sync
            def _(sp):
                for s in range(2):
                    sp.dma_start(kk[s][:, :], pT[SWA_HEADS * HD + s * HD:SWA_HEADS * HD + (s + 1) * HD, :])\
                      .then_inc(const_in, 16)
                sp.dma_start(vv[:, :, :], va.rearrange("(i p) n -> p i n", p=P)).then_inc(const_in, 16)
                sp.dma_start(sink[:, :], rows(sinks)).then_inc(const_in, 16)

                def load(j, s):
                    reached(sp, out, NT * (2 * j + s - 1))
                    h = j + SWA_GROUP * s
                    sp.dma_start(q[s][:, :], pT[ds(h * HD, HD), :]).then_inc(loaded[s], 16)
                    sp.dma_start(band[s][:, :], bands(h)).then_inc(loaded[s], 16)

                def store(j, s):
                    sp.wait_ge(out, NT * (2 * j + s + 1))
                    sp.dma_start(mix[:, ds((j + SWA_GROUP * s) * HD, HD)].rearrange("(i p) d -> p i d", p=P),
                                 o[s][:, :, :]).then_inc(stored[s], 16)
                load(0, 0)
                load(0, 1)

                def body(j):
                    for s in range(2):
                        load(j + 1, s)
                        store(j, s)
                looped(sp, bodies - 1, body)
                for s in range(2):
                    store(bodies - 1, s)
                for s in range(2):
                    sp.wait_ge(stored[s], 16 * bodies)

            @block.tensor
            def _(pe):
                pe.wait_ge(const_in, 64)

                def scores(n, pos, j):
                    s, i = pos // NT, pos % NT
                    a, b = keys(i)
                    if i == 0:
                        pe.wait_ge(loaded[s], 32 * (j + 1))
                    reached(pe, logit, n - 1)
                    pe.matmul(k.bank[pos % 2][:, 0:b - a], q[s][:, i * P:(i + 1) * P], kk[s][:, a:b],
                              start=True, stop=True).then_inc(z_done, 1)

                def turn_p(n, pos, j):
                    i = pos % NT
                    pe.wait_ge(p_done, n + 1)
                    reached(pe, pT_done, n - 1)
                    for b in range(2 if i else 1):
                        mm = pe.transpose(k.bank[2 + pos % 2][:, b * P:(b + 1) * P],
                                          p[pos % 2][:, b * P:(b + 1) * P], k.ident[:, :])
                    mm.then_inc(turned, 1)

                def values(n, pos, j):
                    s, i = pos // NT, pos % NT
                    pe.wait_ge(pT_done, n + 1)
                    reached(pe, out, n - 1)
                    nb = 2 if i else 1
                    for b in range(nb):
                        mm = pe.matmul(k.bank[4 + pos % 2][:, 0:HD], pT_[pos % 2][:, b, :],
                                       vv[:, max(i - 1, 0) + b, s * HD:(s + 1) * HD], start=b == 0, stop=b == nb - 1)
                    mm.then_inc(pv, 1)
                pipelined(pe, bodies, per, [(0, scores), (2, turn_p), (3, values)])

            @block.scalar
            def _(act):
                def weights(n, pos, j):
                    i = pos % NT
                    L = 2 * P if i else P
                    act.wait_ge(shifted, 2 * n + 2)
                    act.activation(p[pos % 2][:, 0:L], p[pos % 2][:, 0:L], ACT.Exp, bias=col("shift", pos),
                                   accum_out=col("den", pos)).then_inc(p_done, 1)
                    act.activation(col("esink", pos), col("sinkd", pos), ACT.Exp).then_inc(e_done, 1)

                def copy_turned(n, pos, j):
                    L = 2 * P if pos % NT else P
                    act.wait_ge(turned, n + 1)
                    reached(act, pv, n - 1)
                    act.activation(pT_[pos % 2][:, 0:L // P, :],
                                   k.bank[2 + pos % 2][:, 0:L].rearrange("p (a b) -> p a b", b=P), ACT.Copy)\
                       .then_inc(pT_done, 1)
                pipelined(act, bodies, per, [(0, weights), (1, copy_turned)])

            @block.vector
            def _(dve):
                dve.wait_ge(const_in, 64)

                def logits(n, pos, j):
                    s, i = pos // NT, pos % NT
                    L = 2 * P if i else P
                    w = p[pos % 2][:, 0:L]
                    dve.wait_ge(z_done, n + 1)
                    if i == 0:
                        dve.wait_ge(loaded[s], 32 * (j + 1))
                    reached(dve, turned, n - 1)
                    dve.scalar_tensor_tensor(out=w, in0=k.bank[pos % 2][:, 0:L], scalar=HD ** -0.5,
                                             in1=band[s][:, 2 * P - L:2 * P], op0=ALU.mult, op1=ALU.add)\
                       .then_inc(logit, 1)
                    dve.wait_ge(logit, n + 1)
                    dve.tensor_reduce(col("max", pos), w, AX, ALU.max).then_inc(maxed, 1)
                    dve.wait_ge(maxed, n + 1)
                    snk = sink[:, ds(j + SWA_GROUP * s, 1)]
                    dve.tensor_scalar(col("shift", pos), snk, col("max", pos), -1.0, ALU.max, ALU.mult)\
                       .then_inc(shifted, 1)
                    dve.wait_ge(shifted, 2 * n + 1)
                    dve.tensor_tensor(col("sinkd", pos), snk, col("shift", pos), ALU.add).then_inc(shifted, 1)

                def output(n, pos, j):
                    s, i = pos // NT, pos % NT
                    dve.wait_ge(e_done, n + 1)
                    dve.tensor_tensor(col("den", pos), col("den", pos), col("esink", pos), ALU.add)\
                       .then_inc(added, 1)
                    dve.wait_ge(added, n + 1)
                    dve.reciprocal(col("rden", pos), col("den", pos)).then_inc(rden, 1)
                    dve.wait_ge(rden, n + 1)
                    dve.wait_ge(pv, n + 1)
                    if i == 0:
                        dve.wait_ge(stored[s], 16 * j)
                    dve.tensor_scalar(o[s][:, i, :], k.bank[4 + pos % 2][:, 0:HD], col("rden", pos), None,
                                      ALU.mult).then_inc(out, 1)
                pipelined(dve, bodies, per, [(0, logits), (3, output)])



def sparse_prepare(k, cbT, ik_dram, iw_dram, cn, cT, ikT, iw):
    nc, d = k.nc, k.dram
    HI = DSA_HEADS
    with ExitStack() as c:
        sem = lambda n: k.sem("prep_" + n)
        raw = k.sb(c, "prep_cbT", [P, S])
        ik = k.sb(c, "prep_ik", [P, NT, HD])
        gc = k.sb(c, "prep_gc", [P, DC])
        gi = k.sb(c, "prep_gi", [P, HD])
        bi = k.sb(c, "prep_bi", [P, HD])
        junk = k.sb(c, "prep_junk", [P, DC])
        eps = k.sb(c, "prep_eps", [P, 1])
        ms = k.sb(c, "prep_ms", [P, 2 * NT])
        rs = k.sb(c, "prep_rs", [P, 2 * NT])
        st = k.sb(c, "prep_st", [P, NT, 6])
        mv = k.sb(c, "prep_mv", [P, NT, 2])
        loaded, made, turned, sq, stats, aggr, std, rstd, scaled, cn_done, ik_steps, cT_mm, ikT_mm, copied = (
            sem(n) for n in ("loaded", "eps_made", "turned", "sq", "stats", "aggr", "std", "rstd", "scaled",
                             "cn", "ik_steps", "cT_mm", "ikT_mm", "copied"))
        with nc.Block() as block:
            @block.sync
            def _(sp):
                sp.dma_start(raw[:, :], cbT).then_inc(loaded, 16)
                sp.dma_start(ik[:, :, :], ik_dram.rearrange("(i p) n -> p i n", p=P)).then_inc(loaded, 16)
                sp.dma_start(iw[:, :, :], iw_dram.rearrange("(i p) n -> p i n", p=P)).then_inc(loaded, 16)
                sp.dma_start(gc[:, :], rows(d["kv_g"])).then_inc(loaded, 16)
                sp.dma_start(gi[:, :], rows(d["ik_g"])).then_inc(loaded, 16)
                sp.dma_start(bi[:, :], rows(d["ik_b"])).then_inc(loaded, 16)

            @block.gpsimd
            def _(pool):
                pool.memset(eps[:, :], LN_EPS).then_inc(made, 1)

            @block.tensor
            def _(pe):
                pe.wait_ge(loaded, 96)
                for i in range(NT):
                    mm = pe.transpose(k.bank[i // 4][:, (i % 4) * P:(i % 4 + 1) * P], raw[:, i * P:(i + 1) * P],
                                      k.ident[:, :])
                mm.then_inc(turned, 1)
                pe.wait_ge(cn_done, NT)
                for i in range(NT):
                    mm = pe.transpose(k.bank[2 + i // 4][:, (i % 4) * P:(i % 4 + 1) * P], cn[:, i, :], k.ident[:, :])
                mm.then_inc(cT_mm, 1)
                pe.wait_ge(ik_steps, 3 * NT)
                for i in range(NT):
                    mm = pe.transpose(k.bank[4 + i // 4][0:HD, (i % 4) * P:(i % 4 + 1) * P], ik[:, i, :],
                                      k.ident[:, :])
                mm.then_inc(ikT_mm, 1)

            @block.scalar
            def _(act):
                act.wait_ge(turned, 1)
                for i in range(NT):
                    reached(act, sq, i)
                    act.activation(junk[:, :], k.bank[i // 4][:, (i % 4) * P:(i % 4 + 1) * P], ACT.Square,
                                   scale=DC ** -0.5, accum_out=ms[:, i:i + 1]).then_inc(sq, 1)
                act.wait_ge(made, 1)
                act.wait_ge(sq, NT)
                act.wait_ge(aggr, 2)
                act.activation(rs[:, :], ms[:, :], ACT.Sqrt, bias=eps[:, 0:1]).then_inc(std, 1)
                act.wait_ge(cT_mm, 1)
                act.activation(cT[:, :], k.psum[:, 1024:2048], ACT.Copy).then_inc(copied, 1)
                act.wait_ge(ikT_mm, 1)
                act.activation(ikT[:, :], k.psum[0:HD, 2048:3072], ACT.Copy).then_inc(copied, 1)
                act.wait_ge(copied, 2)

            @block.vector
            def _(dve):
                dve.wait_ge(loaded, 96)
                dve.tensor_scalar(iw[:, :, :], iw[:, :, :], HI ** -0.5, None, ALU.mult).then_inc(stats, 1)
                for i in range(NT):
                    dve.bn_stats(st[:, i, :], ik[:, i, :]).then_inc(stats, 1)
                dve.wait_ge(stats, NT + 1)
                for i in range(NT):
                    a = dve.bn_aggr(mv[:, i, :], st[:, i, :])
                a.then_inc(aggr, 1)
                dve.wait_ge(aggr, 1)
                dve.tensor_copy(ms[:, NT:2 * NT], mv[:, :, 1]).then_inc(aggr, 1)
                dve.wait_ge(std, 1)
                dve.reciprocal(rs[:, :], rs[:, :]).then_inc(rstd, 1)
                dve.wait_ge(rstd, 1)
                for i in range(NT):
                    dve.scalar_tensor_tensor(out=cn[:, i, :], in0=k.bank[i // 4][:, (i % 4) * P:(i % 4 + 1) * P],
                                             scalar=rs[:, i:i + 1], in1=gc[:, :], op0=ALU.mult, op1=ALU.mult)\
                       .then_inc(cn_done, 1)
                for i in range(NT):
                    dve.tensor_scalar(ik[:, i, :], ik[:, i, :], mv[:, i, 0:1], rs[:, NT + i:NT + i + 1],
                                      ALU.subtract, ALU.mult).then_inc(ik_steps, 1)
                dve.wait_ge(ik_steps, NT)
                for i in range(NT):
                    dve.tensor_tensor(ik[:, i, :], ik[:, i, :], gi[:, :], ALU.mult).then_inc(ik_steps, 1)
                dve.wait_ge(ik_steps, 2 * NT)
                for i in range(NT):
                    dve.tensor_tensor(ik[:, i, :], ik[:, i, :], bi[:, :], ALU.add).then_inc(ik_steps, 1)


def index_scores(k, iqT, ikT, iw, score):
    nc = k.nc
    with ExitStack() as c:
        sem = lambda n: k.sem("idx_" + n)
        q = [k.sb(c, f"idx_q{s}", [HD, S]) for s in range(2)]
        r = [k.sb(c, f"idx_r{s}", [P, S]) for s in range(2)]
        loaded = [sem(f"loaded{s}") for s in range(2)]
        zeroed, z_done, r_done, added, masked = (sem(n) for n in ("zeroed", "z", "relu", "added", "masked"))
        bodies, per = DSA_HEADS // 2, 2 * NT
        zs = lambda pos, lo, hi: k.psum[:, 1024 * (pos % 2) + lo:1024 * (pos % 2) + hi]
        with nc.Block() as block:
            @block.sync
            def _(sp):
                def load(j, s):
                    reached(sp, r_done, NT * (2 * j + s - 1))
                    sp.dma_start(q[s][:, :], iqT[ds((2 * j + s) * HD, HD), :]).then_inc(loaded[s], 16)
                load(0, 0)
                load(0, 1)
                looped(sp, bodies - 1, lambda j: [load(j + 1, s) for s in range(2)])

            @block.tensor
            def _(pe):
                def scores(n, pos, j):
                    s, i = pos // NT, pos % NT
                    L = (i + 1) * P
                    if i == 0:
                        pe.wait_ge(loaded[s], 16 * (j + 1))
                    reached(pe, r_done, n - 1)
                    for a in range(0, L, 512):
                        b = min(L, a + 512)
                        mm = pe.matmul(zs(pos, a, b), q[s][:, i * P:(i + 1) * P], ikT[:, a:b],
                                       start=True, stop=True)
                    mm.then_inc(z_done, 1)
                pipelined(pe, bodies, per, [(0, scores)])

            @block.scalar
            def _(act):
                def relu(n, pos, j):
                    L = (pos % NT + 1) * P
                    act.wait_ge(z_done, n + 1)
                    reached(act, added, n - 1)
                    act.activation(r[pos % 2][:, 0:L], zs(pos, 0, L), ACT.Relu, scale=HD ** -0.5)\
                       .then_inc(r_done, 1)
                pipelined(act, bodies, per, [(0, relu)])

            @block.gpsimd
            def _(pool):
                pool.memset(score[:, :, :], 0.0).then_inc(zeroed, 1)
                pool.wait_ge(added, bodies * per)
                for i in range(NT):
                    blk = score[:, i, i * P:(i + 1) * P]
                    pool.affine_select(out=blk, in_=blk, compare_op=ALU.is_ge, fill=NEG, base=0,
                                       pattern=[[-1, P]], channel_multiplier=1).then_inc(masked, 1)
                pool.wait_ge(masked, NT)

            @block.vector
            def _(dve):
                dve.wait_ge(zeroed, 1)

                def add(n, pos, j):
                    s, i = pos // NT, pos % NT
                    L = (i + 1) * P
                    dve.wait_ge(r_done, n + 1)
                    if isinstance(n, int) and n < NT:
                        pass
                    else:
                        dve.wait_ge(added, n - NT + 1)
                    dve.scalar_tensor_tensor(out=score[:, i, 0:L], in0=r[pos % 2][:, 0:L],
                                             scalar=iw[:, i, ds(2 * j + s, 1)], in1=score[:, i, 0:L],
                                             op0=ALU.mult, op1=ALU.add).then_inc(added, 1)
                pipelined(dve, bodies, per, [(0, add)])


def select_top(k, score):
    nc = k.nc
    T0 = TOPK // P
    tiles = range(T0, NT)
    n = len(tiles)
    with ExitStack() as c:
        sem = lambda x: k.sem("top_" + x)
        u = k.sb(c, "top_u", [P, n], U32)
        cand = k.sb(c, "top_cand", [P, n], U32)
        flip = k.sb(c, "top_flip", [P, n], U32)
        thr = k.sb(c, "top_thr", [P, n], U32)
        bit = k.sb(c, "top_bit", [P, n], U32)
        cnt = k.sb(c, "top_cnt", [P, n])
        enough = k.sb(c, "top_enough", [P, n], U32)
        need = k.sb(c, "top_need", [P, n])
        hit = [k.sb(c, f"top_hit{j}", [P, S]) for j in range(2)]
        gt = k.sb(c, "top_gt", [P, S])
        eq = k.sb(c, "top_eq", [P, S])
        rank = k.sb(c, "top_rank", [P, S])
        step, counted = sem("step"), sem("counted")
        thr_f = lambda: thr[:, :].bitcast(F)
        with nc.Block() as block:
            @block.vector
            def _(dve):
                dve.memset(u[:, :], 0).then_inc(step, 1)
                dve.memset(bit[:, :], 1 << 31).then_inc(step, 1)
                dve.wait_ge(step, 2)
                SMALL = 7

                def one_bit(b):
                    def chained(m):
                        dve.wait_ge(step, b * SMALL + 2 + m)
                    dve.tensor_tensor(cand[:, :], u[:, :], bit[:, :], ALU.bitwise_or).then_inc(step, 1)
                    chained(1)
                    dve.tensor_scalar(flip[:, :].bitcast(I32), cand[:, :].bitcast(I32), 31, -1,
                                      ALU.arith_shift_right, ALU.bitwise_xor).then_inc(step, 1)
                    chained(2)
                    dve.tensor_scalar(flip[:, :].bitcast(I32), flip[:, :].bitcast(I32), -(1 << 31), None,
                                      ALU.bitwise_or).then_inc(step, 1)
                    chained(3)
                    dve.tensor_tensor(thr[:, :], cand[:, :], flip[:, :], ALU.bitwise_xor).then_inc(step, 1)
                    chained(4)
                    for t, i in enumerate(tiles):
                        L = (i + 1) * P
                        if t >= 2:
                            dve.wait_ge(counted, b * n + t - 1)
                        dve.tensor_scalar(hit[t % 2][:, 0:L], score[:, i, 0:L], thr_f()[:, t:t + 1], None, ALU.is_ge,
                                          ALU.add, accum_out=cnt[:, t:t + 1]).then_inc(counted, 1)
                    dve.wait_ge(counted, b * n + n)
                    dve.tensor_scalar(enough[:, :], cnt[:, :], float(TOPK), None, ALU.is_ge).then_inc(step, 1)
                    chained(5)
                    dve.tensor_scalar(bit[:, :], bit[:, :], 1, None, ALU.logical_shift_right).then_inc(step, 1)
                    dve.copy_predicated(u[:, :], enough[:, :], cand[:, :]).then_inc(step, 1)
                    chained(7)
                looped(dve, 32, one_bit)
                v = 32 * SMALL + 2

                for m, op in enumerate((
                        lambda: dve.tensor_scalar(flip[:, :].bitcast(I32), u[:, :].bitcast(I32), 31, -1,
                                                  ALU.arith_shift_right, ALU.bitwise_xor),
                        lambda: dve.tensor_scalar(flip[:, :].bitcast(I32), flip[:, :].bitcast(I32), -(1 << 31),
                                                  None, ALU.bitwise_or),
                        lambda: dve.tensor_tensor(thr[:, :], u[:, :], flip[:, :], ALU.bitwise_xor))):
                    op().then_inc(step, 1)
                    dve.wait_ge(step, v + m + 1)
                v += 3
                for t, i in enumerate(tiles):
                    L = (i + 1) * P
                    sc, th = score[:, i, 0:L], thr_f()[:, t:t + 1]
                    dve.tensor_scalar(gt[:, 0:L], sc, th, None, ALU.is_gt, ALU.add,
                                      accum_out=cnt[:, t:t + 1]).then_inc(step, 1)
                    dve.tensor_scalar(eq[:, 0:L], sc, th, None, ALU.is_equal).then_inc(step, 1)
                    dve.wait_ge(step, v + 2)
                    dve.tensor_scalar(need[:, t:t + 1], cnt[:, t:t + 1], -1.0, float(TOPK), ALU.mult, ALU.add)\
                       .then_inc(step, 1)
                    dve.tensor_tensor_scan(rank[:, 0:L], eq[:, 0:L], eq[:, 0:L], 0.0, ALU.add, ALU.max)\
                       .then_inc(step, 1)
                    dve.wait_ge(step, v + 4)
                    dve.scalar_tensor_tensor(out=eq[:, 0:L], in0=rank[:, 0:L], scalar=need[:, t:t + 1],
                                             in1=eq[:, 0:L], op0=ALU.is_le, op1=ALU.mult).then_inc(step, 1)
                    dve.wait_ge(step, v + 5)
                    dve.tensor_tensor(gt[:, 0:L], gt[:, 0:L], eq[:, 0:L], ALU.add).then_inc(step, 1)
                    dve.wait_ge(step, v + 6)
                    dve.tensor_scalar(sc, gt[:, 0:L], -1.0, -NEG, ALU.add, ALU.mult).then_inc(step, 1)
                    dve.wait_ge(step, v + 7)
                    v += 7
                for i in range(T0):
                    L = (i + 1) * P
                    sc = score[:, i, 0:L]
                    dve.tensor_scalar(gt[:, 0:L], sc, NEG, None, ALU.is_gt).then_inc(step, 1)
                    dve.wait_ge(step, v + 1)
                    dve.tensor_scalar(sc, gt[:, 0:L], -1.0, -NEG, ALU.add, ALU.mult).then_inc(step, 1)
                    dve.wait_ge(step, v + 2)
                    v += 2


def sparse_attention(k, qbT, w_uk, w_uv, cn, cT, mask, bands, rel_last, mix):
    nc = k.nc
    with ExitStack() as c:
        sem = lambda n: k.sem("dsa_" + n)
        q = [k.sb(c, f"dsa_q{s}", [HD, S]) for s in range(2)]
        uk = [k.sb(c, f"dsa_uk{s}", [HD, DC]) for s in range(2)]
        uv = [k.sb(c, f"dsa_uv{s}", [DC, HD]) for s in range(2)]
        ql = [k.sb(c, f"dsa_ql{s}", [DC, S]) for s in range(2)]
        band = [k.sb(c, f"dsa_band{s}", [P, 2 * P]) for s in range(2)]
        far = k.sb(c, "dsa_far", [P, DSA_HEADS])
        p = [k.sb(c, f"dsa_p{s}", [P, S]) for s in range(2)]
        pT_ = [k.sb(c, f"dsa_pT{s}", [P, NT, P]) for s in range(2)]
        ol = [k.sb(c, f"dsa_ol{s}", [DC, P]) for s in range(2)]
        st = {n: k.sb(c, "dsa_" + n, [P, 2 * NT]) for n in ("shift", "den", "rden")}
        o = [k.sb(c, f"dsa_o{s}", [P, NT, HD]) for s in range(2)]
        far_in = sem("far_in")
        loaded = [sem(f"loaded{s}") for s in range(2)]
        stored = [sem(f"stored{s}") for s in range(2)]
        qlat, ql_done, z_done, logit, biased, shifted, p_done, turned, pT_done, lat, lat_done, rden, pv, out = (
            sem(n) for n in ("qlat", "ql", "z", "logit", "biased", "shift", "p", "turned", "pT", "lat",
                             "lat_copied", "rden", "pv", "out"))
        bodies, per = DSA_HEADS // 2, 2 * NT
        zs = lambda pos, lo, hi: k.psum[:, 1024 * (pos % 2) + lo:1024 * (pos % 2) + hi]
        col = lambda name, pos: st[name][:, pos:pos + 1]
        with nc.Block() as block:
            @block.sync
            def _(sp):
                sp.dma_start(far[:, :], rows(rel_last)).then_inc(far_in, 16)

                def load(j, s):
                    h = 2 * j + s
                    reached(sp, out, NT * (h - 1))
                    sp.dma_start(q[s][:, :], qbT[ds(h * HD, HD), :]).then_inc(loaded[s], 16)
                    sp.dma_start(uk[s][:, :], w_uk[h, :, :]).then_inc(loaded[s], 16)
                    sp.dma_start(uv[s][:, :], w_uv[h, :, :]).then_inc(loaded[s], 16)
                    sp.dma_start(band[s][:, :], bands(h)).then_inc(loaded[s], 16)

                def store(j, s):
                    h = 2 * j + s
                    sp.wait_ge(out, NT * (h + 1))
                    sp.dma_start(mix[:, ds(h * HD, HD)].rearrange("(i p) d -> p i d", p=P), o[s][:, :, :])\
                      .then_inc(stored[s], 16)
                load(0, 0)
                load(0, 1)

                def body(j):
                    for s in range(2):
                        load(j + 1, s)
                        store(j, s)
                looped(sp, bodies - 1, body)
                for s in range(2):
                    store(bodies - 1, s)
                for s in range(2):
                    sp.wait_ge(stored[s], 16 * bodies)

            @block.tensor
            def _(pe):
                def scores(n, pos, j):
                    s, i = pos // NT, pos % NT
                    L = (i + 1) * P
                    if i == 0:
                        h = 2 * j + s
                        pe.wait_ge(loaded[s], 64 * (j + 1))
                        reached(pe, pT_done, n - 1)
                        for half in range(2):
                            mm = pe.matmul(k.bank[4 + half], uk[s][:, :], q[s][:, half * 512:half * 512 + 512],
                                           start=True, stop=True)
                        mm.then_inc(qlat, 1)
                        pe.wait_ge(ql_done, h + 1)
                    reached(pe, biased, n - 1)
                    for a in range(0, L, 512):
                        b = min(L, a + 512)
                        mm = pe.matmul(zs(pos, a, b), ql[s][:, i * P:(i + 1) * P], cT[:, a:b],
                                       start=True, stop=True)
                    mm.then_inc(z_done, 1)

                def turn_p(n, pos, j):
                    i = pos % NT
                    pe.wait_ge(p_done, n + 1)
                    reached(pe, pT_done, n)
                    for b in range(i + 1):
                        mm = pe.transpose(k.bank[4 + b // 4][:, (b % 4) * P:(b % 4 + 1) * P],
                                          p[pos % 2][:, b * P:(b + 1) * P], k.ident[:, :])
                    mm.then_inc(turned, 1)

                def latents(n, pos, j):
                    i = pos % NT
                    pe.wait_ge(pT_done, n + 1)
                    reached(pe, lat_done, n)
                    for b in range(i + 1):
                        mm = pe.matmul(k.bank[6][:, 0:P], cn[:, b, :], pT_[pos % 2][:, b, :],
                                       start=b == 0, stop=b == i)
                    mm.then_inc(lat, 1)

                def values(n, pos, j):
                    s = pos // NT
                    pe.wait_ge(lat_done, n + 1)
                    reached(pe, out, n)
                    pe.matmul(k.bank[7][:, 0:HD], ol[pos % 2][:, :], uv[s][:, :], start=True, stop=True)\
                      .then_inc(pv, 1)
                pipelined(pe, bodies, per, [(2, turn_p), (0, scores), (3, latents), (4, values)])

            @block.scalar
            def _(act):
                def scale_q(n, pos, j):
                    s, i = pos // NT, pos % NT
                    if i == 0:
                        act.wait_ge(qlat, 2 * j + s + 1)
                        act.activation(ql[s][:, :], k.psum[:, 2048:3072], ACT.Copy, scale=HD ** -0.5)\
                           .then_inc(ql_done, 1)

                def weights(n, pos, j):
                    L = (pos % NT + 1) * P
                    act.wait_ge(shifted, n + 1)
                    act.activation(p[pos % 2][:, 0:L], p[pos % 2][:, 0:L], ACT.Exp, bias=col("shift", pos),
                                   accum_out=col("den", pos)).then_inc(p_done, 1)

                def copy_turned(n, pos, j):
                    i = pos % NT
                    act.wait_ge(turned, n + 1)
                    reached(act, lat, n - 1)
                    act.activation(pT_[pos % 2][:, 0:i + 1, :],
                                   k.psum[:, 2048:2048 + (i + 1) * P].rearrange("p (a b) -> p a b", b=P),
                                   ACT.Copy).then_inc(pT_done, 1)
                pipelined(act, bodies, per, [(2, copy_turned), (0, scale_q), (1, weights)])

            @block.vector
            def _(dve):
                dve.wait_ge(far_in, 16)

                def logits(n, pos, j):
                    s, i = pos // NT, pos % NT
                    L = (i + 1) * P
                    near = 2 * P if i else P
                    f = L - near
                    w, m = p[pos % 2], mask[:, i, :]
                    dve.wait_ge(z_done, n + 1)
                    if i == 0:
                        dve.wait_ge(loaded[s], 64 * (j + 1))
                    reached(dve, turned, n - 1)
                    dve.tensor_tensor(w[:, f:L], zs(pos, f, L), m[:, f:L], ALU.add).then_inc(logit, 1)
                    if f:
                        dve.scalar_tensor_tensor(out=w[:, 0:f], in0=zs(pos, 0, f),
                                                 scalar=far[:, ds(2 * j + s, 1)], in1=m[:, 0:f],
                                                 op0=ALU.add, op1=ALU.add)
                    dve.wait_ge(logit, n + 1)
                    dve.tensor_tensor(w[:, f:L], w[:, f:L], band[s][:, 2 * P - near:2 * P], ALU.add)\
                       .then_inc(biased, 1)
                    dve.wait_ge(biased, n + 1)
                    dve.tensor_reduce(col("shift", pos), w[:, 0:L], AX, ALU.max, negate=True).then_inc(shifted, 1)

                def copy_latents(n, pos, j):
                    dve.wait_ge(lat, n + 1)
                    reached(dve, pv, n - 1)
                    dve.tensor_copy(ol[pos % 2][:, :], k.bank[6][:, 0:P]).then_inc(lat_done, 1)

                def output(n, pos, j):
                    s, i = pos // NT, pos % NT
                    dve.wait_ge(p_done, n + 1)
                    dve.reciprocal(col("rden", pos), col("den", pos)).then_inc(rden, 1)
                    dve.wait_ge(rden, n + 1)
                    dve.wait_ge(pv, n + 1)
                    if i == 0:
                        dve.wait_ge(stored[s], 16 * j)
                    dve.tensor_scalar(o[s][:, i, :], k.bank[7][:, 0:HD], col("rden", pos), None, ALU.mult)\
                       .then_inc(out, 1)
                pipelined(dve, bodies, per, [(0, logits), (3, copy_latents), (4, output)])



def memory_keys_values(k, w_kv, b_k, b_v, mh, ml, kT, v):
    nc = k.nc
    n = D // CW
    for name, kind, off in (("mk", "T", 0), ("mv", "N", n)):
        lin = Linear(k, w_kv[off:off + n, :, :], n, kind, mh, ml, tokens=MEM)
        with ExitStack() as c:
            bias = k.sb(c, f"{name}_bias", [P, 2 * n] if kind == "T" else [P, D])
            bias_in = k.sem(f"{name}_bias_in")
            with nc.Block() as block:
                @block.sync
                def _(sp):
                    sp.dma_start(bias[:, :], b_k if kind == "T" else rows(b_v)).then_inc(bias_in, 16)
                    lin.chunks(sp, lambda c, i, s: lin.load(sp, c, i, s))

                @block.scalar
                def _(act):
                    lin.split_hi(act)

                @block.gpsimd
                def _(pool):
                    lin.split_lo(pool)

                @block.tensor
                def _(pe):
                    lin.products(pe)

                @block.vector
                def _(dve):
                    dve.wait_ge(bias_in, 16)

                    def step(c, i, s):
                        dve.wait_ge(*lin.at("lin_mm", s, i + 1))
                        for f in range(2):
                            src = lin.out(s, 0)[:, f * CW:(f + 1) * CW]
                            if kind == "T":
                                e = dve.tensor_scalar(kT[:, ds(2 * c + f, 1), :].rearrange("p a m -> p (a m)"),
                                                      src, bias[:, ds(2 * c + f, 1)], None, ALU.add)
                            else:
                                e = dve.tensor_tensor(v[:, f, ds(c * CW, CW)], src, bias[:, ds(c * CW, CW)], ALU.add)
                        e.then_inc(k.wsem["lin_evac"][s], 1)
                    lin.chunks(dve, step)
                    for s in range(2):
                        dve.wait_ge(*lin.at("lin_evac", s, n // 2))


def memory_attention(k, qT, kT, v, mix):
    nc = k.nc
    KF = MEM_HD // P
    with ExitStack() as c:
        sem = lambda n: k.sem("xa_" + n)
        q = [k.sb(c, f"xa_q{s}", [P, KF, S]) for s in range(2)]
        p = [k.sb(c, f"xa_p{s}", [P, MEM]) for s in range(2)]
        pT_ = [k.sb(c, f"xa_pT{s}", [P, 2, P]) for s in range(2)]
        st = {n: k.sb(c, "xa_" + n, [P, 4 * NT]) for n in ("max", "shift", "den", "rden")}
        o = [k.sb(c, f"xa_o{s}", [P, NT, MEM_HD]) for s in range(2)]
        loaded = [sem(f"loaded{s}") for s in range(2)]
        stored = [sem(f"stored{s}") for s in range(2)]
        z_done, maxed, shifted, p_done, turned, pT_done, rden, pv, out = (
            sem(n) for n in ("z", "max", "shift", "p", "turned", "pT", "rden", "pv", "out"))
        col = lambda name, n: st[name][:, n:n + 1]
        N = MEM_HEADS * NT
        with nc.Block() as block:
            @block.sync
            def _(sp):
                for h in range(MEM_HEADS + 1):
                    if h < MEM_HEADS:
                        reached(sp, out, NT * (h - 1))
                        sp.dma_start(q[h % 2][:, :, :], qT[h * MEM_HD:(h + 1) * MEM_HD, :]
                                     .rearrange("(a p) t -> p a t", p=P)).then_inc(loaded[h % 2], 16)
                    if h:
                        g = h - 1
                        sp.wait_ge(out, NT * h)
                        sp.dma_start(mix[:, g * MEM_HD:(g + 1) * MEM_HD].rearrange("(i p) d -> p i d", p=P),
                                     o[g % 2][:, :, :]).then_inc(stored[g % 2], 16)
                for s in range(2):
                    sp.wait_ge(stored[s], 16 * MEM_HEADS // 2)

            @block.tensor
            def _(pe):
                def scores(n, pos, j):
                    h, i = n // NT, n % NT
                    pe.wait_ge(loaded[h % 2], 16 * (h // 2 + 1))
                    reached(pe, p_done, n - 1)
                    for a in range(KF):
                        mm = pe.matmul(k.bank[n % 2][:, 0:MEM], q[h % 2][:, a, i * P:(i + 1) * P],
                                       kT[:, KF * h + a, :], start=a == 0, stop=a == KF - 1)
                    mm.then_inc(z_done, 1)

                def turn_p(n, pos, j):
                    pe.wait_ge(p_done, n + 1)
                    reached(pe, pT_done, n - 1)
                    for b in range(2):
                        mm = pe.transpose(k.bank[2 + n % 2][:, b * P:(b + 1) * P], p[n % 2][:, b * P:(b + 1) * P],
                                          k.ident[:, :])
                    mm.then_inc(turned, 1)

                def values(n, pos, j):
                    h = n // NT
                    pe.wait_ge(pT_done, n + 1)
                    reached(pe, out, n - 1)
                    for b in range(2):
                        mm = pe.matmul(k.bank[4 + n % 2][:, 0:MEM_HD], pT_[n % 2][:, b, :],
                                       v[:, b, h * MEM_HD:(h + 1) * MEM_HD], start=b == 0, stop=b == 1)
                    mm.then_inc(pv, 1)
                pipelined(pe, 1, N, [(0, scores), (2, turn_p), (3, values)])

            @block.scalar
            def _(act):
                def weights(n, pos, j):
                    act.wait_ge(shifted, n + 1)
                    reached(act, turned, n - 1)
                    act.activation(p[n % 2][:, :], k.bank[n % 2][:, 0:MEM], ACT.Exp, bias=col("shift", n),
                                   scale=MEM_HD ** -0.5, accum_out=col("den", n)).then_inc(p_done, 1)

                def copy_turned(n, pos, j):
                    act.wait_ge(turned, n + 1)
                    reached(act, pv, n - 1)
                    act.activation(pT_[n % 2][:, :, :], k.bank[2 + n % 2][:, 0:MEM]
                                   .rearrange("p (a b) -> p a b", b=P), ACT.Copy).then_inc(pT_done, 1)
                pipelined(act, 1, N, [(0, weights), (1, copy_turned)])

            @block.vector
            def _(dve):
                def maximum(n, pos, j):
                    dve.wait_ge(z_done, n + 1)
                    dve.tensor_reduce(col("max", n), k.bank[n % 2][:, 0:MEM], AX, ALU.max).then_inc(maxed, 1)
                    dve.wait_ge(maxed, n + 1)
                    dve.tensor_scalar(col("shift", n), col("max", n), -(MEM_HD ** -0.5), None, ALU.mult)\
                       .then_inc(shifted, 1)

                def output(n, pos, j):
                    h, i = n // NT, n % NT
                    dve.wait_ge(p_done, n + 1)
                    dve.reciprocal(col("rden", n), col("den", n)).then_inc(rden, 1)
                    dve.wait_ge(rden, n + 1)
                    dve.wait_ge(pv, n + 1)
                    reached(dve, stored[h % 2], 16 * (h // 2))
                    dve.tensor_scalar(o[h % 2][:, i, :], k.bank[4 + n % 2][:, 0:MEM_HD], col("rden", n), None,
                                      ALU.mult).then_inc(out, 1)
                pipelined(dve, 1, N, [(0, maximum), (3, output)])



def build(nc, d, out):
    with ExitStack() as ctx:
        k = Kernel(nc, ctx, d)
        p1T = k.scratch("p1T", [1280, S])
        p1N = k.scratch("p1N", [S, 1792])
        p1F = k.scratch("p1F", [S, RANK])
        p2T = k.scratch("p2T", [1792, S])
        p2N = k.scratch("p2N", [S, 200])
        xqT = k.scratch("xqT", [D, S])
        mix = k.scratch("mix", [S, D])
        bands = k.scratch("bands", [SWA_HEADS + DSA_HEADS, P, BAND])

        def halves(c, n=S):
            return (k.sb(c, "h_hi", [P, KT, n], R), k.sb(c, "h_lo", [P, KT, n], R))

        setup(k)
        load_x(k)
        with ExitStack() as c:
            mod = k.sb(c, "mod", [P, 6 * D])
            modulation(k, mod)
            shift1, scale1, gate1, shift2, scale2, gate2 = (mod[:, j * D:(j + 1) * D] for j in range(6))
            gain_rows(k, (("g_norm1", scale1), ("g_norm2", scale2)))
            with ExitStack() as c2:
                hh, hl = halves(c2)
                norm(k, "n1", "rms", scale1, shift1, hh, hl)
                project(k, "in1T", d["w_in_T"], 5, "T", hh, hl, p1T)
                project(k, "in1N", d["w_in_N"], 7, "N", hh, hl, p1N)
                project(k, "in1F", d["w_in_F"], 1, "N", hh, hl, p1F, width=RANK)
            k.free_sems()
            stick_breaking(k, p1T[0:1024, :], p1N[:, 0:512], mix[:, 0:512])
            gla(k, p1T[1024:1280, :], p1N[:, 512:1792], p1F, d["w_fg2"], d["b_fg2"], d["g_gla_out"], mix[:, 512:1024])
            with ExitStack() as c2:
                hh, hl = halves(c2)
                turn(k, "t1", mix, hh, hl)
                project_residual(k, "out1", d["w_out"], hh, hl, gate=gate1)
            mod2 = k.scratch("mod2", [3, D])
            save_rows(k, ((shift2, mod2[0, :]), (scale2, mod2[1, :]), (gate2, mod2[2, :])))
        k.free_sems()
        with ExitStack() as c:
            g2 = k.sb(c, "gate2", [P, D])
            load_rows(k, mod2[2, :], g2)
            hh, hl = halves(c)
            norm(k, "n2", "rms", mod2[1, :], mod2[0, :], hh, hl)
            ffn_conv(k, d["w_up"], d["w_down"], d["conv"], hh, hl, g2)
        norm(k, "n3", "rms", d["g_final"], None)

        with ExitStack() as c:
            hh, hl = halves(c)
            norm(k, "n4", "ln", d["ln_emb_g"], d["ln_emb_b"], hh, hl)
            project(k, "in2T", d["w_in2_T"], 7, "T", hh, hl, p2T, bias=d["b_in2_T"])
            project(k, "in2N", d["w_in2_N"], 1, "N", hh, hl, p2N, bias=d["b_in2_N"], width=200)
        k.free_sems()
        bias_bands(k, bands)
        window_attention(k, p2T[0:640, :], p2N[:, 0:128], lambda h: band_of(bands, h), d["sinks"], mix[:, 0:512])
        with ExitStack() as c:
            cn = k.sb(c, "latents", [P, NT, DC])
            cT = k.sb(c, "latentsT", [DC, S])
            ikT = k.sb(c, "index_kT", [HD, S])
            iw = k.sb(c, "index_w", [P, NT, DSA_HEADS])
            score = k.sb(c, "index_score", [P, NT, S])
            sparse_prepare(k, p2T[1664:1792, :], p2N[:, 128:192], p2N[:, 192:200], cn, cT, ikT, iw)
            index_scores(k, p2T[1152:1664, :], ikT, iw, score)
            select_top(k, score)
            sparse_attention(k, p2T[640:1152, :], d["w_ukT"], d["w_uv"], cn, cT, score,
                             lambda h: band_of(bands, SWA_HEADS + h), d["rel_last"], mix[:, 512:1024])
        k.free_sems()
        with ExitStack() as c:
            hh, hl = halves(c)
            turn(k, "t2", mix, hh, hl)
            project_residual(k, "out2", d["w_o"], hh, hl, bias=d["b_o"])
            norm(k, "n5", "ln", d["ln1_g"], d["ln1_b"], hh, hl)
            project(k, "xq", d["xa_wq"], 4, "T", hh, hl, xqT, bias=d["xa_bq"])
        with ExitStack() as c:
            kT = k.sb(c, "mem_kT", [P, KT, MEM])
            v = k.sb(c, "mem_v", [P, MEM // P, D])
            with ExitStack() as c2:
                mh, ml = halves(c2, MEM)
                turn(k, "t3", d["mem"], mh, ml, MEM // P)
                memory_keys_values(k, d["xa_wkv"], d["xa_bk"], d["xa_bv"], mh, ml, kT, v)
            memory_attention(k, xqT, kT, v, mix)
        k.free_sems()
        with ExitStack() as c:
            hh, hl = halves(c)
            turn(k, "t4", mix, hh, hl)
            project_residual(k, "out3", d["xa_wo"], hh, hl, bias=d["xa_bo"])
            norm(k, "n6", "ln", d["ln2_g"], d["ln2_b"], hh, hl)
            ffn_squared_relu(k, d["w_up2"], d["w_down2"], d["b_up2"], d["b_down2"], hh, hl)
        norm(k, "n7", "ln", d["ln3_g"], d["ln3_b"], out=out)


def gain_rows(k, pairs):
    with ExitStack() as c:
        g = [k.sb(c, "gain_row", [P, D]) for _ in pairs]
        loaded, done = k.sem("gain_in"), k.sem("gain_done")
        with k.nc.Block() as block:
            @block.sync
            def _(sp):
                for (name, _), t in zip(pairs, g):
                    sp.dma_start(t[:, :], rows(k.dram[name])).then_inc(loaded, 16)

            @block.vector
            def _(dve):
                dve.wait_ge(loaded, 16 * len(pairs))
                for (_, row), t in zip(pairs, g):
                    dve.tensor_tensor(row, row, t[:, :], ALU.mult).then_inc(done, 1)
                dve.wait_ge(done, len(pairs))


def save_rows(k, pairs):
    stored = k.sem("rows_stored")
    with k.nc.Block() as block:
        @block.sync
        def _(sp):
            for row, dst in pairs:
                sp.dma_start(dst.rearrange("(a n) -> a n", a=1), row[0:1, :]).then_inc(stored, 16)
            sp.wait_ge(stored, 16 * len(pairs))


def load_rows(k, src, tile):
    loaded = k.sem("rows_loaded")
    with k.nc.Block() as block:
        @block.sync
        def _(sp):
            sp.dma_start(tile[:, :], rows(src)).then_inc(loaded, 16)
            sp.wait_ge(loaded, 16)



def chunked(w, width=CW):
    n = w.shape[1] // width
    return np.ascontiguousarray(w.reshape(KT, P, n, width).transpose(2, 1, 0, 3)).reshape(n, P, KT * width)


def row_chunked(w):
    return np.ascontiguousarray(w.reshape(-1, 2, P, D).transpose(0, 2, 1, 3)).reshape(-1, P, 2 * D)


def columns(b):
    return np.ascontiguousarray(b.reshape(-1, P).T)


def laid_out(i):
    i = {name: np.asarray(a) for name, a in i.items()}
    w = i["w_in"][0]
    q, kk, v, gq, gk, gv, gg, gf = np.split(w, np.cumsum([512, 512, 512, 256, 256, 512, 512]), axis=1)
    w2 = i["w_in_2"][0]
    cuts = np.cumsum([512, 128, 128, 512, 128, 512, 64])
    qa, ka, va, qb, cb, iq, ik, iw = np.split(w2, cuts, axis=1)
    bqa, bka, bva, bqb, bcb, biq, bik, biw = np.split(i["b_in_2"][0], cuts)
    up = i["w_up"][0].reshape(D, 2, NF1, P).transpose(0, 2, 1, 3).reshape(D, 2 * NF1 * P)
    conv = np.concatenate([i["w_conv"][0], i["b_conv"]], 0).reshape(4, 2, NF1, P)
    return {
        "x": i["x"][0], "c": columns(i["c"][0]), "w_ada": chunked(i["w_ada"][0]), "b_ada": i["b_ada"][0],
        "g_norm1": i["g_norm1"][0], "g_norm2": i["g_norm2"][0],
        "w_in_T": chunked(np.concatenate([q, kk, gq], 1)), "w_in_N": chunked(np.concatenate([v, gk, gv, gg], 1)),
        "w_in_F": chunked(gf, RANK), "w_fg2": i["w_fg2"][0], "b_fg2": i["b_fg2"][0],
        "g_gla_out": i["g_gla_out"][0], "w_out": chunked(i["w_out"][0]), "w_up": chunked(up),
        "conv": np.ascontiguousarray(conv.transpose(3, 2, 1, 0)), "w_down": row_chunked(i["w_down"][0]),
        "g_final": i["g_final"],
        "mem": i["mem_2"][0], "ln_emb_g": i["ln_emb_g_2"], "ln_emb_b": i["ln_emb_b_2"],
        "w_in2_T": chunked(np.concatenate([qa, ka, qb, iq, cb], 1)),
        "b_in2_T": columns(np.concatenate([bqa, bka, bqb, biq, bcb])),
        "w_in2_N": chunked(np.concatenate([va, ik, iw], 1), 200), "b_in2_N": np.concatenate([bva, bik, biw]),
        "sinks": i["swa_sinks_2"][0], "kv_g": i["dsa_kv_norm_g_2"][0], "ik_g": i["idx_k_ln_g_2"][0],
        "ik_b": i["idx_k_ln_b_2"][0], "w_ukT": np.ascontiguousarray(i["dsa_w_uk_2"][0].transpose(0, 2, 1)),
        "w_uv": i["dsa_w_uv_2"][0], "rel_bias": i["rel_bias_2"],
        "rel_last": np.ascontiguousarray(i["rel_bias_2"][BUCKETS - 1, SWA_HEADS:]),
        "buckets": np.stack([distance_buckets(P), distance_buckets(None)]),
        "w_o": chunked(i["w_o_2"][0]), "b_o": i["b_o_2"][0], "ln1_g": i["ln1_g_2"][0], "ln1_b": i["ln1_b_2"][0],
        "xa_wq": chunked(i["xa_wq_2"][0]), "xa_bq": columns(i["xa_bq_2"][0]), "xa_wkv": chunked(i["xa_wkv_2"][0]),
        "xa_bk": columns(i["xa_bkv_2"][0][:D]), "xa_bv": np.ascontiguousarray(i["xa_bkv_2"][0][D:]),
        "xa_wo": chunked(i["xa_wo_2"][0]), "xa_bo": i["xa_bo_2"][0], "ln2_g": i["ln2_g_2"][0],
        "ln2_b": i["ln2_b_2"][0], "w_up2": chunked(i["w_up_2"][0]), "b_up2": columns(i["b_up_2"][0]),
        "w_down2": row_chunked(i["w_down_2"][0]), "b_down2": i["b_down_2"][0], "ln3_g": i["ln3_g_2"][0],
        "ln3_b": i["ln3_b_2"][0],
    }


def kernel(**inputs):
    import concourse.bacc as bacc
    from concourse.bass_utils import run_bass_kernel_spmd

    nc = bacc.Bacc("TRN2", target_bir_lowering=False, num_devices=1)
    arrays = {name: np.ascontiguousarray(a) for name, a in laid_out(inputs).items()}
    dram = {name: nc.dram_tensor(f"in_{name}", a.shape, F, kind="ExternalInput").ap() for name, a in arrays.items()}
    out = nc.dram_tensor("out_0_dram", (S, D), F, kind="ExternalOutput").ap()
    build(nc, dram, out)
    result = run_bass_kernel_spmd(nc, [{f"in_{name}": a for name, a in arrays.items()}], core_ids=[0])
    return result.results[0]["out_0_dram"].reshape(1, S, D)
```

```python
from contextlib import ExitStack

import numpy as np
import concourse.bass as bass
from concourse import mybir
from concourse.alu_op_type import AluOpType as ALU

F = mybir.dt.float32
R = mybir.dt.float32r
U32 = mybir.dt.uint32
I32 = mybir.dt.int32
BF = mybir.dt.bfloat16
ACT = mybir.ActivationFunctionType
AX = mybir.AxisListType.X
ds = bass.ds

P = 128
S = 1024
D = 1024
NT = S // P
KT = D // P
CW = 256
NEG = -1e30
EPS = 1e-6
LN_EPS = 1e-5
ALPHA = 2.0 ** 0.25

SB_HEADS, HD = 8, 64
GLA_HEADS, DK, DV, CHUNK = 4, 64, 128, 64
RANK = 16
GLA_IN = GLA_HEADS * (DK + 2 * DV) + RANK
GATE_TAU = 16.0
NF1 = 2816 // P
F2C = 4096 // CW
SWA_HEADS, SWA_GROUP = 8, 4
DSA_HEADS, DC = 8, 128
TOPK = 256
BUCKETS, MAX_DIST = 32, 128
MEM, MEM_HEADS, MEM_HD = 256, 4, 256
BAND = 384


class Kernel:

    def __init__(self, nc, ctx, dram):
        self.nc, self.ctx, self.dram = nc, ctx, dram
        self.named, self.used_sems = {}, []
        self.psum = ctx.enter_context(nc.psum_tensor("psum", [P, 8 * 512], F))
        self.bank = [self.psum[:, 512 * b:512 * b + 512] for b in range(8)]
        self.x = self.sb(ctx, "residual", [P, NT, D])
        self.ident = self.sb(ctx, "ident", [P, P])
        self.stats = self.sb(ctx, "x_stats", [P, NT, 12])
        self.w_raw = [self.sb(ctx, f"w_raw{s}", [P, KT * CW]) for s in range(2)]
        self.w_hl = [self.sb(ctx, f"w_hl{s}", [P, 2, KT * CW], R) for s in range(2)]
        self.w_hi, self.w_lo = ([w[:, part, :] for w in self.w_hl] for part in range(2))
        names = ("w_loaded", "w_hi_done", "w_ready", "lin_mm", "lin_evac", "lin_stored")
        self.wsem = {n: [self.sem(f"{n}{s}") for s in range(2)] for n in names}
        self.wbase = {n: [0, 0] for n in names}
        self.next_slot = 0
        self.used_sems = []

    def sb(self, ctx, name, shape, dt=F):
        self.named[name] = self.named.get(name, 0) + 1
        if self.named[name] > 1:
            name = f"{name}_{self.named[name]}"
        return ctx.enter_context(self.nc.sbuf_tensor(name, shape, dt))

    def sem(self, name):
        handle = self.nc.alloc_semaphore(name=name)
        self.used_sems.append(handle)
        return handle

    def x_stats(self, dve, tile, done=None):
        for j in range(2):
            e = dve.bn_stats(self.stats[:, tile, 6 * j:6 * j + 6], self.x[:, tile, 512 * j:512 * j + 512])
        if done is not None:
            e.then_inc(done, 1)

    def free_sems(self):
        self.nc.clear_and_free_semaphores(self.used_sems)
        self.nc.all_engine_barrier()
        self.used_sems = []

    def is_dram(self, ap):
        return len(ap.shape) == 1

    def scratch(self, name, shape):
        return self.nc.dram_tensor(name, shape, F, kind="Internal").ap()


def rows(ap, n=P):
    return ap.rearrange("(a n) -> a n", a=1).broadcast_to([n, ap.shape[0]])


def looped(e, n, body, peel=1):
    for i in range(min(n, peel)):
        body(i)
    if n == peel + 1:
        body(peel)
    elif n > peel + 1:
        with e.Fori(peel, n) as i:
            body(i)



def setup(k):
    nc = k.nc
    made = k.sem("ident_made")
    with nc.Block() as block:
        @block.gpsimd
        def _(pool):
            pool.memset(k.ident[:, :], 0.0).then_inc(made, 1)
            pool.wait_ge(made, 1)
            pool.affine_select(out=k.ident[:, :], in_=k.ident[:, :], compare_op=ALU.not_equal,
                               fill=1.0, base=0, pattern=[[-1, P]], channel_multiplier=1).then_inc(made, 1)
            pool.wait_ge(made, 2)



def modulation(k, mod, gate1):
    nc, d = k.nc, k.dram
    n = 6 * D // CW
    with ExitStack() as c:
        NS = 3
        w = [k.sb(c, f"ada_w{s}", [P, KT * CW]) for s in range(NS)]
        ccol = k.sb(c, "ada_c", [P, KT])
        csig = k.sb(c, "ada_csig", [P, KT])
        cb = k.sb(c, "ada_cb", [P, KT, P])
        bias = mod[0:1, :]
        ones = k.sb(c, "ada_ones", [P, P])
        gains = [k.w_raw[j][:, 0:D] for j in range(2)]
        half = n // NS // 2
        tiles = NT // half
        gains_in = k.sem("ada_gains_in")
        c_in, b_in, silu, bc, ones_made, x_in = (
            k.sem("ada_" + x) for x in ("c_in", "b_in", "silu", "bcast", "ones", "x_in"))
        loaded = [k.sem(f"ada_loaded{s}") for s in range(NS)]
        used = [k.sem(f"ada_used{s}") for s in range(NS)]
        mm_done = [k.sem(f"ada_mm{s}") for s in range(NS)]
        evac = [k.sem(f"ada_evac{s}") for s in range(NS)]
        with nc.Block() as block:
            @block.sync
            def _(sp):
                sp.dma_start(ccol[:, :], d["c"]).then_inc(c_in, 16)
                sp.dma_start(bias, d["b_ada"].rearrange("(a n) -> a n", a=1)).then_inc(b_in, 16)

                def body(i):
                    for s in range(NS):
                        sp.wait_ge(used[s], i)
                        sp.dma_start(w[s][:, :], d["w_ada"][i * NS + s, :, :]).then_inc(loaded[s], 16)
                body(0)
                for i in range(NT):
                    sp.dma_start(k.x[:, i, :], d["x"][i * P:(i + 1) * P, :]).then_inc(x_in, 16)
                for j, name in enumerate(("g_norm1", "g_norm2")):
                    sp.dma_start(gains[j], rows(d[name])).then_inc(gains_in, 16)
                with sp.Fori(1, n // NS) as i:
                    body(i)

            @block.gpsimd
            def _(pool):
                pool.memset(ones[:, :], 1.0).then_inc(ones_made, 1)

            @block.scalar
            def _(act):
                act.wait_ge(c_in, 16)
                act.activation(csig[:, :], ccol[:, :], ACT.Silu).then_inc(silu, 1)

            @block.tensor
            def _(pe):
                pe.wait_ge(b_in, 16)
                pe.wait_ge(bc, KT)

                def body(i):
                    for s in range(NS):
                        pe.wait_ge(loaded[s], i * 16 + 16)
                        pe.wait_ge(evac[s], i)
                        for t in range(KT):
                            mm = pe.matmul(k.bank[s][:, 0:CW], cb[:, t, :], w[s][:, t * CW:(t + 1) * CW],
                                           start=t == 0, stop=False)
                        mm.then_inc(used[s], 1)
                        pe.matmul(k.bank[s][:, 0:CW], ones[0:1, :], bias[:, ds((i * NS + s) * CW, CW)],
                                  start=False, stop=True).then_inc(mm_done[s], 1)
                looped(pe, n // NS, body)

            @block.vector
            def _(dve):
                dve.wait_ge(silu, 1)
                dve.wait_ge(ones_made, 1)
                for t in range(KT):
                    dve.tensor_scalar(cb[:, t, :], ones[:, :], csig[:, t:t + 1], None, ALU.mult).then_inc(bc, 1)

                def body(i):
                    for s in range(NS):
                        dve.wait_ge(mm_done[s], i + 1)
                        dve.tensor_copy(mod[:, ds((i * NS + s) * CW, CW)], k.bank[s][:, 0:CW]).then_inc(evac[s], 1)
                looped(dve, half, body)
                dve.wait_ge(x_in, 16 * NT)
                with dve.Fori(half, n // NS) as i:
                    body(i)
                    for j in range(tiles):
                        for h in range(2):
                            tile = ds((i - half) * tiles + j, 1)
                            dve.bn_stats(k.stats[:, tile, 6 * h:6 * h + 6].rearrange("p a s -> p (a s)"),
                                         k.x[:, tile, 512 * h:512 * h + 512].rearrange("p a f -> p (a f)"))
                for s in range(NS):
                    dve.wait_ge(evac[s], n // NS)
                dve.wait_ge(gains_in, 32)
                row = lambda j: mod[:, j * D:(j + 1) * D]
                for j, g in ((1, gains[0]), (4, gains[1])):
                    dve.scalar_tensor_tensor(out=row(j), in0=row(j), scalar=1.0, in1=g, op0=ALU.add,
                                             op1=ALU.mult).then_inc(bc, 1)
                for j, dst in ((2, gate1[:, :]), (5, row(5))):
                    dve.tensor_scalar(dst, row(j), 1.0, None, ALU.add).then_inc(bc, 1)
                dve.wait_ge(bc, KT + 4)



def turn(k, name, src, hh, hl, n_tiles=NT, ahead=None):
    nc = k.nc
    NB = 4
    with ExitStack() as c:
        y = [k.sb(c, f"{name}_y{s}", [P, D]) for s in range(NB)]
        loaded = [k.sem(f"{name}_loaded{s}") for s in range(NB)]
        turned, hi, lo = (k.sem(f"{name}_{x}") for x in ("turned", "hi", "lo"))
        with nc.Block() as block:
            @block.sync
            def _(sp):
                for i in range(n_tiles):
                    if i >= NB:
                        sp.wait_ge(turned, 2 * (i - NB + 1))
                    sp.dma_start(y[i % NB][:, :], src[i * P:(i + 1) * P, :]).then_inc(loaded[i % NB], 16)
                if ahead:
                    ahead.early(sp, "load", 2)

            @block.gpsimd
            def _(pool):
                if ahead:
                    ahead.early(pool, "lo", 1)

            @block.tensor
            def _(pe):
                for n in range(2 * n_tiles):
                    i, half = n // 2, n % 2
                    pe.wait_ge(loaded[i % NB], 16 * (i // NB + 1))
                    if n >= 8:
                        pe.wait_ge(lo, n - 7)
                    for j in range(4):
                        t = half * 4 + j
                        mm = pe.transpose(k.bank[n % 8][:, j * P:(j + 1) * P], y[i % NB][:, t * P:(t + 1) * P],
                                          k.ident[:, :])
                    mm.then_inc(turned, 1)

            @block.scalar
            def _(act):
                if ahead:
                    ahead.early(act, "hi", min(1, ahead.early_done["load"]))
                for n in range(2 * n_tiles):
                    i, half = n // 2, n % 2
                    act.wait_ge(turned, n + 1)
                    act.activation(hh[:, half * 4:half * 4 + 4, i * P:(i + 1) * P],
                                   k.bank[n % 8][:, :].rearrange("p (a b) -> p a b", a=4), ACT.Copy).then_inc(hi, 1)
                if ahead:
                    ahead.early(act, "hi", 1)

            @block.vector
            def _(dve):
                for n in range(2 * n_tiles):
                    i, half = n // 2, n % 2
                    dst = (slice(None), slice(half * 4, half * 4 + 4), slice(i * P, (i + 1) * P))
                    dve.wait_ge(hi, n + 1)
                    dve.tensor_tensor(hl[dst], k.bank[n % 8][:, :].rearrange("p (a b) -> p a b", a=4),
                                      hh[dst].bitcast(F), ALU.subtract).then_inc(lo, 1)
                dve.wait_ge(lo, 2 * n_tiles)


def norm(k, name, kind, gain, shift, hh=None, hl=None, out=None, ahead=None, saved=()):
    nc = k.nc
    into_x = out is None and not (hh is not None and kind == "rms")
    with ExitStack() as c:
        NB = 2
        y = [k.sb(c, f"{name}_y{s}", [P, D]) for s in range(NB)]
        mv = k.sb(c, f"{name}_mv", [P, NT, 2])
        std = k.sb(c, f"{name}_std", [P, NT])
        minus_mean = k.sb(c, f"{name}_minus_mean", [P, NT])
        rstd = k.sb(c, f"{name}_rstd", [P, NT])
        eps = k.sb(c, f"{name}_eps", [P, 1])
        sem = lambda x: k.sem(f"{name}_{x}")
        rows_in, eps_made, aggr, stats, std_done, rstd_done, centred, scaled, ready = (
            sem(x) for x in ("rows_in", "eps_made", "aggr", "stats", "std_done", "rstd_done",
                             "centred", "scaled", "ready"))
        late = ahead and not ahead.early_done["load"]
        rows_out = sem("rows_out") if saved else None
        g_rows = gain
        s_rows = shift
        n_rows = 0
        if k.is_dram(gain):
            g_rows = k.sb(c, f"{name}_g", [P, D])[:, :]
            n_rows += 1
        if shift is not None and k.is_dram(shift):
            s_rows = k.sb(c, f"{name}_s", [P, D])[:, :]
            n_rows += 1
        stored = [sem(f"stored{s}") for s in range(NB)] if out is not None else None
        turned, hi, lo = (sem(x) for x in ("turned", "hi", "lo")) if hh is not None else (None,) * 3
        target = lambda i: k.x[:, i, :] if into_x else y[i % NB][:, :]

        with nc.Block() as block:
            @block.sync
            def _(sp):
                if k.is_dram(gain):
                    sp.dma_start(g_rows, rows(gain)).then_inc(rows_in, 16)
                if shift is not None and k.is_dram(shift):
                    sp.dma_start(s_rows, rows(shift)).then_inc(rows_in, 16)
                if ahead:
                    ahead.early(sp, "load", 2)
                for row, dst in saved:
                    sp.dma_start(dst.rearrange("(a n) -> a n", a=1), row[0:1, :]).then_inc(rows_out, 16)
                if saved:
                    sp.wait_ge(rows_out, 16 * len(saved))
                if out is not None:
                    for i in range(NT):
                        sp.wait_ge(ready, i + 1)
                        sp.dma_start(out[i * P:(i + 1) * P, :], y[i % NB][:, :]).then_inc(stored[i % NB], 16)
                    for s in range(NB):
                        sp.wait_ge(stored[s], 16 * (NT // NB))

            @block.gpsimd
            def _(pool):
                pool.memset(eps[:, :], EPS if kind == "rms" else LN_EPS).then_inc(eps_made, 1)
                if ahead and (not late or shift is None):
                    ahead.early(pool, "lo", 1)
                if shift is not None:
                    pool.wait_ge(rows_in, 16 * n_rows)
                    for i in range(NT):
                        pool.wait_ge(scaled, i + 1)
                        pool.tensor_tensor(target(i), target(i), s_rows, ALU.add).then_inc(ready, 1)
                if ahead:
                    ahead.early(pool, "lo", 1)

            @block.scalar
            def _(act):
                if ahead and not late:
                    ahead.early(act, "hi", 1)
                act.wait_ge(eps_made, 1)
                act.wait_ge(stats, 1)
                act.activation(std[:, :], mv[:, :, 1], ACT.Sqrt, bias=eps[:, 0:1]).then_inc(std_done, 1)

                def centre(i):
                    if kind == "ln" and i < NT:
                        if out is not None:
                            reached(act, stored[i % NB], 16 * (i // NB))
                        act.activation(target(i), k.x[:, i, :], ACT.Identity, bias=minus_mean[:, i:i + 1])\
                           .then_inc(centred, 1)
                centre(0)
                if late:
                    ahead.early(act, "hi", 1)
                if hh is None:
                    for i in range(1, NT):
                        centre(i)
                else:
                    for n in range(2 * NT):
                        i, half = n // 2, n % 2
                        if half == 0:
                            centre(i + 1)
                        act.wait_ge(turned, n + 1)
                        act.activation(hh[:, half * 4:half * 4 + 4, i * P:(i + 1) * P],
                                       k.bank[n % 8][:, :].rearrange("p (a b) -> p a b", a=4),
                                       ACT.Copy).then_inc(hi, 1)
                if ahead:
                    ahead.early(act, "hi", 1)

            @block.vector
            def _(dve):
                for i in range(NT):
                    a = dve.bn_aggr(mv[:, i, :], k.stats[:, i, :])
                    a.then_inc(aggr, 1)
                dve.wait_ge(aggr, NT)
                if kind == "ln":
                    dve.tensor_scalar(minus_mean[:, :], mv[:, :, 0], -1.0, None, ALU.mult).then_inc(stats, 1)
                if kind == "rms":
                    dve.tensor_tensor(std[:, :], mv[:, :, 0], mv[:, :, 0], ALU.mult).then_inc(aggr, 1)
                    dve.wait_ge(aggr, NT + 1)
                    dve.tensor_tensor(mv[:, :, 1], mv[:, :, 1], std[:, :], ALU.add).then_inc(stats, 1)
                dve.wait_ge(std_done, 1)
                dve.reciprocal(rstd[:, :], std[:, :]).then_inc(rstd_done, 1)
                dve.wait_ge(rstd_done, 1)
                dve.wait_ge(rows_in, 16 * n_rows)

                def scale(i):
                    if not into_x and i >= NB:
                        if hh is not None:
                            dve.wait_ge(turned, 2 * (i - NB + 1))
                        else:
                            dve.wait_ge(stored[i % NB], 16 * (i // NB))
                    src = k.x[:, i, :]
                    if kind == "ln":
                        dve.wait_ge(centred, i + 1)
                        src = target(i)
                    dve.scalar_tensor_tensor(out=target(i), in0=src, scalar=rstd[:, i:i + 1], in1=g_rows,
                                             op0=ALU.mult, op1=ALU.mult)\
                       .then_inc(scaled if shift is not None else ready, 1)

                def lows(n):
                    i, half = n // 2, n % 2
                    dst = (slice(None), slice(half * 4, half * 4 + 4), slice(i * P, (i + 1) * P))
                    dve.wait_ge(hi, n + 1)
                    dve.tensor_tensor(hl[dst], k.bank[n % 8][:, :].rearrange("p (a b) -> p a b", a=4),
                                      hh[dst].bitcast(F), ALU.subtract).then_inc(lo, 1)

                scale(0)
                for i in range(NT):
                    if i + 1 < NT:
                        scale(i + 1)
                    if hh is not None:
                        lows(2 * i)
                        lows(2 * i + 1)
                    elif out is None:
                        dve.wait_ge(ready, i + 1)
                        k.x_stats(dve, i)
                if hh is not None:
                    dve.wait_ge(lo, 2 * NT)
                if out is None:
                    dve.wait_ge(ready, NT)

            if hh is not None:
                @block.tensor
                def _(pe):
                    for n in range(2 * NT):
                        i, half = n // 2, n % 2
                        pe.wait_ge(ready, i + 1)
                        if n >= 8:
                            pe.wait_ge(lo, n - 7)
                        for j in range(4):
                            t = half * 4 + j
                            mm = pe.transpose(k.bank[n % 8][:, j * P:(j + 1) * P],
                                              target(i)[:, t * P:(t + 1) * P], k.ident[:, :])
                        mm.then_inc(turned, 1)



class Linear:

    def __init__(self, k, w, n, kind, hh=None, hl=None, width=CW, tokens=S, banks=None):
        self.k, self.w, self.n, self.kind, self.hh, self.hl = k, w, n, kind, hh, hl
        self.width, self.tokens = width, tokens
        self.banks = (2 * tokens // S if tokens == S else 0) * 2 if kind == "T" else tokens // (2 * P)
        if tokens < S:
            self.banks = 1
        self.banks = banks or self.banks
        self.base = {name: list(v) for name, v in k.wbase.items()}
        self.early_done = {"load": 0, "hi": 0, "lo": 0}
        self.s0 = k.next_slot
        k.next_slot ^= n % 2
        self.uses = [0, 0]
        for s in range(2):
            uses = self.uses[s] = (n + 1 - (s ^ self.s0)) // 2
            for name, step in (("w_loaded", 16), ("w_hi_done", 1), ("w_ready", 1), ("lin_mm", self.banks),
                               ("lin_evac", self.banks)):
                k.wbase[name][s] += step * uses

    def at(self, name, s, count):
        return self.k.wsem[name][s], self.base[name][s] + count

    def chunks(self, e, step):
        def pair(i):
            for s in range(2):
                step(2 * i + s, i, s ^ self.s0)
        looped(e, self.n // 2, pair)
        if self.n % 2:
            step(self.n - 1, self.n // 2, self.s0)

    def early(self, e, what, upto):
        for c in range(self.early_done[what], min(upto, self.n)):
            {"load": self.load, "hi": self.hi, "lo": self.lo}[what](e, c, 0, c ^ self.s0)
        self.early_done[what] = max(self.early_done[what], min(upto, self.n))

    def own(self, what, c):
        return not isinstance(c, int) or c >= self.early_done[what]

    def load(self, sp, c, i, s):
        if not self.own("load", c):
            return
        sp.wait_ge(*self.at("w_ready", s, i))
        sp.dma_start(self.k.w_raw[s][:, 0:KT * self.width], self.w[c, :, :]).then_inc(self.k.wsem["w_loaded"][s], 16)

    def hi(self, act, c, i, s):
        if not self.own("hi", c):
            return
        act.wait_ge(*self.at("w_loaded", s, 16 * i + 16))
        act.wait_ge(*self.at("lin_mm", s, self.banks * i))
        n = KT * self.width
        act.activation(self.k.w_hi[s][:, 0:n], self.k.w_raw[s][:, 0:n], ACT.Copy)\
           .then_inc(self.k.wsem["w_hi_done"][s], 1)

    def lo(self, pool, c, i, s):
        if not self.own("lo", c):
            return
        pool.wait_ge(*self.at("w_hi_done", s, i + 1))
        n = KT * self.width
        pool.tensor_tensor(self.k.w_lo[s][:, 0:n], self.k.w_raw[s][:, 0:n],
                           self.k.w_hi[s][:, 0:n].bitcast(F), ALU.subtract)\
            .then_inc(self.k.wsem["w_ready"][s], 1)

    def split_hi(self, act):
        self.chunks(act, lambda c, i, s: self.hi(act, c, i, s))

    def split_lo(self, pool):
        self.chunks(pool, lambda c, i, s: self.lo(pool, c, i, s))

    def out(self, s, b):
        return self.k.bank[4 * s + b]

    def products(self, pe):
        k, W, T = self.k, self.width, self.tokens

        def step(c, i, s):
            pe.wait_ge(*self.at("w_ready", s, i + 1))
            pe.wait_ge(*self.at("lin_evac", s, self.banks * i))
            wh, wl = k.w_hi[s], k.w_lo[s]
            for b in range(self.banks):
                if self.kind == "T" and T == S:
                    f, half = b // 2, b % 2
                    groups = [(k.bank[4 * s + b][:, :], f, half * 512, 512)]
                elif self.kind == "T":
                    groups = [(k.bank[4 * s][:, f * T:(f + 1) * T], f, 0, T) for f in range(2)]
                else:
                    groups = [(k.bank[4 * s + b][:, j * W:(j + 1) * W], 2 * b + j, 0, 0) for j in range(2)]
                for out, tile, t0, tn in groups:
                    for t in range(KT):
                        for p in range(3):
                            w = (wh, wl, wh)[p]
                            h = (self.hh, self.hh, self.hl)[p]
                            if self.kind == "T":
                                lhs = w[:, t * W + tile * P:t * W + tile * P + P]
                                rhs = h[:, t, t0:t0 + tn]
                            else:
                                lhs = h[:, t, tile * P:(tile + 1) * P]
                                rhs = w[:, t * W:(t + 1) * W]
                            mm = pe.matmul(out, lhs, rhs, start=t == 0 and p == 0, stop=t == KT - 1 and p == 2)
                mm.then_inc(k.wsem["lin_mm"][s], 1)
        self.chunks(pe, step)


def project(k, name, lin, dst, bias=None, ahead=None):
    nc = k.nc
    n, kind, width = lin.n, lin.kind, lin.width
    with ExitStack() as c:
        stage = [k.sb(c, f"{name}_stage{s}", [P, 8 * width]) for s in range(2)]
        bias_in = k.sem(f"{name}_bias_in")
        stored = [k.sem(f"{name}_stored{s}") for s in range(2)]
        if bias is not None:
            bt = k.sb(c, f"{name}_bias", [P, 2 * n] if kind == "T" else [P, n * width])
        with nc.Block() as block:
            @block.sync
            def _(sp):
                if bias is not None:
                    sp.dma_start(bt[:, :], bias if kind == "T" else rows(bias)).then_inc(bias_in, 16)

                def store(c, i, s):
                    sp.wait_ge(*lin.at("lin_evac", s, 4 * i + 4))
                    if kind == "T":
                        sp.dma_start(dst[ds(c * CW, CW), :].rearrange("(f p) t -> p f t", p=P),
                                     stage[s][:, :].rearrange("p (f t) -> p f t", f=2)).then_inc(stored[s], 16)
                    else:
                        sp.dma_start(dst[:, ds(c * width, width)].rearrange("(i p) n -> p i n", p=P),
                                     stage[s][:, :].rearrange("p (i n) -> p i n", i=NT)).then_inc(stored[s], 16)

                pairs, s0 = n // 2, lin.s0
                if pairs:
                    for s in range(2):
                        lin.load(sp, s, 0, s ^ s0)

                    def ahead_by_two(j):
                        i = j + 1
                        for s in range(2):
                            lin.load(sp, 2 * i + s, i, s ^ s0)
                            store(2 * i + s - 2, i - 1, s ^ s0)
                    looped(sp, pairs - 1, ahead_by_two)
                if n % 2:
                    lin.load(sp, n - 1, n // 2, s0)
                for s in range(2 if pairs else 0):
                    store(2 * pairs - 2 + s, pairs - 1, s ^ s0)
                if ahead:
                    ahead.early(sp, "load", 2)
                if n % 2:
                    store(n - 1, n // 2, s0)
                for s in range(2):
                    if lin.uses[s]:
                        sp.wait_ge(stored[s], 16 * lin.uses[s])

            @block.scalar
            def _(act):
                lin.split_hi(act)
                if ahead:
                    ahead.early(act, "hi", 1)

            @block.gpsimd
            def _(pool):
                lin.split_lo(pool)
                if ahead:
                    ahead.early(pool, "lo", 1)

            @block.tensor
            def _(pe):
                lin.products(pe)

            @block.vector
            def _(dve):
                if bias is not None:
                    dve.wait_ge(bias_in, 16)

                def step(c, i, s):
                    reached(dve, stored[s], 16 * i)
                    for b in range(4):
                        dve.wait_ge(*lin.at("lin_mm", s, 4 * i + b + 1))
                        if kind == "T":
                            dst_, src = stage[s][:, 512 * b:512 * b + 512], lin.out(s, b)[:, :]
                            if bias is None:
                                e = dve.tensor_copy(dst_, src)
                            else:
                                e = dve.tensor_scalar(dst_, src, bt[:, ds(c * 2 + b // 2, 1)], None, ALU.add)
                            e.then_inc(k.wsem["lin_evac"][s], 1)
                        elif bias is None:
                            dve.tensor_copy(stage[s][:, 2 * b * width:2 * (b + 1) * width],
                                            lin.out(s, b)[:, 0:2 * width]).then_inc(k.wsem["lin_evac"][s], 1)
                        else:
                            for j in range(2):
                                e = dve.tensor_tensor(stage[s][:, (2 * b + j) * width:(2 * b + j + 1) * width],
                                                      lin.out(s, b)[:, j * width:(j + 1) * width],
                                                      bt[:, ds(c * width, width)], ALU.add)
                            e.then_inc(k.wsem["lin_evac"][s], 1)
                lin.chunks(dve, step)


def scaled_residual(k, dve, brow, done):
    for i in range(NT):
        dve.scalar_tensor_tensor(out=k.x[:, i, :], in0=k.x[:, i, :], scalar=ALPHA, in1=brow,
                                 op0=ALU.mult, op1=ALU.add).then_inc(done, 1)
    dve.wait_ge(done, NT)


def project_residual(k, name, lin, gate=None, bias=None, ahead=None):
    nc, n = k.nc, lin.n
    with ExitStack() as c:
        scaled, bias_in, gated = (k.sem(f"{name}_{x}") for x in ("scaled", "bias_in", "gated"))
        brow = k.sb(c, f"{name}_bias", [P, D]) if bias is not None else None
        tmp = k.sb(c, f"{name}_gated", [P, 2, CW])
        with nc.Block() as block:
            @block.sync
            def _(sp):
                if bias is not None:
                    sp.dma_start(brow[:, :], rows(bias)).then_inc(bias_in, 16)
                lin.chunks(sp, lambda c, i, s: lin.load(sp, c, i, s))
                if ahead:
                    ahead.early(sp, "load", 2)

            @block.scalar
            def _(act):
                lin.split_hi(act)
                if ahead:
                    ahead.early(act, "hi", 1)

            @block.gpsimd
            def _(pool):
                lin.split_lo(pool)
                if ahead:
                    ahead.early(pool, "lo", 1)

            @block.tensor
            def _(pe):
                lin.products(pe)

            @block.vector
            def _(dve):
                if bias is not None:
                    dve.wait_ge(bias_in, 16)
                    scaled_residual(k, dve, brow[:, :], scaled)

                def step(c, i, s):
                    for b in range(4):
                        dve.wait_ge(*lin.at("lin_mm", s, 4 * i + b + 1))
                        for j in range(2):
                            src = lin.out(s, b)[:, j * CW:(j + 1) * CW]
                            xt = k.x[:, 2 * b + j, ds(c * CW, CW)]
                            if gate is not None:
                                m = dve.tensor_tensor(tmp[:, j, :], src, gate[:, ds(c * CW, CW)], ALU.mult)
                                m.then_inc(gated, 1)
                                dve.wait_ge(gated, c * 8 + (2 * b + j + 1))
                                src = tmp[:, j, :]
                            e = dve.tensor_tensor(xt, xt, src, ALU.add)
                        e.then_inc(k.wsem["lin_evac"][s], 1)
                        if isinstance(c, int) and c == n - 1:
                            dve.wait_ge(*lin.at("lin_evac", s, 4 * i + b + 1))
                            for tile in (2 * b, 2 * b + 1):
                                k.x_stats(dve, tile)
                lin.chunks(dve, step)
                for s in range(2):
                    dve.wait_ge(*lin.at("lin_evac", s, 4 * (n // 2)))



class Slots:

    def __init__(self, k, uses, w_up, w_down):
        self.k, self.uses, self.first = k, uses, (w_up[0, :, :], w_down[0, :, :])
        self.early_done = {"load": 0, "hi": 0, "lo": 0}
        self.base = {name: list(v) for name, v in k.wbase.items()}
        for s in range(2):
            k.wbase["w_loaded"][s] += 16 * uses[s]
            k.wbase["w_hi_done"][s] += uses[s]
            k.wbase["w_ready"][s] += uses[s]

    def at(self, name, s, count):
        return self.k.wsem[name][s], self.base[name][s] + count

    def early(self, e, what, upto):
        for s in range(self.early_done[what], upto):
            if what == "load":
                self.load(e, s, 0, self.first[s])
            else:
                {"hi": self.split_hi, "lo": self.split_lo}[what](e, s, 0)
        self.early_done[what] = max(self.early_done[what], upto)

    def own(self, what, s, use):
        return not isinstance(use, int) or use > 0 or s >= self.early_done[what]

    def load(self, sp, s, use, src):
        if self.own("load", s, use):
            sp.wait_ge(*self.at("w_ready", s, use))
            sp.dma_start(self.k.w_raw[s][:, :], src).then_inc(self.k.wsem["w_loaded"][s], 16)

    def split_hi(self, act, s, use):
        if self.own("hi", s, use):
            act.wait_ge(*self.at("w_loaded", s, 16 * use + 16))
            if isinstance(use, int) and use == 0:
                act.wait_ge(*self.at("lin_mm", s, 0))
            act.activation(self.k.w_hi[s][:, :], self.k.w_raw[s][:, :], ACT.Copy)\
               .then_inc(self.k.wsem["w_hi_done"][s], 1)

    def split_lo(self, pool, s, use):
        if self.own("lo", s, use):
            pool.wait_ge(*self.at("w_hi_done", s, use + 1))
            pool.tensor_tensor(self.k.w_lo[s][:, :], self.k.w_raw[s][:, :], self.k.w_hi[s][:, :].bitcast(F),
                               ALU.subtract).then_inc(self.k.wsem["w_ready"][s], 1)


def up_products(k, pe, hh, hl, mm):
    for f in range(2):
        for half in range(2):
            b = 2 * f + half
            for t in range(KT):
                for w, h in ((k.w_hi[0], hh), (k.w_lo[0], hh), (k.w_hi[0], hl)):
                    m = pe.matmul(k.bank[b][:, :], w[:, t * CW + f * P:t * CW + (f + 1) * P],
                                  h[:, t, half * 512:half * 512 + 512],
                                  start=t == 0 and w is k.w_hi[0] and h is hh,
                                  stop=t == KT - 1 and h is hl)
            m.then_inc(mm, 1)


def down_products(k, pe, a_hi, a_lo, out, mm, waits):
    tile, half = out // 2, out % 2
    waits()
    for f in range(2):
        for n, (w, a) in enumerate(((k.w_hi[1], a_hi), (k.w_lo[1], a_hi), (k.w_hi[1], a_lo))):
            m = pe.matmul(k.bank[4 + out % 4][:, :], a[:, f, tile * P:(tile + 1) * P],
                          w[:, f * D + half * 512:f * D + half * 512 + 512],
                          start=f == 0 and n == 0, stop=f == 1 and n == 2)
    m.then_inc(mm, 1)


def ffn_conv(k, wt, w_up, w_down, conv, hh, hl, gate):
    nc = k.nc
    G = NF1 // 2
    PAD = 2
    with ExitStack() as c:
        sem = lambda n: k.sem("ffn1_" + n)
        raw = [k.sb(c, f"ffn1_raw{s}", [P, 2, PAD + S]) for s in range(2)]
        u = [k.sb(c, f"ffn1_u{s}", [P, 2, S]) for s in range(2)]
        a_hi = k.sb(c, "ffn1_a_hi", [P, 2, S], R)
        a_lo = k.sb(c, "ffn1_a_lo", [P, 2, S], R)
        cw = k.sb(c, "ffn1_conv", [P, NF1, 2, 4])
        tmp = k.sb(c, "ffn1_gated", [P, 2, 512])
        conv_in, padded, up_mm, up_out, conved, silued, prod, mult, a_hi_done, a_lo_done, dn_mm, dn_out, gated = (
            sem(n) for n in ("conv_in", "padded", "up_mm", "up_out", "conved", "silued", "prod", "mult",
                             "a_hi", "a_lo", "dn_mm", "dn_out", "gated"))
        with nc.Block() as block:
            @block.sync
            def _(sp):
                sp.dma_start(cw[:, :, :, :], conv).then_inc(conv_in, 16)
                wt.load(sp, 0, 0, w_up[0, :, :])
                wt.load(sp, 0, 1, w_up[1, :, :])
                wt.load(sp, 1, 0, w_down[0, :, :])

                def body(j):
                    g = j + 1
                    wt.load(sp, 0, 2 * g, w_up[2 * g, :, :])
                    wt.load(sp, 0, 2 * g + 1, w_up[2 * g + 1, :, :])
                    wt.load(sp, 1, g, w_down[g, :, :])
                looped(sp, G - 1, body)

            @block.tensor
            def _(pe):
                def up(n):
                    pe.wait_ge(*wt.at("w_ready", 0, n + 1))
                    pe.wait_ge(up_out, 4 * n)
                    up_products(k, pe, hh, hl, up_mm)

                def down(g, outs):
                    pe.wait_ge(*wt.at("w_ready", 1, g + 1))
                    pe.wait_ge(a_lo_done, 2 * g + 2)
                    for o in outs:
                        free = 16 * g + o - 3
                        down_products(k, pe, a_hi, a_lo, o, dn_mm,
                                      (lambda: pe.wait_ge(dn_out, free)) if not isinstance(g, int) or free > 0
                                      else (lambda: None))
                up(0)
                up(1)
                up(2)
                down(0, range(8))
                up(3)
                down(0, range(8, 16))

                def body(j):
                    g = j + 2
                    up(2 * g)
                    down(g - 1, range(8))
                    up(2 * g + 1)
                    down(g - 1, range(8, 16))
                looped(pe, G - 2, body)
                down(G - 1, range(16))

            @block.scalar
            def _(act):
                def evac(n, s):
                    for b in range(4):
                        act.wait_ge(up_mm, 4 * n + b + 1)
                        if b == 0:
                            act.wait_ge(conved, 2 * (n - 1) if isinstance(n, int) and n < 2 else 2 * (n - 1))
                        act.activation(raw[s][:, b // 2, PAD + (b % 2) * 512:PAD + (b % 2) * 512 + 512],
                                       k.bank[b][:, :], ACT.Copy).then_inc(up_out, 1)

                def evac_first(n, s):
                    for b in range(4):
                        act.wait_ge(up_mm, 4 * n + b + 1)
                        act.activation(raw[s][:, b // 2, PAD + (b % 2) * 512:PAD + (b % 2) * 512 + 512],
                                       k.bank[b][:, :], ACT.Copy).then_inc(up_out, 1)

                def w_up_hi(n):
                    reached(act, up_mm, 4 * n)
                    wt.split_hi(act, 0, n)

                def w_down_hi(g):
                    act.wait_ge(dn_mm, 16 * g)
                    wt.split_hi(act, 1, g)

                def silu(n, s):
                    act.wait_ge(conved, 2 * n + 2)
                    act.activation(u[s][:, 1, :], u[s][:, 1, :], ACT.Silu).then_inc(silued, 1)

                def a_part(n, s):
                    act.wait_ge(mult, n + 1)
                    act.activation(a_hi[:, s, :], u[s][:, 0, :], ACT.Copy).then_inc(a_hi_done, 1)

                w_up_hi(0)
                evac_first(0, 0)
                w_up_hi(1)
                silu(0, 0)
                evac_first(1, 1)
                w_up_hi(2)
                w_down_hi(0)
                a_part(0, 0)
                silu(1, 1)
                a_part(1, 1)

                def body(j):
                    g = j + 1
                    evac(2 * g, 0)
                    w_up_hi(2 * g + 1)
                    silu(2 * g, 0)
                    evac(2 * g + 1, 1)
                    w_up_hi(2 * g + 2)
                    w_down_hi(g)
                    a_part(2 * g, 0)
                    silu(2 * g + 1, 1)
                    a_part(2 * g + 1, 1)
                looped(act, G - 2, body)
                g = G - 1
                evac(2 * g, 0)
                w_up_hi(2 * g + 1)
                silu(2 * g, 0)
                evac(2 * g + 1, 1)
                w_down_hi(g)
                a_part(2 * g, 0)
                silu(2 * g + 1, 1)
                a_part(2 * g + 1, 1)

            @block.gpsimd
            def _(pool):
                for s in range(2):
                    pool.memset(raw[s][:, :, 0:PAD], 0.0).then_inc(padded, 1)

                def a_part(n, s):
                    pool.wait_ge(a_hi_done, n + 1)
                    pool.tensor_tensor(a_lo[:, s, :], u[s][:, 0, :], a_hi[:, s, :].bitcast(F),
                                       ALU.subtract).then_inc(a_lo_done, 1)

                def group(g, more):
                    wt.split_lo(pool, 0, 2 * g + 1)
                    if more:
                        wt.split_lo(pool, 0, 2 * g + 2)
                    wt.split_lo(pool, 1, g)
                    a_part(2 * g, 0)
                    a_part(2 * g + 1, 1)
                wt.split_lo(pool, 0, 0)
                looped(pool, G - 1, lambda g: group(g, True))
                group(G - 1, False)

            @block.vector
            def _(dve):
                dve.wait_ge(conv_in, 16)
                dve.wait_ge(padded, 2)

                def conv_steps(n, s, first):
                    dve.wait_ge(up_out, 4 * n + 4)
                    if not first:
                        dve.wait_ge(a_lo_done, n - 1)
                    for v in range(2):
                        co = lambda j: cw[:, n, v, j:j + 1] if isinstance(n, int) else cw[:, ds(n, 1), v, j]
                        dve.tensor_scalar(u[s][:, v, :], raw[s][:, v, 2:2 + S], co(2), co(3),
                                          ALU.mult, ALU.add).then_inc(prod, 1)
                    for j in (1, 0):
                        for v in range(2):
                            co = cw[:, n, v, j:j + 1] if isinstance(n, int) else cw[:, ds(n, 1), v, j]
                            dve.wait_ge(prod, n * 4 + (1 - j) * 2 + v + 1)
                            dve.scalar_tensor_tensor(out=u[s][:, v, :], in0=raw[s][:, v, j:j + S], scalar=co,
                                                     in1=u[s][:, v, :], op0=ALU.mult, op1=ALU.add)\
                               .then_inc(prod if j else conved, 1)
                    dve.wait_ge(silued, n + 1)
                    dve.tensor_tensor(u[s][:, 0, :], u[s][:, 0, :], u[s][:, 1, :], ALU.mult).then_inc(mult, 1)

                def add_down(g, outs):
                    for o in outs:
                        tile, half = o // 2, o % 2
                        cols = slice(half * 512, half * 512 + 512)
                        dve.wait_ge(dn_mm, 16 * g + o + 1)
                        dve.tensor_tensor(tmp[:, o % 2, :], k.bank[4 + o % 4][:, :], gate[:, cols], ALU.mult)\
                           .then_inc(gated, 1)
                        dve.wait_ge(gated, 16 * g + o + 1)
                        dve.tensor_tensor(k.x[:, tile, cols], k.x[:, tile, cols], tmp[:, o % 2, :], ALU.add)\
                           .then_inc(dn_out, 1)
                        if isinstance(g, int) and g == G - 1 and o % 2 and o > 1:
                            k.x_stats(dve, tile - 1)

                conv_steps(0, 0, True)
                conv_steps(1, 1, True)

                def body(j):
                    g = j + 1
                    add_down(g - 1, range(8))
                    conv_steps(2 * g, 0, False)
                    add_down(g - 1, range(8, 16))
                    conv_steps(2 * g + 1, 1, False)
                looped(dve, G - 1, body)
                add_down(G - 1, range(16))
                dve.wait_ge(dn_out, 16 * G)
                k.x_stats(dve, NT - 1)


def ffn_squared_relu(k, wt, w_up, w_down, b_up, b_down, hh, hl):
    nc = k.nc
    G = F2C
    with ExitStack() as c:
        sem = lambda n: k.sem("ffn2_" + n)
        r = k.sb(c, "ffn2_relu", [P, 2, S])
        a_hi = k.sb(c, "ffn2_a_hi", [P, 2, S], R)
        a_lo = k.sb(c, "ffn2_a_lo", [P, 2, S], R)
        bu = k.sb(c, "ffn2_b_up", [P, 2 * G])
        brow = k.sb(c, "ffn2_b_down", [P, D])
        bias_in, scaled, up_mm, up_out, squared, a_hi_done, a_lo_done, dn_mm, dn_out = (
            sem(n) for n in ("bias_in", "scaled", "up_mm", "up_out", "squared", "a_hi", "a_lo", "dn_mm", "dn_out"))
        with nc.Block() as block:
            @block.sync
            def _(sp):
                sp.dma_start(bu[:, :], b_up).then_inc(bias_in, 16)
                sp.dma_start(brow[:, :], rows(b_down)).then_inc(bias_in, 16)

                def body(g):
                    wt.load(sp, 0, g, w_up[g, :, :])
                    wt.load(sp, 1, g, w_down[g, :, :])
                looped(sp, G, body)

            @block.tensor
            def _(pe):
                def up(g):
                    pe.wait_ge(*wt.at("w_ready", 0, g + 1))
                    pe.wait_ge(up_out, 4 * g)
                    up_products(k, pe, hh, hl, up_mm)

                def down(g):
                    pe.wait_ge(*wt.at("w_ready", 1, g + 1))
                    pe.wait_ge(a_lo_done, g + 1)
                    for o in range(16):
                        free = 16 * g + o - 3
                        down_products(k, pe, a_hi, a_lo, o, dn_mm,
                                      (lambda: pe.wait_ge(dn_out, free)) if not isinstance(g, int) or free > 0
                                      else (lambda: None))
                up(0)
                up(1)
                down(0)

                def body(j):
                    up(j + 2)
                    down(j + 1)
                looped(pe, G - 2, body)
                down(G - 1)

            @block.scalar
            def _(act):
                def w_up_hi(g):
                    act.wait_ge(up_mm, 4 * g)
                    wt.split_hi(act, 0, g)

                def group(g, more):
                    if more:
                        w_up_hi(g + 1)
                    act.wait_ge(dn_mm, 16 * g)
                    wt.split_hi(act, 1, g)
                    act.wait_ge(squared, g + 1)
                    act.activation(a_hi[:, :, :], r[:, :, :], ACT.Copy).then_inc(a_hi_done, 1)
                w_up_hi(0)
                looped(act, G - 1, lambda g: group(g, True))
                group(G - 1, False)

            @block.gpsimd
            def _(pool):
                def group(g, more):
                    if more:
                        wt.split_lo(pool, 0, g + 1)
                    wt.split_lo(pool, 1, g)
                    pool.wait_ge(a_hi_done, g + 1)
                    pool.tensor_tensor(a_lo[:, :, :], r[:, :, :], a_hi[:, :, :].bitcast(F),
                                       ALU.subtract).then_inc(a_lo_done, 1)
                wt.split_lo(pool, 0, 0)
                looped(pool, G - 1, lambda g: group(g, True))
                group(G - 1, False)

            @block.vector
            def _(dve):
                dve.wait_ge(bias_in, 32)
                scaled_residual(k, dve, brow[:, :], scaled)

                def square(g):
                    dve.wait_ge(a_lo_done, g)
                    for b in range(4):
                        dve.wait_ge(up_mm, 4 * g + b + 1)
                        dve.tensor_scalar(r[:, b // 2, (b % 2) * 512:(b % 2) * 512 + 512], k.bank[b][:, :],
                                          bu[:, ds(2 * g + b // 2, 1)], 0.0, ALU.add, ALU.max).then_inc(up_out, 1)
                    dve.wait_ge(up_out, 4 * g + 4)
                    dve.tensor_tensor(r[:, :, :], r[:, :, :], r[:, :, :], ALU.mult).then_inc(squared, 1)

                def add_down(g):
                    for o in range(16):
                        xt = k.x[:, o // 2, (o % 2) * 512:(o % 2) * 512 + 512]
                        dve.wait_ge(dn_mm, 16 * g + o + 1)
                        dve.tensor_tensor(xt, xt, k.bank[4 + o % 4][:, :], ALU.add).then_inc(dn_out, 1)
                        if isinstance(g, int) and g == G - 1 and o % 2 and o > 1:
                            dve.wait_ge(dn_out, 16 * g + o - 1)
                            k.x_stats(dve, o // 2 - 1)
                square(0)

                def body(j):
                    square(j + 1)
                    add_down(j)
                looped(dve, G - 1, body)
                add_down(G - 1)
                dve.wait_ge(dn_out, 16 * G)
                k.x_stats(dve, NT - 1)



def pipelined(e, bodies, per, stages):
    deepest = max(lag for lag, _ in stages)
    for m in range(per):
        for lag, stage in stages:
            if m >= lag:
                stage(m - lag, m - lag, 0)

    def body(b):
        for m in range(per):
            for lag, stage in stages:
                pos = (m - lag) % per
                stage((b + 1) * per + m - lag, pos, b + 1 if m >= lag else b)
    looped(e, bodies - 1, body, peel=0)
    for m in range(deepest):
        for lag, stage in stages:
            if m < lag:
                stage(bodies * per + m - lag, (m - lag) % per, bodies - 1)


def reached(e, sem, value):
    if not isinstance(value, int) or value > 0:
        e.wait_ge(sem, value)


def stick_breaking(k, qkT, v, mix, lin, lin_dst):
    nc = k.nc
    with ExitStack() as c:
        sem = lambda n: k.sem("sb_" + n)
        q = [k.sb(c, f"sb_q{s}", [HD, S]) for s in range(2)]
        kk = [k.sb(c, f"sb_k{s}", [HD, S]) for s in range(2)]
        vv = [k.sb(c, f"sb_v{s}", [P, NT, HD]) for s in range(2)]
        soft = [k.sb(c, f"sb_soft{s}", [P, S]) for s in range(2)]
        wgt = [k.sb(c, f"sb_wgt{s}", [P, S]) for s in range(2)]
        wT = [k.sb(c, f"sb_wT{s}", [P, NT, P]) for s in range(2)]
        o = [k.sb(c, f"sb_o{s}", [P, NT, HD]) for s in range(2)]
        keep = k.sb(c, "sb_keep", [P, P])
        limit = k.sb(c, "sb_limit", [P, P])
        eighth = k.sb(c, "sb_eighth", [HD, P])
        LW = lin.width
        stage = [k.sb(c, f"sb_stage{s}", [P, NT // 2, LW]) for s in range(2)]
        lin_stored = [sem(f"lin_stored{s}") for s in range(2)]
        hi_lo = sem("hi_lo")
        made = sem("keep_made")
        loaded = [sem(f"loaded{s}") for s in range(2)]
        scaled_q = [sem(f"scaled_q{s}") for s in range(2)]
        stored = [sem(f"stored{s}") for s in range(2)]
        z_done, step_a, soft_done, plus, masked, summed, diff, cut, w_done, turned, wT_done, pv, out = (
            sem(n) for n in ("z", "act_step", "soft", "plus", "masked", "summed", "diff", "cut", "w",
                             "turned", "wT", "pv", "out"))
        bodies, per = SB_HEADS // 2, 2 * NT
        zs = lambda n, lo, hi: k.psum[:, 1024 * (n % 2) + lo:1024 * (n % 2) + hi]
        par = lambda pos: pos % 2
        assert lin.n == 2 * bodies
        LATE = 4
        slot = lambda pos: (pos // NT) ^ lin.s0

        with nc.Block() as block:
            @block.sync
            def _(sp):
                def load(j, s):
                    h = 2 * j + s
                    reached(sp, out, NT * (h - 1))
                    sp.dma_start(q[s][:, :], qkT[ds(h * HD, HD), :]).then_inc(loaded[s], 16)
                    sp.dma_start(kk[s][:, :], qkT[ds(SB_HEADS * HD + h * HD, HD), :]).then_inc(loaded[s], 16)
                    sp.dma_start(vv[s][:, :, :], v[:, ds(h * HD, HD)].rearrange("(i p) d -> p i d", p=P))\
                      .then_inc(loaded[s], 16)

                def store(j, s):
                    sp.wait_ge(out, 8 * (2 * j + s + 1))
                    sp.dma_start(mix[:, ds((2 * j + s) * HD, HD)].rearrange("(i p) d -> p i d", p=P),
                                 o[s][:, :, :]).then_inc(stored[s], 16)
                def store_lin(j, half):
                    sl, use = (half // 2) ^ lin.s0, NT * j + 4 * (half % 2) + 4
                    sp.wait_ge(*lin.at("lin_evac", sl, use))
                    sp.dma_start(lin_dst[(half % 2) * 512:(half % 2) * 512 + 512, ds((2 * j + half // 2) * LW, LW)]
                                 .rearrange("(i p) n -> p i n", p=P), stage[half % 2][:, :, :])\
                      .then_inc(lin_stored[half % 2], 16)
                load(0, 0)
                load(0, 1)
                for s in range(2):
                    lin.load(sp, s, 0, s ^ lin.s0)

                def body(j, more=True):
                    store_lin(j, 0)
                    if more:
                        lin.load(sp, 2 * j + 2, j + 1, lin.s0)
                    if more:
                        load(j + 1, 0)
                    store_lin(j, 1)
                    store(j, 0)
                    store_lin(j, 2)
                    if more:
                        lin.load(sp, 2 * j + 3, j + 1, 1 ^ lin.s0)
                        load(j + 1, 1)
                    store_lin(j, 3)
                    store(j, 1)
                looped(sp, bodies - 1, body)
                body(bodies - 1, more=False)
                for s in range(2):
                    sp.wait_ge(stored[s], 16 * bodies)
                    sp.wait_ge(lin_stored[s], 16 * lin.n)

            @block.gpsimd
            def _(pool):
                pool.memset(keep[:, :], 1.0).then_inc(made, 1)
                pool.memset(limit[:, :], 0.0).then_inc(made, 1)
                pool.memset(eighth[:, :], HD ** -0.5).then_inc(made, 1)
                pool.wait_ge(made, 3)
                for tile, fill in ((keep, 0.0), (limit, NEG)):
                    pool.affine_select(out=tile[:, :], in_=tile[:, :], compare_op=ALU.is_gt, fill=fill, base=0,
                                       pattern=[[-1, P]], channel_multiplier=1).then_inc(made, 1)
                pool.wait_ge(made, 5)

                def scale_q(n, pos, j):
                    if pos % NT == 0:
                        s = pos // NT
                        pool.wait_ge(loaded[s], 48 * (j + 1))
                        pool.tensor_tensor(q[s][:, :], q[s][:, :], eighth[:, 0:1].broadcast_to([HD, S]), ALU.mult)\
                            .then_inc(scaled_q[s], 1)

                def cut_diagonal(n, pos, j):
                    i = pos % NT
                    blk = wgt[par(pos)][:, i * P:(i + 1) * P]
                    pool.wait_ge(diff, n + 1)
                    pool.tensor_tensor(blk, blk, limit[:, :], ALU.add).then_inc(cut, 1)
                def split_lo(n, pos, j):
                    part, sl = pos % NT, slot(pos)
                    if part < 4:
                        if part == 0:
                            pool.wait_ge(*lin.at("w_hi_done", sl, j + 1))
                        cols = slice(part * KT * LW // 4, (part + 1) * KT * LW // 4)
                        lo = pool.tensor_tensor(k.w_lo[sl][:, cols], k.w_raw[sl][:, cols],
                                                k.w_hi[sl][:, cols].bitcast(F), ALU.subtract)
                        if part == 3:
                            lo.then_inc(k.wsem["w_ready"][sl], 1)
                pipelined(pool, bodies, per, [(0, scale_q), (1, cut_diagonal), (0, split_lo)])

            @block.tensor
            def _(pe):
                def scores(n, pos, j):
                    s, i = pos // NT, pos % NT
                    L = (i + 1) * P
                    if i == 0:
                        pe.wait_ge(scaled_q[s], j + 1)
                    reached(pe, diff, n - 1)
                    for a in range(0, L, 512):
                        b = min(L, a + 512)
                        mm = pe.matmul(zs(pos, a, b), q[s][:, i * P:(i + 1) * P], kk[s][:, a:b],
                                       start=True, stop=True)
                    mm.then_inc(z_done, 1)

                def turn_w(n, pos, j):
                    i = pos % NT
                    pe.wait_ge(w_done, n + 1)
                    reached(pe, wT_done, n)
                    for b in range(i + 1):
                        mm = pe.transpose(k.bank[4 + b // 4][:, (b % 4) * P:(b % 4 + 1) * P],
                                          wgt[par(pos)][:, b * P:(b + 1) * P], k.ident[:, :])
                    mm.then_inc(turned, 1)

                def values(n, pos, j):
                    s, i = pos // NT, pos % NT
                    pe.wait_ge(wT_done, n + 1)
                    reached(pe, out, n)
                    for b in range(i + 1):
                        mm = pe.matmul(k.bank[6][:, 0:HD], wT[par(pos)][:, b, :], vv[s][:, b, :],
                                       start=b == 0, stop=b == i)
                    mm.then_inc(pv, 1)
                def project_tile(n, pos, j):
                    tile, sl = pos % NT, slot(pos)
                    if tile == 0:
                        pe.wait_ge(*lin.at("w_ready", sl, j + 1))
                    before = (sl, NT * j + tile) if tile else (sl ^ 1, NT * j + (NT if pos else 0))
                    pe.wait_ge(*lin.at("lin_evac", *before))
                    w2 = k.w_hl[sl][:, :, :]
                    for t in range(KT):
                        tokens = slice(tile * P, (tile + 1) * P)
                        pe.matmul(k.bank[7][:, 0:2 * LW].rearrange("p (a n) -> p a n", a=2),
                                  lin.hh[:, t, tokens], w2[:, :, t * LW:(t + 1) * LW], start=t == 0, stop=False)
                        mm = pe.matmul(k.bank[7][:, 0:LW], lin.hl[:, t, tokens], w2[:, 0, t * LW:(t + 1) * LW],
                                       start=False, stop=t == KT - 1)
                    mm.then_inc(k.wsem["lin_mm"][sl], 1)
                pipelined(pe, bodies, per, [(0, scores), (LATE, project_tile), (2, turn_w), (3, values)])

            @block.scalar
            def _(act):
                act.preload_act_table_set("natural_log_exp_and_others")

                def softplus_part(n, pos, j):
                    L = (pos % NT + 1) * P
                    e = soft[par(pos)][:, 0:L]
                    act.wait_ge(z_done, n + 1)
                    reached(act, plus, n - 1)
                    act.activation(e, zs(pos, 0, L), ACT.Abs).then_inc(step_a, 1)
                    act.wait_ge(step_a, 2 * n + 1)
                    act.activation(e, e, ACT.Exp, scale=-1.0).then_inc(step_a, 1)
                    act.wait_ge(step_a, 2 * n + 2)
                    act.activation(e, e, ACT.Ln, bias=1.0).then_inc(soft_done, 1)

                def weights(n, pos, j):
                    L = (pos % NT + 1) * P
                    act.wait_ge(cut, n + 1)
                    act.activation(wgt[par(pos)][:, 0:L], wgt[par(pos)][:, 0:L], ACT.Exp).then_inc(w_done, 1)

                def copy_turned(n, pos, j):
                    i = pos % NT
                    act.wait_ge(turned, n + 1)
                    reached(act, pv, n - 1)
                    act.activation(wT[par(pos)][:, 0:i + 1, :],
                                   k.psum[:, 2048:2048 + (i + 1) * P].rearrange("p (a b) -> p a b", b=P),
                                   ACT.Copy).then_inc(wT_done, 1)
                def split_hi(n, pos, j):
                    if pos % NT == 0:
                        lin.hi(act, 2 * j + pos // NT, j, slot(pos))
                pipelined(act, bodies, per, [(0, split_hi), (0, softplus_part), (1, weights), (2, copy_turned)])

            @block.vector
            def _(dve):
                dve.wait_ge(made, 5)

                def suffix(n, pos, j):
                    i = pos % NT
                    L = (i + 1) * P
                    w = wgt[par(pos)]
                    dve.wait_ge(soft_done, n + 1)
                    reached(dve, turned, n - 1)
                    dve.scalar_tensor_tensor(out=w[:, 0:L], in0=zs(pos, 0, L), scalar=0.0,
                                             in1=soft[par(pos)][:, 0:L], op0=ALU.max, op1=ALU.add)\
                       .then_inc(plus, 1)
                    dve.wait_ge(plus, n + 1)
                    dve.tensor_tensor(w[:, L - P:L], w[:, L - P:L], keep[:, :], ALU.mult).then_inc(masked, 1)
                    dve.wait_ge(masked, n + 1)
                    back = w[:, 0:L][:, ::-1]
                    dve.tensor_tensor_scan(back, back, back, 0.0, ALU.add, ALU.max).then_inc(summed, 1)
                    dve.wait_ge(summed, n + 1)
                    dve.tensor_tensor(w[:, 0:L], zs(pos, 0, L), w[:, 0:L], ALU.subtract).then_inc(diff, 1)

                def output(n, pos, j):
                    s, i = pos // NT, pos % NT
                    dve.wait_ge(pv, n + 1)
                    if i == 0:
                        dve.wait_ge(stored[s], 16 * j)
                    dve.tensor_copy(o[s][:, i, :], k.bank[6][:, 0:HD]).then_inc(out, 1)

                def stage_lin(n, pos, j):
                    tile, sl, half = pos % NT, slot(pos), pos % NT // 4
                    dve.wait_ge(*lin.at("lin_mm", sl, NT * j + tile + 1))
                    if tile % 4 == 0:
                        reached(dve, lin_stored[half], 16 * (2 * j + pos // NT))
                    dve.tensor_copy(stage[half][:, tile % 4, :], k.bank[7][:, LW:2 * LW]).then_inc(hi_lo, 1)
                    dve.wait_ge(hi_lo, n + 1)
                    dve.tensor_tensor(stage[half][:, tile % 4, :], k.bank[7][:, 0:LW], stage[half][:, tile % 4, :],
                                      ALU.add).then_inc(k.wsem["lin_evac"][sl], 1)
                pipelined(dve, bodies, per, [(LATE, stage_lin), (0, suffix), (3, output)])


def gla(k, gqT, pn, gf, w_fg, b_fg, g_out, mix, ahead=None):
    nc = k.nc
    KW, VW = GLA_HEADS * DK, GLA_HEADS * DV
    NC = S // CHUNK
    with ExitStack() as c:
        sem = lambda n: k.sem("gla_" + n)
        qT = k.sb(c, "gla_qT", [P, 2, S])
        kd = k.sb(c, "gla_k", [P, NT, KW])
        v = k.sb(c, "gla_v", [P, NT, VW])
        gg = k.sb(c, "gla_gate", [P, NT, VW])
        f = k.sb(c, "gla_f", [P, NT, RANK])
        fT = k.sb(c, "gla_fT", [RANK + 1, S])
        wfg = k.sb(c, "gla_wfg", [RANK + 1, KW])
        grow = k.sb(c, "gla_g", [P, VW])
        la = [k.sb(c, f"gla_la{s}", [P, KW]) for s in range(2)]
        ex = [k.sb(c, f"gla_ex{s}", [P, KW]) for s in range(2)]
        dec = [k.sb(c, f"gla_dec{s}", [P, KW]) for s in range(2)]
        decay = k.sb(c, "gla_decay", [P, 2, NC])
        state = k.sb(c, "gla_state", [P, 2, NC, DV])
        later = k.sb(c, "gla_later", [P, P])
        inchunk = k.sb(c, "gla_inchunk", [P, 2])
        eps = k.sb(c, "gla_eps", [P, 1])
        junk = k.sb(c, "gla_junk", [P, DV])
        ss = k.sb(c, "gla_ss", [P, NT * GLA_HEADS])
        rs = k.sb(c, "gla_rs", [P, NT * GLA_HEADS])
        o = [k.sb(c, f"gla_o{s}", [P, VW]) for s in range(2)]
        (in_f, in_w, in_qkv, in_g, made, f_turned, f_copied, pre, abs_done, exp_done, ln_done, la_done,
         suffix, dec_done, kd_done, total, decay_done, silued, gated, kv, stated, outp, sq, std, rstd,
         scaled, o_done) = (sem(n) for n in (
             "in_f", "in_w", "in_qkv", "in_g", "made", "f_turned", "f_copied", "pre", "abs", "exp", "ln",
             "la", "suffix", "dec", "kd", "total", "decay", "silu", "gated", "kv", "state", "out", "sq",
             "std", "rstd", "scaled", "o"))
        stored = [sem(f"stored{s}") for s in range(2)]
        TURN, PRE, SUF, TOT = k.bank[0], k.bank[1], k.bank[2], k.bank[3]

        def head_out(i, h):
            return k.bank[2 * (i % 2) + h % 2][:, (h // 2) * DV:(h // 2 + 1) * DV]
        with nc.Block() as block:
            @block.sync
            def _(sp):
                sp.dma_start(f[:, :, :], gf.rearrange("(i p) n -> p i n", p=P)).then_inc(in_f, 16)
                sp.wait_ge(made, 2)
                sp.dma_start(wfg[0:RANK, :], w_fg).then_inc(in_w, 16)
                sp.dma_start(wfg[RANK:RANK + 1, :], b_fg.rearrange("(a n) -> a n", a=1)).then_inc(in_w, 16)
                sp.dma_start(kd[:, :, :], pn[:, 0:KW].rearrange("(i p) n -> p i n", p=P)).then_inc(in_qkv, 16)
                sp.dma_start(v[:, :, :], pn[:, KW:KW + VW].rearrange("(i p) n -> p i n", p=P)).then_inc(in_qkv, 16)
                sp.dma_start(qT[:, :, :], gqT.rearrange("(a p) t -> p a t", p=P)).then_inc(in_qkv, 16)
                sp.dma_start(gg[:, :, :], pn[:, KW + VW:KW + 2 * VW].rearrange("(i p) n -> p i n", p=P))\
                  .then_inc(in_g, 16)
                sp.dma_start(grow[:, :], rows(g_out)).then_inc(in_g, 16)
                if ahead:
                    ahead.early(sp, "load", 2)
                for i in range(NT):
                    sp.wait_ge(o_done, 4 * (i + 1))
                    sp.dma_start(mix[i * P:(i + 1) * P, :], o[i % 2][:, :]).then_inc(stored[i % 2], 16)
                for s in range(2):
                    sp.wait_ge(stored[s], 16 * NT // 2)

            @block.gpsimd
            def _(pool):
                pool.memset(fT[:, :], 1.0).then_inc(made, 1)
                pool.memset(wfg[:, :], 0.0).then_inc(made, 1)
                pool.memset(eps[:, :], EPS).then_inc(made, 1)
                pool.memset(later[:, :], 1.0).then_inc(made, 1)
                pool.memset(inchunk[:, :], 0.0).then_inc(made, 1)
                pool.wait_ge(made, 5)
                for j in range(2):
                    pool.memset(inchunk[j * CHUNK:(j + 1) * CHUNK, j:j + 1], 1.0).then_inc(made, 1)
                    pool.wait_ge(made, 6 + j)
                pool.affine_select(out=later[:, :], in_=later[:, :], compare_op=ALU.is_gt, fill=0.0, base=0,
                                   pattern=[[-1, P]], channel_multiplier=1).then_inc(made, 1)
                pool.wait_ge(made, 8)
                pool.memset(later[CHUNK:P, 0:CHUNK], 0.0).then_inc(made, 1)
                pool.wait_ge(made, 9)
                for i in range(NT):
                    pool.wait_ge(in_g, 32)
                    pool.wait_ge(silued, i + 1)
                    pool.tensor_tensor(gg[:, i, :], gg[:, i, :], grow[:, :], ALU.mult).then_inc(gated, 1)

            @block.tensor
            def _(pe):
                pe.wait_ge(in_f, 16)
                for i in range(NT):
                    reached(pe, f_copied, i)
                    pe.transpose(TURN[0:RANK, 0:P], f[:, i, :], k.ident[:, :]).then_inc(f_turned, 1)
                pe.wait_ge(in_w, 32)
                pe.wait_ge(made, 9)
                for i in range(NT):
                    pe.wait_ge(f_copied, i + 1)
                    reached(pe, la_done, i)
                    pe.matmul(PRE[:, 0:KW], fT[:, i * P:(i + 1) * P], wfg[:, :], start=True, stop=True)\
                      .then_inc(pre, 1)
                    pe.wait_ge(la_done, i + 1)
                    reached(pe, dec_done, i)
                    pe.matmul(SUF[:, 0:KW], later[:, :], la[i % 2][:, :], start=True, stop=True)\
                      .then_inc(suffix, 1)
                    for pair in range(2):
                        mm = pe.matmul(TOT[:, 16 * pair + 2 * i:16 * pair + 2 * i + 2],
                                       la[i % 2][:, pair * P:(pair + 1) * P], inchunk[:, :], start=True, stop=True)
                    mm.then_inc(total, 1)
                for n in range(2 * NC):
                    ch, pair = n // 2, n % 2
                    i, r0 = ch // 2, (ch % 2) * CHUNK
                    pe.wait_ge(kd_done, i + 1)
                    reached(pe, stated, 2 * (n - 3))
                    pe.matmul(k.bank[4 + n % 4][:, 0:2 * DV], kd[r0:r0 + CHUNK, i, pair * P:(pair + 1) * P],
                              v[r0:r0 + CHUNK, i, pair * 2 * DV:(pair + 1) * 2 * DV],
                              start=True, stop=True).then_inc(kv, 1)
                for i in range(NT):
                    pe.wait_ge(stated, 4 * 2 * (i + 1))
                    reached(pe, o_done, 4 * (i - 1))
                    for h in range(GLA_HEADS):
                        pair, r0 = h // 2, (h % 2) * DK
                        for j in range(2):
                            mm = pe.matmul(head_out(i, h)[j * CHUNK:(j + 1) * CHUNK, :],
                                           qT[r0:r0 + DK, pair, i * P + j * CHUNK:i * P + (j + 1) * CHUNK],
                                           state[r0:r0 + DK, pair, 2 * i + j, :], start=True, stop=True)
                    mm.then_inc(outp, 1)

            @block.scalar
            def _(act):
                act.preload_act_table_set("natural_log_exp_and_others")
                for i in range(NT):
                    s = i % 2
                    act.wait_ge(pre, i + 1)
                    reached(act, la_done, i - 1)
                    act.activation(ex[s][:, :], PRE[:, 0:KW], ACT.Abs).then_inc(abs_done, 1)
                    act.wait_ge(abs_done, i + 1)
                    act.activation(ex[s][:, :], ex[s][:, :], ACT.Exp, scale=-1.0).then_inc(exp_done, 1)
                    act.wait_ge(exp_done, i + 1)
                    act.activation(ex[s][:, :], ex[s][:, :], ACT.Ln, bias=1.0).then_inc(ln_done, 1)
                    act.wait_ge(suffix, i + 1)
                    reached(act, kd_done, i - 1)
                    act.activation(dec[s][:, :], SUF[:, 0:KW], ACT.Exp, scale=1.0 / GATE_TAU).then_inc(dec_done, 1)
                act.wait_ge(total, NT)
                act.activation(decay[:, :, :], TOT[:, 0:2 * NC].rearrange("p (a b) -> p a b", a=2), ACT.Exp,
                               scale=1.0 / GATE_TAU).then_inc(decay_done, 1)
                act.wait_ge(in_g, 32)
                for i in range(NT):
                    act.activation(gg[:, i, :], gg[:, i, :], ACT.Silu).then_inc(silued, 1)
                for i in range(NT):
                    act.wait_ge(outp, i + 1)
                    for h in range(GLA_HEADS):
                        n = i * GLA_HEADS + h
                        reached(act, sq, n)
                        act.activation(junk[:, :], head_out(i, h), ACT.Square,
                                       scale=DK ** -0.5, accum_out=ss[:, n:n + 1]).then_inc(sq, 1)
                    act.wait_ge(sq, 4 * i + 4)
                    act.activation(rs[:, 4 * i:4 * i + 4], ss[:, 4 * i:4 * i + 4], ACT.Sqrt, bias=eps[:, 0:1],
                                   scale=1.0 / DV).then_inc(std, 1)

            @block.vector
            def _(dve):
                dve.wait_ge(made, 9)
                for i in range(NT):
                    dve.wait_ge(f_turned, i + 1)
                    dve.tensor_copy(fT[0:RANK, i * P:(i + 1) * P], TURN[0:RANK, 0:P]).then_inc(f_copied, 1)
                dve.wait_ge(in_qkv, 48)
                for i in range(NT):
                    s = i % 2
                    dve.wait_ge(ln_done, i + 1)
                    reached(dve, total, i - 1)
                    dve.scalar_tensor_tensor(out=la[s][:, :], in0=PRE[:, 0:KW], scalar=0.0, in1=ex[s][:, :],
                                             op0=ALU.min, op1=ALU.subtract).then_inc(la_done, 1)
                    dve.wait_ge(dec_done, i + 1)
                    dve.tensor_tensor(kd[:, i, :], kd[:, i, :], dec[s][:, :], ALU.mult).then_inc(kd_done, 1)
                dve.wait_ge(decay_done, 1)
                for n in range(2 * NC):
                    ch, pair = n // 2, n % 2
                    dve.wait_ge(kv, n + 1)
                    reached(dve, stated, 2 * (n - 1))
                    for r in range(2):
                        rows_ = slice(r * DK, (r + 1) * DK)
                        new = k.bank[4 + n % 4][rows_, r * DV:(r + 1) * DV]
                        if ch == 0:
                            dve.tensor_copy(state[rows_, pair, 0, :], new).then_inc(stated, 1)
                        else:
                            dve.scalar_tensor_tensor(out=state[rows_, pair, ch, :],
                                                     in0=state[rows_, pair, ch - 1, :],
                                                     scalar=decay[rows_, pair, ch:ch + 1], in1=new,
                                                     op0=ALU.mult, op1=ALU.add).then_inc(stated, 1)
                for i in range(NT):
                    r4 = rs[:, 4 * i:4 * i + 4]
                    dve.wait_ge(std, i + 1)
                    dve.reciprocal(r4, r4).then_inc(rstd, 1)
                    dve.wait_ge(rstd, i + 1)
                    dve.tensor_scalar(r4, r4, DK ** -0.5, None, ALU.mult).then_inc(scaled, 1)
                    dve.wait_ge(scaled, i + 1)
                    dve.wait_ge(gated, i + 1)
                    reached(dve, stored[i % 2], 16 * (i // 2))
                    for h in range(GLA_HEADS):
                        cols = slice(h * DV, (h + 1) * DV)
                        dve.scalar_tensor_tensor(out=o[i % 2][:, cols], in0=head_out(i, h),
                                                 scalar=rs[:, 4 * i + h:4 * i + h + 1], in1=gg[:, i, cols],
                                                 op0=ALU.mult, op1=ALU.mult).then_inc(o_done, 1)



def distance_buckets(window):
    exact = BUCKETS // 2
    hot = np.zeros((BUCKETS + 1, BAND), np.float32)
    for y in range(BAND):
        dist = 2 * P - 1 - y
        if dist < 0 or (window is not None and dist >= window):
            b = BUCKETS
        elif dist < exact:
            b = dist
        else:
            b = min(BUCKETS - 1, exact + int(np.log(dist / exact) / np.log(MAX_DIST / exact) * (BUCKETS - exact)))
        hot[b, y] = 1.0
    return hot


def band_of(scratch, g):
    flat = scratch[g, :, :].rearrange("p y -> (p y)")
    return flat[P - 1:P - 1 + P * (BAND - 1)].rearrange("(p y) -> p y", y=BAND - 1)[:, 0:2 * P]


def window_attention(k, qT, kT, va, bands, sinks, mix):
    nc = k.nc
    with ExitStack() as c:
        sem = lambda n: k.sem("swa_" + n)
        q = [k.sb(c, f"swa_q{s}", [HD, S]) for s in range(2)]
        kk = [k.sb(c, f"swa_k{s}", [HD, S]) for s in range(2)]
        vv = k.sb(c, "swa_v", [P, NT, 2 * HD])
        band = [k.sb(c, f"swa_band{s}", [P, 2 * P]) for s in range(2)]
        sink = k.sb(c, "swa_sink", [P, SWA_HEADS])
        p = [k.sb(c, f"swa_p{s}", [P, 2 * P]) for s in range(2)]
        pT_ = [k.sb(c, f"swa_pT{s}", [P, 2, P]) for s in range(2)]
        st = {n: k.sb(c, "swa_" + n, [P, 2 * NT]) for n in ("max", "shift", "sinkd", "esink", "den", "rden")}
        o = [k.sb(c, f"swa_o{s}", [P, NT, HD]) for s in range(2)]
        const_in = sem("const_in")
        loaded = [sem(f"loaded{s}") for s in range(2)]
        stored = [sem(f"stored{s}") for s in range(2)]
        z_done, logit, maxed, shifted, p_done, e_done, added, rden, turned, pT_done, pv, out = (
            sem(n) for n in ("z", "logit", "max", "shift", "p", "esink", "added", "rden", "turned", "pT", "pv", "out"))
        bodies, per = SWA_GROUP, 2 * NT
        col = lambda name, pos: st[name][:, pos:pos + 1]
        keys = lambda i: ((i - 1) * P if i else 0, (i + 1) * P)
        with nc.Block() as block:
            @block.sync
            def _(sp):
                for s in range(2):
                    sp.dma_start(kk[s][:, :], kT[s * HD:(s + 1) * HD, :])\
                      .then_inc(const_in, 16)
                sp.dma_start(vv[:, :, :], va.rearrange("(i p) n -> p i n", p=P)).then_inc(const_in, 16)
                sp.dma_start(sink[:, :], rows(sinks)).then_inc(const_in, 16)

                def load(j, s):
                    reached(sp, out, NT * (2 * j + s - 1))
                    h = j + SWA_GROUP * s
                    sp.dma_start(q[s][:, :], qT[ds(h * HD, HD), :]).then_inc(loaded[s], 16)
                    sp.dma_start(band[s][:, :], bands(h)).then_inc(loaded[s], 16)

                def store(j, s):
                    sp.wait_ge(out, NT * (2 * j + s + 1))
                    sp.dma_start(mix[:, ds((j + SWA_GROUP * s) * HD, HD)].rearrange("(i p) d -> p i d", p=P),
                                 o[s][:, :, :]).then_inc(stored[s], 16)
                load(0, 0)
                load(0, 1)

                def body(j):
                    for s in range(2):
                        load(j + 1, s)
                        store(j, s)
                looped(sp, bodies - 1, body)
                for s in range(2):
                    store(bodies - 1, s)
                for s in range(2):
                    sp.wait_ge(stored[s], 16 * bodies)

            @block.tensor
            def _(pe):
                pe.wait_ge(const_in, 64)

                def scores(n, pos, j):
                    s, i = pos // NT, pos % NT
                    a, b = keys(i)
                    if i == 0:
                        pe.wait_ge(loaded[s], 32 * (j + 1))
                    reached(pe, logit, n - 1)
                    pe.matmul(k.bank[pos % 2][:, 0:b - a], q[s][:, i * P:(i + 1) * P], kk[s][:, a:b],
                              start=True, stop=True).then_inc(z_done, 1)

                def turn_p(n, pos, j):
                    i = pos % NT
                    pe.wait_ge(p_done, n + 1)
                    reached(pe, pT_done, n - 1)
                    for b in range(2 if i else 1):
                        mm = pe.transpose(k.bank[2 + pos % 2][:, b * P:(b + 1) * P],
                                          p[pos % 2][:, b * P:(b + 1) * P], k.ident[:, :])
                    mm.then_inc(turned, 1)

                def values(n, pos, j):
                    s, i = pos // NT, pos % NT
                    pe.wait_ge(pT_done, n + 1)
                    reached(pe, out, n - 1)
                    nb = 2 if i else 1
                    for b in range(nb):
                        mm = pe.matmul(k.bank[4 + pos % 2][:, 0:HD], pT_[pos % 2][:, b, :],
                                       vv[:, max(i - 1, 0) + b, s * HD:(s + 1) * HD], start=b == 0, stop=b == nb - 1)
                    mm.then_inc(pv, 1)
                pipelined(pe, bodies, per, [(0, scores), (2, turn_p), (3, values)])

            @block.scalar
            def _(act):
                def weights(n, pos, j):
                    i = pos % NT
                    L = 2 * P if i else P
                    act.wait_ge(shifted, 2 * n + 2)
                    act.activation(p[pos % 2][:, 0:L], p[pos % 2][:, 0:L], ACT.Exp, bias=col("shift", pos),
                                   accum_out=col("den", pos)).then_inc(p_done, 1)
                    act.activation(col("esink", pos), col("sinkd", pos), ACT.Exp).then_inc(e_done, 1)

                def copy_turned(n, pos, j):
                    L = 2 * P if pos % NT else P
                    act.wait_ge(turned, n + 1)
                    reached(act, pv, n - 1)
                    act.activation(pT_[pos % 2][:, 0:L // P, :],
                                   k.bank[2 + pos % 2][:, 0:L].rearrange("p (a b) -> p a b", b=P), ACT.Copy)\
                       .then_inc(pT_done, 1)
                pipelined(act, bodies, per, [(0, weights), (1, copy_turned)])

            @block.vector
            def _(dve):
                dve.wait_ge(const_in, 64)

                def logits(n, pos, j):
                    s, i = pos // NT, pos % NT
                    L = 2 * P if i else P
                    w = p[pos % 2][:, 0:L]
                    dve.wait_ge(z_done, n + 1)
                    if i == 0:
                        dve.wait_ge(loaded[s], 32 * (j + 1))
                    reached(dve, turned, n - 1)
                    dve.scalar_tensor_tensor(out=w, in0=k.bank[pos % 2][:, 0:L], scalar=HD ** -0.5,
                                             in1=band[s][:, 2 * P - L:2 * P], op0=ALU.mult, op1=ALU.add)\
                       .then_inc(logit, 1)
                    dve.wait_ge(logit, n + 1)
                    dve.tensor_reduce(col("max", pos), w, AX, ALU.max).then_inc(maxed, 1)
                    dve.wait_ge(maxed, n + 1)
                    snk = sink[:, ds(j + SWA_GROUP * s, 1)]
                    dve.tensor_scalar(col("shift", pos), snk, col("max", pos), -1.0, ALU.max, ALU.mult)\
                       .then_inc(shifted, 1)
                    dve.wait_ge(shifted, 2 * n + 1)
                    dve.tensor_tensor(col("sinkd", pos), snk, col("shift", pos), ALU.add).then_inc(shifted, 1)

                def output(n, pos, j):
                    s, i = pos // NT, pos % NT
                    dve.wait_ge(e_done, n + 1)
                    dve.tensor_tensor(col("den", pos), col("den", pos), col("esink", pos), ALU.add)\
                       .then_inc(added, 1)
                    dve.wait_ge(added, n + 1)
                    dve.reciprocal(col("rden", pos), col("den", pos)).then_inc(rden, 1)
                    dve.wait_ge(rden, n + 1)
                    dve.wait_ge(pv, n + 1)
                    if i == 0:
                        dve.wait_ge(stored[s], 16 * j)
                    dve.tensor_scalar(o[s][:, i, :], k.bank[4 + pos % 2][:, 0:HD], col("rden", pos), None,
                                      ALU.mult).then_inc(out, 1)
                pipelined(dve, bodies, per, [(0, logits), (3, output)])



def sparse_prepare(k, cbT, ik_dram, iw_dram, cn, cT, ikT, iw):
    nc, d = k.nc, k.dram
    HI = DSA_HEADS
    with ExitStack() as c:
        sem = lambda n: k.sem("prep_" + n)
        raw = k.sb(c, "prep_cbT", [P, S])
        ik = k.sb(c, "prep_ik", [P, NT, HD])
        gc = k.sb(c, "prep_gc", [P, DC])
        gi = k.sb(c, "prep_gi", [P, HD])
        bi = k.sb(c, "prep_bi", [P, HD])
        junk = k.sb(c, "prep_junk", [P, DC])
        eps = k.sb(c, "prep_eps", [P, 1])
        ms = k.sb(c, "prep_ms", [P, 2 * NT])
        rs = k.sb(c, "prep_rs", [P, 2 * NT])
        st = k.sb(c, "prep_st", [P, NT, 6])
        mv = k.sb(c, "prep_mv", [P, NT, 2])
        loaded, made, turned, sq, stats, aggr, std, rstd, scaled, cn_done, ik_steps, cT_mm, ikT_mm, copied = (
            sem(n) for n in ("loaded", "eps_made", "turned", "sq", "stats", "aggr", "std", "rstd", "scaled",
                             "cn", "ik_steps", "cT_mm", "ikT_mm", "copied"))
        with nc.Block() as block:
            @block.sync
            def _(sp):
                sp.dma_start(raw[:, :], cbT).then_inc(loaded, 16)
                sp.dma_start(ik[:, :, :], ik_dram.rearrange("(i p) n -> p i n", p=P)).then_inc(loaded, 16)
                sp.dma_start(iw[:, :, :], iw_dram.rearrange("(i p) n -> p i n", p=P)).then_inc(loaded, 16)
                sp.dma_start(gc[:, :], rows(d["kv_g"])).then_inc(loaded, 16)
                sp.dma_start(gi[:, :], rows(d["ik_g"])).then_inc(loaded, 16)
                sp.dma_start(bi[:, :], rows(d["ik_b"])).then_inc(loaded, 16)

            @block.gpsimd
            def _(pool):
                pool.memset(eps[:, :], LN_EPS).then_inc(made, 1)

            @block.tensor
            def _(pe):
                pe.wait_ge(loaded, 96)
                for i in range(NT):
                    mm = pe.transpose(k.bank[i // 4][:, (i % 4) * P:(i % 4 + 1) * P], raw[:, i * P:(i + 1) * P],
                                      k.ident[:, :])
                mm.then_inc(turned, 1)
                pe.wait_ge(cn_done, NT)
                for i in range(NT):
                    mm = pe.transpose(k.bank[2 + i // 4][:, (i % 4) * P:(i % 4 + 1) * P], cn[:, i, :], k.ident[:, :])
                mm.then_inc(cT_mm, 1)
                pe.wait_ge(ik_steps, 3 * NT)
                for i in range(NT):
                    mm = pe.transpose(k.bank[4 + i // 4][0:HD, (i % 4) * P:(i % 4 + 1) * P], ik[:, i, :],
                                      k.ident[:, :])
                mm.then_inc(ikT_mm, 1)

            @block.scalar
            def _(act):
                act.wait_ge(turned, 1)
                for i in range(NT):
                    reached(act, sq, i)
                    act.activation(junk[:, :], k.bank[i // 4][:, (i % 4) * P:(i % 4 + 1) * P], ACT.Square,
                                   scale=DC ** -0.5, accum_out=ms[:, i:i + 1]).then_inc(sq, 1)
                act.wait_ge(made, 1)
                act.wait_ge(sq, NT)
                act.wait_ge(aggr, 2)
                act.activation(rs[:, :], ms[:, :], ACT.Sqrt, bias=eps[:, 0:1]).then_inc(std, 1)
                act.wait_ge(cT_mm, 1)
                act.activation(cT[:, :], k.psum[:, 1024:2048], ACT.Copy).then_inc(copied, 1)
                act.wait_ge(ikT_mm, 1)
                act.activation(ikT[:, :], k.psum[0:HD, 2048:3072], ACT.Copy).then_inc(copied, 1)
                act.wait_ge(copied, 2)

            @block.vector
            def _(dve):
                dve.wait_ge(loaded, 96)
                dve.tensor_scalar(iw[:, :, :], iw[:, :, :], HI ** -0.5, None, ALU.mult).then_inc(stats, 1)
                for i in range(NT):
                    dve.bn_stats(st[:, i, :], ik[:, i, :]).then_inc(stats, 1)
                dve.wait_ge(stats, NT + 1)
                for i in range(NT):
                    a = dve.bn_aggr(mv[:, i, :], st[:, i, :])
                a.then_inc(aggr, 1)
                dve.wait_ge(aggr, 1)
                dve.tensor_copy(ms[:, NT:2 * NT], mv[:, :, 1]).then_inc(aggr, 1)
                dve.wait_ge(std, 1)
                dve.reciprocal(rs[:, :], rs[:, :]).then_inc(rstd, 1)
                dve.wait_ge(rstd, 1)
                for i in range(NT):
                    dve.scalar_tensor_tensor(out=cn[:, i, :], in0=k.bank[i // 4][:, (i % 4) * P:(i % 4 + 1) * P],
                                             scalar=rs[:, i:i + 1], in1=gc[:, :], op0=ALU.mult, op1=ALU.mult)\
                       .then_inc(cn_done, 1)
                for i in range(NT):
                    dve.tensor_scalar(ik[:, i, :], ik[:, i, :], mv[:, i, 0:1], rs[:, NT + i:NT + i + 1],
                                      ALU.subtract, ALU.mult).then_inc(ik_steps, 1)
                dve.wait_ge(ik_steps, NT)
                for i in range(NT):
                    dve.tensor_tensor(ik[:, i, :], ik[:, i, :], gi[:, :], ALU.mult).then_inc(ik_steps, 1)
                dve.wait_ge(ik_steps, 2 * NT)
                for i in range(NT):
                    dve.tensor_tensor(ik[:, i, :], ik[:, i, :], bi[:, :], ALU.add).then_inc(ik_steps, 1)


def index_scores(k, iqT, ikT, iw, score, ahead=None):
    nc = k.nc
    with ExitStack() as c:
        sem = lambda n: k.sem("idx_" + n)
        q = [k.sb(c, f"idx_q{s}", [HD, S]) for s in range(2)]
        r = [k.sb(c, f"idx_r{s}", [P, S]) for s in range(2)]
        loaded = [sem(f"loaded{s}") for s in range(2)]
        zeroed, z_done, r_done, added, masked = (sem(n) for n in ("zeroed", "z", "relu", "added", "masked"))
        bodies, per = DSA_HEADS // 2, 2 * NT
        zs = lambda pos, lo, hi: k.psum[:, 1024 * (pos % 2) + lo:1024 * (pos % 2) + hi]
        with nc.Block() as block:
            @block.sync
            def _(sp):
                def load(j, s):
                    reached(sp, r_done, NT * (2 * j + s - 1))
                    sp.dma_start(q[s][:, :], iqT[ds((2 * j + s) * HD, HD), :]).then_inc(loaded[s], 16)
                load(0, 0)
                load(0, 1)
                looped(sp, bodies - 1, lambda j: [load(j + 1, s) for s in range(2)])
                if ahead:
                    ahead.early(sp, "load", 2)

            @block.tensor
            def _(pe):
                def scores(n, pos, j):
                    s, i = pos // NT, pos % NT
                    L = (i + 1) * P
                    if i == 0:
                        pe.wait_ge(loaded[s], 16 * (j + 1))
                    reached(pe, r_done, n - 1)
                    for a in range(0, L, 512):
                        b = min(L, a + 512)
                        mm = pe.matmul(zs(pos, a, b), q[s][:, i * P:(i + 1) * P], ikT[:, a:b],
                                       start=True, stop=True)
                    mm.then_inc(z_done, 1)
                pipelined(pe, bodies, per, [(0, scores)])

            @block.scalar
            def _(act):
                def relu(n, pos, j):
                    L = (pos % NT + 1) * P
                    act.wait_ge(z_done, n + 1)
                    reached(act, added, n - 1)
                    act.activation(r[pos % 2][:, 0:L], zs(pos, 0, L), ACT.Relu, scale=HD ** -0.5)\
                       .then_inc(r_done, 1)
                pipelined(act, bodies, per, [(0, relu)])

            @block.gpsimd
            def _(pool):
                pool.memset(score[:, :, :], 0.0).then_inc(zeroed, 1)
                pool.wait_ge(added, bodies * per)
                for i in range(NT):
                    blk = score[:, i, i * P:(i + 1) * P]
                    pool.affine_select(out=blk, in_=blk, compare_op=ALU.is_ge, fill=NEG, base=0,
                                       pattern=[[-1, P]], channel_multiplier=1).then_inc(masked, 1)
                pool.wait_ge(masked, NT)

            @block.vector
            def _(dve):
                dve.wait_ge(zeroed, 1)

                def add(n, pos, j):
                    s, i = pos // NT, pos % NT
                    L = (i + 1) * P
                    dve.wait_ge(r_done, n + 1)
                    if isinstance(n, int) and n < NT:
                        pass
                    else:
                        dve.wait_ge(added, n - NT + 1)
                    dve.scalar_tensor_tensor(out=score[:, i, 0:L], in0=r[pos % 2][:, 0:L],
                                             scalar=iw[:, i, ds(2 * j + s, 1)], in1=score[:, i, 0:L],
                                             op0=ALU.mult, op1=ALU.add).then_inc(added, 1)
                pipelined(dve, bodies, per, [(0, add)])


def select_top(k, score, jobs, mem, b_v, hh, hl, bands):
    nc = k.nc
    T0 = TOPK // P
    tiles = range(T0, NT)
    n = len(tiles)
    lin_q, lin_k, lin_v = (job[0] for job in jobs)
    flat = lambda h: h[:, :, :].rearrange("p a t -> p (a t)")
    with ExitStack() as c:
        sem = lambda x: k.sem("top_" + x)
        u = k.sb(c, "top_u", [P, n], U32)
        cand = k.sb(c, "top_cand", [P, n], U32)
        flip = k.sb(c, "top_flip", [P, n], U32)
        thr = k.sb(c, "top_thr", [P, n], U32)
        bit = k.sb(c, "top_bit", [P, n], U32)
        cnt = k.sb(c, "top_cnt", [P, n])
        enough = k.sb(c, "top_enough", [P, n], U32)
        need = k.sb(c, "top_need", [P, n])
        hit = [k.sb(c, f"top_hit{j}", [P, S], BF) for j in range(2)]
        gt, eq = hit
        rank = k.sb(c, "top_rank", [P, S])
        stage = [k.sb(c, f"top_stage{j}", [P, S]) for j in range(2)]
        bq = k.sb(c, "top_bias_q", [P, 2 * lin_q.n])
        bk = k.sb(c, "top_bias_k", [P, 2 * lin_k.n])
        rel_made, rel_in, rel_mm, rel_out, rel_stored = (
            sem(x) for x in ("rel_made", "rel_in", "rel_mm", "rel_out", "rel_stored"))
        step, counted = sem("step"), sem("counted")
        bias_in, mem_in, mem_hi, mem_lo, staged = (
            sem(x) for x in ("bias_in", "mem_in", "mem_hi", "mem_lo", "staged"))
        stored = [sem(f"stored{j}") for j in range(2)]
        thr_f = lambda: thr[:, :].bitcast(F)

        M = KT * MEM
        mh, ml = (flat(h)[:, 0:M].rearrange("p (a m) -> p a m", a=KT) for h in (hh, hl))
        v_row = k.sb(c, "top_v_row", [P, D])
        raw_half = lambda j: stage[j][:, :].rearrange("p (a m) -> p a m", a=KT // 2)
        rel = k.sb(c, "top_rel", [BUCKETS + 1, SWA_HEADS + DSA_HEADS])
        hot = v_row[0:BUCKETS + 1, 0:2 * BAND].rearrange("b (a y) -> b a y", a=2)
        band_row = stage[0][0:SWA_HEADS, 0:2 * BAND].rearrange("h (a y) -> h a y", a=2)
        for lin in (lin_k, lin_v):
            lin.hh, lin.hl = mh, ml

        steps = [(lin, ch, ch // 2, (ch % 2) ^ lin.s0) for lin in (lin_q, lin_k, lin_v) for ch in range(lin.n)]
        pieces = [st + (f,) for st in steps for f in range(2 if st[0] is lin_q else 1)]
        first_v = 2 * lin_q.n + lin_k.n

        with nc.Block() as block:
            @block.sync
            def _(sp):
                sp.dma_start(bq[:, :], jobs[0][2]).then_inc(bias_in, 16)
                sp.dma_start(bk[:, :], jobs[1][2]).then_inc(bias_in, 16)
                sp.dma_start(v_row[:, :], rows(b_v)).then_inc(bias_in, 16)

                def load(m):
                    if m < len(steps):
                        lin, ch, i, sl = steps[m]
                        lin.load(sp, ch, i, sl)
                load(0)
                load(1)
                for m, piece in enumerate(pieces):
                    lin, ch, i, sl, f = piece
                    if f == 0:
                        load(steps.index(piece[:4]) + 2)
                    if piece[:4] == steps[lin_q.n] and f == 0:
                        for j in range(2):
                            sp.wait_ge(stored[j], 16 * lin_q.n)
                            sp.dma_start(stage[j][:, :], mem[:, j * S:(j + 1) * S]).then_inc(mem_in, 16)
                    if lin is lin_v:
                        sp.wait_ge(staged, ch + 1)
                    else:
                        sp.wait_ge(*lin.at("lin_evac", sl, 4 * i + 2 * f + 2 if lin is lin_q else i + 1))
                    dst, src = jobs[(lin_q, lin_k, lin_v).index(lin)][1], stage[m % 2]
                    if lin is lin_q:
                        r0 = ch * CW + f * P
                        sp.dma_start(dst[r0:r0 + P, :], src[:, :]).then_inc(stored[m % 2], 16)
                    elif lin is lin_k:
                        sp.dma_start(dst[ch * CW:(ch + 1) * CW, :].rearrange("(f p) m -> p f m", p=P),
                                     src[:, 0:2 * MEM].rearrange("p (f m) -> p f m", f=2)).then_inc(stored[m % 2], 16)
                    else:
                        sp.dma_start(dst[:, ch * CW:(ch + 1) * CW].rearrange("(i p) n -> p i n", p=P),
                                     src[:, 0:2 * CW].rearrange("p (i n) -> p i n", i=2)).then_inc(stored[m % 2], 16)
                for j in range(2):
                    sp.wait_ge(stored[j], 16 * ((len(pieces) + 1 - j) // 2))
                sp.wait_ge(rel_made, 1)
                sp.dma_start(hot, k.dram["buckets"].rearrange("a b y -> b a y")).then_inc(rel_in, 16)
                sp.dma_start(rel[0:BUCKETS, :], k.dram["rel_bias"]).then_inc(rel_in, 16)
                for a in range(2):
                    sp.wait_ge(rel_out, a + 1)
                    sp.dma_start(bands[a * SWA_HEADS:(a + 1) * SWA_HEADS, :, :],
                                 band_row[:, a:a + 1, :].broadcast_to([SWA_HEADS, P, BAND])).then_inc(rel_stored, 16)
                sp.wait_ge(rel_stored, 32)

            @block.tensor
            def _(pe):
                lin_q.products(pe)
                pe.wait_ge(mem_lo, 2)
                for j in range(2):
                    pe.wait_ge(*lin_q.at("lin_evac", j, lin_q.banks * lin_q.uses[j]))
                lin_k.products(pe)
                lin_v.products(pe)
                pe.wait_ge(rel_in, 32)
                for a in range(2):
                    pe.matmul(k.bank[1 + a][0:SWA_HEADS, 0:BAND], rel[:, a * SWA_HEADS:(a + 1) * SWA_HEADS],
                              hot[:, a, :], start=True, stop=True).then_inc(rel_mm, 1)

            @block.scalar
            def _(act):
                act.wait_ge(bias_in, 48)

                def hi(m):
                    if m < len(steps):
                        steps[m][0].hi(act, *steps[m][1:])
                hi(0)
                hi(1)
                for m, piece in enumerate(pieces):
                    lin, ch, i, sl, f = piece
                    reached(act, stored[m % 2], 16 * (m // 2))
                    if lin is lin_q:
                        for b in (2 * f, 2 * f + 1):
                            act.wait_ge(*lin.at("lin_mm", sl, 4 * i + b + 1))
                            act.activation(stage[m % 2][:, (b % 2) * 512:(b % 2) * 512 + 512], lin.out(sl, b)[:, :],
                                           ACT.Identity, bias=bq[:, 2 * ch + f:2 * ch + f + 1])\
                               .then_inc(k.wsem["lin_evac"][sl], 1)
                    else:
                        act.wait_ge(*lin.at("lin_mm", sl, i + 1))
                        for g in range(2):
                            cols = slice(g * CW, (g + 1) * CW)
                            a = act.activation(stage[m % 2][:, cols], lin.out(sl, 0)[:, cols], ACT.Identity,
                                               bias=bk[:, 2 * ch + g:2 * ch + g + 1] if lin is lin_k else 0.0)
                        a.then_inc(k.wsem["lin_evac"][sl], 1)
                    if lin is not lin_q or f == 1:
                        hi(steps.index(piece[:4]) + 2)
                    if piece[:4] == steps[lin_q.n - 1] and f == 1:
                        for j in range(2):
                            act.wait_ge(*lin_q.at("lin_mm", j, lin_q.banks * lin_q.uses[j]))
                        for j in range(2):
                            act.wait_ge(mem_in, 32)
                            act.activation(mh[:, j * KT // 2:(j + 1) * KT // 2, :], raw_half(j), ACT.Copy)\
                               .then_inc(mem_hi, 1)
                for a in range(2):
                    act.wait_ge(rel_mm, a + 1)
                    act.activation(band_row[:, a, :], k.bank[1 + a][0:SWA_HEADS, 0:BAND], ACT.Copy)\
                       .then_inc(rel_out, 1)

            @block.gpsimd
            def _(pool):
                pool.memset(rel[:, :], NEG).then_inc(rel_made, 1)

                def add_bias(v):
                    m = first_v + v
                    pool.wait_ge(bias_in, 48)
                    lin, ch, i, sl, f = pieces[m]
                    pool.wait_ge(*lin.at("lin_evac", sl, i + 1))
                    for g in range(2):
                        cols = slice(g * CW, (g + 1) * CW)
                        a = pool.tensor_tensor(stage[m % 2][:, cols], stage[m % 2][:, cols],
                                               v_row[:, v * CW:(v + 1) * CW], ALU.add)
                    a.then_inc(staged, 1)

                def lo(m):
                    if m < len(steps):
                        steps[m][0].lo(pool, *steps[m][1:])
                for m in range(lin_q.n + 1):
                    lo(m)
                for j in range(2):
                    half = slice(j * KT // 2, (j + 1) * KT // 2)
                    pool.wait_ge(mem_hi, j + 1)
                    pool.tensor_tensor(ml[:, half, :], raw_half(j), mh[:, half, :].bitcast(F),
                                       ALU.subtract).then_inc(mem_lo, 1)
                for m in range(lin_q.n + 1, len(steps)):
                    lo(m)
                    v = m - 2 - lin_q.n - lin_k.n
                    if v >= 0:
                        add_bias(v)
                for v in range(max(0, lin_v.n - 2), lin_v.n):
                    add_bias(v)
                pool.wait_ge(staged, lin_v.n)

            @block.vector
            def _(dve):
                dve.memset(u[:, :], 0).then_inc(step, 1)
                dve.memset(bit[:, :], 1 << 31).then_inc(step, 1)
                dve.wait_ge(step, 2)
                SMALL = 7

                def one_bit(b):
                    def chained(m):
                        dve.wait_ge(step, b * SMALL + 2 + m)
                    dve.tensor_tensor(cand[:, :], u[:, :], bit[:, :], ALU.bitwise_or).then_inc(step, 1)
                    chained(1)
                    dve.tensor_scalar(flip[:, :].bitcast(I32), cand[:, :].bitcast(I32), 31, -1,
                                      ALU.arith_shift_right, ALU.bitwise_xor).then_inc(step, 1)
                    chained(2)
                    dve.tensor_scalar(flip[:, :].bitcast(I32), flip[:, :].bitcast(I32), -(1 << 31), None,
                                      ALU.bitwise_or).then_inc(step, 1)
                    chained(3)
                    dve.tensor_tensor(thr[:, :], cand[:, :], flip[:, :], ALU.bitwise_xor).then_inc(step, 1)
                    chained(4)
                    for t, i in enumerate(tiles):
                        L = (i + 1) * P
                        if t >= 2:
                            dve.wait_ge(counted, b * n + t - 1)
                        dve.tensor_scalar(hit[t % 2][:, 0:L], score[:, i, 0:L], thr_f()[:, t:t + 1], None, ALU.is_ge,
                                          ALU.add, accum_out=cnt[:, t:t + 1]).then_inc(counted, 1)
                    dve.wait_ge(counted, b * n + n)
                    dve.tensor_scalar(enough[:, :], cnt[:, :], float(TOPK), None, ALU.is_ge).then_inc(step, 1)
                    chained(5)
                    dve.tensor_scalar(bit[:, :], bit[:, :], 1, None, ALU.logical_shift_right).then_inc(step, 1)
                    dve.copy_predicated(u[:, :], enough[:, :], cand[:, :]).then_inc(step, 1)
                    chained(7)
                looped(dve, 32, one_bit, peel=0)
                v = 32 * SMALL + 2

                for m, op in enumerate((
                        lambda: dve.tensor_scalar(flip[:, :].bitcast(I32), u[:, :].bitcast(I32), 31, -1,
                                                  ALU.arith_shift_right, ALU.bitwise_xor),
                        lambda: dve.tensor_scalar(flip[:, :].bitcast(I32), flip[:, :].bitcast(I32), -(1 << 31),
                                                  None, ALU.bitwise_or),
                        lambda: dve.tensor_tensor(thr[:, :], u[:, :], flip[:, :], ALU.bitwise_xor))):
                    op().then_inc(step, 1)
                    dve.wait_ge(step, v + m + 1)
                v += 3
                for t, i in enumerate(tiles):
                    L = (i + 1) * P
                    sc, th = score[:, i, 0:L], thr_f()[:, t:t + 1]
                    dve.tensor_scalar(gt[:, 0:L], sc, th, None, ALU.is_gt, ALU.add,
                                      accum_out=cnt[:, t:t + 1]).then_inc(step, 1)
                    dve.tensor_scalar(eq[:, 0:L], sc, th, None, ALU.is_equal).then_inc(step, 1)
                    dve.wait_ge(step, v + 2)
                    dve.tensor_scalar(need[:, t:t + 1], cnt[:, t:t + 1], -1.0, float(TOPK), ALU.mult, ALU.add)\
                       .then_inc(step, 1)
                    dve.tensor_tensor_scan(rank[:, 0:L], eq[:, 0:L], eq[:, 0:L], 0.0, ALU.add, ALU.max)\
                       .then_inc(step, 1)
                    dve.wait_ge(step, v + 4)
                    dve.scalar_tensor_tensor(out=eq[:, 0:L], in0=rank[:, 0:L], scalar=need[:, t:t + 1],
                                             in1=eq[:, 0:L], op0=ALU.is_le, op1=ALU.mult).then_inc(step, 1)
                    dve.wait_ge(step, v + 5)
                    dve.tensor_tensor(gt[:, 0:L], gt[:, 0:L], eq[:, 0:L], ALU.add).then_inc(step, 1)
                    dve.wait_ge(step, v + 6)
                    dve.tensor_scalar(sc, gt[:, 0:L], -1.0, -NEG, ALU.add, ALU.mult).then_inc(step, 1)
                    dve.wait_ge(step, v + 7)
                    v += 7
                for i in range(T0):
                    L = (i + 1) * P
                    sc = score[:, i, 0:L]
                    dve.tensor_scalar(gt[:, 0:L], sc, NEG, None, ALU.is_gt).then_inc(step, 1)
                    dve.wait_ge(step, v + 1)
                    dve.tensor_scalar(sc, gt[:, 0:L], -1.0, -NEG, ALU.add, ALU.mult).then_inc(step, 1)
                    dve.wait_ge(step, v + 2)
                    v += 2


def sparse_attention(k, qbT, w_uk, w_uv, cn, cT, mask, bands, rel_last, mix, ahead=None):
    nc = k.nc
    with ExitStack() as c:
        sem = lambda n: k.sem("dsa_" + n)
        q = [k.sb(c, f"dsa_q{s}", [HD, S]) for s in range(2)]
        uk = [k.sb(c, f"dsa_uk{s}", [HD, DC]) for s in range(2)]
        uv = [k.sb(c, f"dsa_uv{s}", [DC, HD]) for s in range(2)]
        ql = [k.sb(c, f"dsa_ql{s}", [DC, S]) for s in range(2)]
        band = [k.sb(c, f"dsa_band{s}", [P, 2 * P]) for s in range(2)]
        far = k.sb(c, "dsa_far", [P, DSA_HEADS])
        p = [k.sb(c, f"dsa_p{s}", [P, S]) for s in range(2)]
        pT_ = [k.sb(c, f"dsa_pT{s}", [P, NT, P]) for s in range(2)]
        ol = [k.sb(c, f"dsa_ol{s}", [DC, P]) for s in range(2)]
        st = {n: k.sb(c, "dsa_" + n, [P, 2 * NT]) for n in ("shift", "den", "rden")}
        o = [k.sb(c, f"dsa_o{s}", [P, NT, HD]) for s in range(2)]
        far_in = sem("far_in")
        loaded = [sem(f"loaded{s}") for s in range(2)]
        stored = [sem(f"stored{s}") for s in range(2)]
        qlat, ql_done, z_done, logit, biased, shifted, p_done, turned, pT_done, lat, lat_done, rden, pv, out = (
            sem(n) for n in ("qlat", "ql", "z", "logit", "biased", "shift", "p", "turned", "pT", "lat",
                             "lat_copied", "rden", "pv", "out"))
        bodies, per = DSA_HEADS // 2, 2 * NT
        zs = lambda pos, lo, hi: k.psum[:, 1024 * (pos % 2) + lo:1024 * (pos % 2) + hi]
        col = lambda name, pos: st[name][:, pos:pos + 1]
        with nc.Block() as block:
            @block.sync
            def _(sp):
                sp.dma_start(far[:, :], rows(rel_last)).then_inc(far_in, 16)

                def load(j, s):
                    h = 2 * j + s
                    reached(sp, out, NT * (h - 1))
                    sp.dma_start(q[s][:, :], qbT[ds(h * HD, HD), :]).then_inc(loaded[s], 16)
                    sp.dma_start(uk[s][:, :], w_uk[h, :, :]).then_inc(loaded[s], 16)
                    sp.dma_start(uv[s][:, :], w_uv[h, :, :]).then_inc(loaded[s], 16)
                    sp.dma_start(band[s][:, :], bands(h)).then_inc(loaded[s], 16)

                def store(j, s):
                    h = 2 * j + s
                    sp.wait_ge(out, NT * (h + 1))
                    sp.dma_start(mix[:, ds(h * HD, HD)].rearrange("(i p) d -> p i d", p=P), o[s][:, :, :])\
                      .then_inc(stored[s], 16)
                load(0, 0)
                load(0, 1)

                def body(j):
                    for s in range(2):
                        load(j + 1, s)
                        store(j, s)
                looped(sp, bodies - 1, body)
                if ahead:
                    ahead.early(sp, "load", 2)
                for s in range(2):
                    store(bodies - 1, s)
                for s in range(2):
                    sp.wait_ge(stored[s], 16 * bodies)

            @block.tensor
            def _(pe):
                def scores(n, pos, j):
                    s, i = pos // NT, pos % NT
                    L = (i + 1) * P
                    if i == 0:
                        h = 2 * j + s
                        pe.wait_ge(loaded[s], 64 * (j + 1))
                        reached(pe, pT_done, n - 1)
                        for half in range(2):
                            mm = pe.matmul(k.bank[4 + half], uk[s][:, :], q[s][:, half * 512:half * 512 + 512],
                                           start=True, stop=True)
                        mm.then_inc(qlat, 1)
                        pe.wait_ge(ql_done, h + 1)
                    reached(pe, biased, n - 1)
                    for a in range(0, L, 512):
                        b = min(L, a + 512)
                        mm = pe.matmul(zs(pos, a, b), ql[s][:, i * P:(i + 1) * P], cT[:, a:b],
                                       start=True, stop=True)
                    mm.then_inc(z_done, 1)

                def turn_p(n, pos, j):
                    i = pos % NT
                    pe.wait_ge(p_done, n + 1)
                    reached(pe, pT_done, n)
                    for b in range(i + 1):
                        mm = pe.transpose(k.bank[4 + b // 4][:, (b % 4) * P:(b % 4 + 1) * P],
                                          p[pos % 2][:, b * P:(b + 1) * P], k.ident[:, :])
                    mm.then_inc(turned, 1)

                def latents(n, pos, j):
                    i = pos % NT
                    pe.wait_ge(pT_done, n + 1)
                    reached(pe, lat_done, n)
                    for b in range(i + 1):
                        mm = pe.matmul(k.bank[6][:, 0:P], cn[:, b, :], pT_[pos % 2][:, b, :],
                                       start=b == 0, stop=b == i)
                    mm.then_inc(lat, 1)

                def values(n, pos, j):
                    s = pos // NT
                    pe.wait_ge(lat_done, n + 1)
                    reached(pe, out, n)
                    pe.matmul(k.bank[7][:, 0:HD], ol[pos % 2][:, :], uv[s][:, :], start=True, stop=True)\
                      .then_inc(pv, 1)
                pipelined(pe, bodies, per, [(2, turn_p), (0, scores), (3, latents), (4, values)])

            @block.scalar
            def _(act):
                def scale_q(n, pos, j):
                    s, i = pos // NT, pos % NT
                    if i == 0:
                        act.wait_ge(qlat, 2 * j + s + 1)
                        act.activation(ql[s][:, :], k.psum[:, 2048:3072], ACT.Copy, scale=HD ** -0.5)\
                           .then_inc(ql_done, 1)

                def weights(n, pos, j):
                    L = (pos % NT + 1) * P
                    act.wait_ge(shifted, n + 1)
                    act.activation(p[pos % 2][:, 0:L], p[pos % 2][:, 0:L], ACT.Exp, bias=col("shift", pos),
                                   accum_out=col("den", pos)).then_inc(p_done, 1)

                def copy_turned(n, pos, j):
                    i = pos % NT
                    act.wait_ge(turned, n + 1)
                    reached(act, lat, n - 1)
                    act.activation(pT_[pos % 2][:, 0:i + 1, :],
                                   k.psum[:, 2048:2048 + (i + 1) * P].rearrange("p (a b) -> p a b", b=P),
                                   ACT.Copy).then_inc(pT_done, 1)
                pipelined(act, bodies, per, [(2, copy_turned), (0, scale_q), (1, weights)])

            @block.vector
            def _(dve):
                dve.wait_ge(far_in, 16)

                def logits(n, pos, j):
                    s, i = pos // NT, pos % NT
                    L = (i + 1) * P
                    near = 2 * P if i else P
                    f = L - near
                    w, m = p[pos % 2], mask[:, i, :]
                    dve.wait_ge(z_done, n + 1)
                    if i == 0:
                        dve.wait_ge(loaded[s], 64 * (j + 1))
                    reached(dve, turned, n - 1)
                    dve.tensor_tensor(w[:, f:L], zs(pos, f, L), m[:, f:L], ALU.add).then_inc(logit, 1)
                    if f:
                        dve.scalar_tensor_tensor(out=w[:, 0:f], in0=zs(pos, 0, f),
                                                 scalar=far[:, ds(2 * j + s, 1)], in1=m[:, 0:f],
                                                 op0=ALU.add, op1=ALU.add)
                    dve.wait_ge(logit, n + 1)
                    dve.tensor_tensor(w[:, f:L], w[:, f:L], band[s][:, 2 * P - near:2 * P], ALU.add)\
                       .then_inc(biased, 1)
                    dve.wait_ge(biased, n + 1)
                    dve.tensor_reduce(col("shift", pos), w[:, 0:L], AX, ALU.max, negate=True).then_inc(shifted, 1)

                def copy_latents(n, pos, j):
                    dve.wait_ge(lat, n + 1)
                    reached(dve, pv, n - 1)
                    dve.tensor_copy(ol[pos % 2][:, :], k.bank[6][:, 0:P]).then_inc(lat_done, 1)

                def output(n, pos, j):
                    s, i = pos // NT, pos % NT
                    dve.wait_ge(p_done, n + 1)
                    dve.reciprocal(col("rden", pos), col("den", pos)).then_inc(rden, 1)
                    dve.wait_ge(rden, n + 1)
                    dve.wait_ge(pv, n + 1)
                    if i == 0:
                        dve.wait_ge(stored[s], 16 * j)
                    dve.tensor_scalar(o[s][:, i, :], k.bank[7][:, 0:HD], col("rden", pos), None, ALU.mult)\
                       .then_inc(out, 1)
                pipelined(dve, bodies, per, [(0, logits), (3, copy_latents), (4, output)])



def memory_linears(k, w_kv):
    n = D // CW
    return [Linear(k, w_kv[off:off + n, :, :], n, kind, tokens=MEM) for kind, off in (("T", 0), ("N", n))]


def memory_attention(k, qT, kT_dram, v_dram, mix, ahead=None):
    nc = k.nc
    KF = MEM_HD // P
    with ExitStack() as c:
        sem = lambda n: k.sem("xa_" + n)
        kT = k.sb(c, "xa_kT", [P, KT, MEM])
        v = k.sb(c, "xa_v", [P, MEM // P, D])
        q = [k.sb(c, f"xa_q{s}", [P, KF, S]) for s in range(2)]
        p = [k.sb(c, f"xa_p{s}", [P, MEM]) for s in range(2)]
        pT_ = [k.sb(c, f"xa_pT{s}", [P, 2, P]) for s in range(2)]
        st = {n: k.sb(c, "xa_" + n, [P, 4 * NT]) for n in ("max", "shift", "den", "rden")}
        o = [k.sb(c, f"xa_o{s}", [P, NT, MEM_HD]) for s in range(2)]
        kv_in = sem("kv_in")
        loaded = [sem(f"loaded{s}") for s in range(2)]
        stored = [sem(f"stored{s}") for s in range(2)]
        z_done, maxed, shifted, p_done, turned, pT_done, rden, pv, out = (
            sem(n) for n in ("z", "max", "shift", "p", "turned", "pT", "rden", "pv", "out"))
        col = lambda name, n: st[name][:, n:n + 1]
        N = MEM_HEADS * NT
        with nc.Block() as block:
            @block.sync
            def _(sp):
                sp.dma_start(kT[:, :, :], kT_dram.rearrange("(a p) m -> p a m", p=P)).then_inc(kv_in, 16)
                sp.dma_start(v[:, :, :], v_dram.rearrange("(b p) n -> p b n", p=P)).then_inc(kv_in, 16)
                for h in range(MEM_HEADS + 1):
                    if h < MEM_HEADS:
                        reached(sp, out, NT * (h - 1))
                        sp.dma_start(q[h % 2][:, :, :], qT[h * MEM_HD:(h + 1) * MEM_HD, :]
                                     .rearrange("(a p) t -> p a t", p=P)).then_inc(loaded[h % 2], 16)
                    if ahead and h == 2:
                        ahead.early(sp, "load", 2)
                    if h:
                        g = h - 1
                        sp.wait_ge(out, NT * h)
                        sp.dma_start(mix[:, g * MEM_HD:(g + 1) * MEM_HD].rearrange("(i p) d -> p i d", p=P),
                                     o[g % 2][:, :, :]).then_inc(stored[g % 2], 16)
                for s in range(2):
                    sp.wait_ge(stored[s], 16 * MEM_HEADS // 2)

            @block.tensor
            def _(pe):
                def scores(n, pos, j):
                    h, i = n // NT, n % NT
                    pe.wait_ge(loaded[h % 2], 16 * (h // 2 + 1))
                    reached(pe, p_done, n - 1)
                    for a in range(KF):
                        mm = pe.matmul(k.bank[n % 2][:, 0:MEM], q[h % 2][:, a, i * P:(i + 1) * P],
                                       kT[:, KF * h + a, :], start=a == 0, stop=a == KF - 1)
                    mm.then_inc(z_done, 1)

                def turn_p(n, pos, j):
                    pe.wait_ge(p_done, n + 1)
                    reached(pe, pT_done, n - 1)
                    for b in range(2):
                        mm = pe.transpose(k.bank[2 + n % 2][:, b * P:(b + 1) * P], p[n % 2][:, b * P:(b + 1) * P],
                                          k.ident[:, :])
                    mm.then_inc(turned, 1)

                def values(n, pos, j):
                    h = n // NT
                    pe.wait_ge(pT_done, n + 1)
                    reached(pe, out, n - 1)
                    for b in range(2):
                        mm = pe.matmul(k.bank[4 + n % 2][:, 0:MEM_HD], pT_[n % 2][:, b, :],
                                       v[:, b, h * MEM_HD:(h + 1) * MEM_HD], start=b == 0, stop=b == 1)
                    mm.then_inc(pv, 1)
                pe.wait_ge(kv_in, 32)
                pipelined(pe, 1, N, [(0, scores), (2, turn_p), (3, values)])

            @block.scalar
            def _(act):
                def weights(n, pos, j):
                    act.wait_ge(shifted, n + 1)
                    reached(act, turned, n - 1)
                    act.activation(p[n % 2][:, :], k.bank[n % 2][:, 0:MEM], ACT.Exp, bias=col("shift", n),
                                   scale=MEM_HD ** -0.5, accum_out=col("den", n)).then_inc(p_done, 1)

                def copy_turned(n, pos, j):
                    act.wait_ge(turned, n + 1)
                    reached(act, pv, n - 1)
                    act.activation(pT_[n % 2][:, :, :], k.bank[2 + n % 2][:, 0:MEM]
                                   .rearrange("p (a b) -> p a b", b=P), ACT.Copy).then_inc(pT_done, 1)
                pipelined(act, 1, N, [(0, weights), (1, copy_turned)])

            @block.vector
            def _(dve):
                def maximum(n, pos, j):
                    dve.wait_ge(z_done, n + 1)
                    dve.tensor_reduce(col("max", n), k.bank[n % 2][:, 0:MEM], AX, ALU.max).then_inc(maxed, 1)
                    dve.wait_ge(maxed, n + 1)
                    dve.tensor_scalar(col("shift", n), col("max", n), -(MEM_HD ** -0.5), None, ALU.mult)\
                       .then_inc(shifted, 1)

                def output(n, pos, j):
                    h, i = n // NT, n % NT
                    dve.wait_ge(p_done, n + 1)
                    dve.reciprocal(col("rden", n), col("den", n)).then_inc(rden, 1)
                    dve.wait_ge(rden, n + 1)
                    dve.wait_ge(pv, n + 1)
                    reached(dve, stored[h % 2], 16 * (h // 2))
                    dve.tensor_scalar(o[h % 2][:, i, :], k.bank[4 + n % 2][:, 0:MEM_HD], col("rden", n), None,
                                      ALU.mult).then_inc(out, 1)
                pipelined(dve, 1, N, [(0, maximum), (3, output)])



def build(nc, d, out):
    with ExitStack() as ctx:
        k = Kernel(nc, ctx, d)
        p1T = k.scratch("p1T", [1280, S])
        p1V = k.scratch("p1V", [S, 512])
        p1G = k.scratch("p1G", [S, GLA_IN])
        p2T = k.scratch("p2T", [1792, S])
        p2N = k.scratch("p2N", [S, 200])
        xqT = k.scratch("xqT", [D, S])
        mkT = k.scratch("mkT", [D, MEM])
        mv = k.scratch("mv", [MEM, D])
        mix = k.scratch("mix", [S, D])
        bands = k.scratch("bands", [SWA_HEADS + DSA_HEADS, P, BAND])

        def halves(c, n=S):
            return (k.sb(c, "h_hi", [P, KT, n], R), k.sb(c, "h_lo", [P, KT, n], R))

        setup(k)
        mod2 = k.scratch("mod2", [3, D])
        with ExitStack() as c:
            gate1 = k.sb(c, "gate1", [P, D])
            with ExitStack() as c2:
                hh, hl = halves(c2)
                lin_T = Linear(k, d["w_in_T"], 5, "T", hh, hl)
                lin_V = Linear(k, d["w_in_V"], 2, "N", hh, hl)
                lin_G = Linear(k, d["w_in_G"], SB_HEADS, "N", hh, hl, width=GLA_IN // SB_HEADS, banks=NT)
                with ExitStack() as c3:
                    mod = k.sb(c3, "mod", [P, 6 * D])
                    modulation(k, mod, gate1)
                    shift1, scale1, _, shift2, scale2, gate2 = (mod[:, j * D:(j + 1) * D] for j in range(6))
                    norm(k, "n1", "rms", scale1, shift1, hh, hl, ahead=lin_T,
                         saved=((shift2, mod2[0, :]), (scale2, mod2[1, :]), (gate2, mod2[2, :])))
                project(k, "in1T", lin_T, p1T, ahead=lin_V)
                project(k, "in1V", lin_V, p1V)
                k.free_sems()
                stick_breaking(k, p1T[0:1024, :], p1V, mix[:, 0:512], lin_G, p1G)
            lin_out = Linear(k, d["w_out"], D // CW, "N")
            ffn = Slots(k, (NF1, NF1 // 2), d["w_up"], d["w_down"])
            gla(k, p1T[1024:1280, :], p1G[:, 0:GLA_IN - RANK], p1G[:, GLA_IN - RANK:GLA_IN], d["w_fg2"], d["b_fg2"],
                d["g_gla_out"], mix[:, 512:1024], ahead=lin_out)
            with ExitStack() as c2:
                lin_out.hh, lin_out.hl = hh, hl = halves(c2)
                turn(k, "t1", mix, hh, hl, ahead=lin_out)
                project_residual(k, "out1", lin_out, gate=gate1[:, :], ahead=ffn)
        k.free_sems()
        with ExitStack() as c:
            g2 = k.sb(c, "gate2", [P, D])
            load_rows(k, mod2[2, :], g2)
            hh, hl = halves(c)
            norm(k, "n2", "rms", mod2[1, :], mod2[0, :], hh, hl, ahead=ffn)
            ffn_conv(k, ffn, d["w_up"], d["w_down"], d["conv"], hh, hl, g2)

        with ExitStack() as c:
            cn = k.sb(c, "latents", [P, NT, DC])
            cT = k.sb(c, "latentsT", [DC, S])
            score = k.sb(c, "index_score", [P, NT, S])
            with ExitStack() as c2:
                hh, hl = halves(c2)
                lin_T1 = Linear(k, d["w_in2_T1"], 3, "T", hh, hl)
                lin_N = Linear(k, d["w_in2_N"], 1, "N", hh, hl, width=200)
                lin_T2 = Linear(k, d["w_in2_T2"], 4, "T", hh, hl)
                lin_mk, lin_mv = memory_linears(k, d["xa_wkv"])
                norm(k, "n3", "rms", d["g_final"], None, ahead=lin_T1)
                norm(k, "n4", "ln", d["ln_emb_g"], d["ln_emb_b"], hh, hl, ahead=lin_T1)
                project(k, "in2T", lin_T1, p2T[0:768, :], bias=d["b_in2_T1"], ahead=lin_N)
                project(k, "in2N", lin_N, p2N, bias=d["b_in2_N"])
                k.free_sems()
                with ExitStack() as c3:
                    ikT = k.sb(c3, "index_kT", [HD, S])
                    iw = k.sb(c3, "index_w", [P, NT, DSA_HEADS])
                    sparse_prepare(k, p2T[512:640, :], p2N[:, 128:192], p2N[:, 192:200], cn, cT, ikT, iw)
                    index_scores(k, p2T[0:512, :], ikT, iw, score, ahead=lin_T2)
                select_top(k, score, ((lin_T2, p2T[768:1792, :], d["b_in2_T2"]), (lin_mk, mkT, d["xa_bk"]),
                                      (lin_mv, mv, None)), d["memT"], d["xa_bv"], hh, hl, bands)
            k.free_sems()
            window_attention(k, p2T[768:1280, :], p2T[640:768, :], p2N[:, 0:128], lambda h: band_of(bands, h),
                             d["sinks"], mix[:, 0:512])
            lin_o = Linear(k, d["w_o"], D // CW, "N")
            lin_q = Linear(k, d["xa_wq"], D // CW, "T")
            sparse_attention(k, p2T[1280:1792, :], d["w_ukT"], d["w_uv"], cn, cT, score,
                             lambda h: band_of(bands, SWA_HEADS + h), d["rel_last"], mix[:, 512:1024], ahead=lin_o)
        k.free_sems()
        with ExitStack() as c:
            hh, hl = halves(c)
            lin_o.hh = lin_q.hh = hh
            lin_o.hl = lin_q.hl = hl
            turn(k, "t2", mix, hh, hl, ahead=lin_o)
            project_residual(k, "out2", lin_o, bias=d["b_o"], ahead=lin_q)
            norm(k, "n5", "ln", d["ln1_g"], d["ln1_b"], hh, hl, ahead=lin_q)
            project(k, "xq", lin_q, xqT, bias=d["xa_bq"])
        with ExitStack() as c:
            lin_xo = Linear(k, d["xa_wo"], D // CW, "N")
            ffn = Slots(k, (F2C, F2C), d["w_up2"], d["w_down2"])
            memory_attention(k, xqT, mkT, mv, mix, ahead=lin_xo)
        k.free_sems()
        with ExitStack() as c:
            lin_xo.hh, lin_xo.hl = hh, hl = halves(c)
            turn(k, "t4", mix, hh, hl, ahead=lin_xo)
            project_residual(k, "out3", lin_xo, bias=d["xa_bo"], ahead=ffn)
            norm(k, "n6", "ln", d["ln2_g"], d["ln2_b"], hh, hl, ahead=ffn)
            ffn_squared_relu(k, ffn, d["w_up2"], d["w_down2"], d["b_up2"], d["b_down2"], hh, hl)
        norm(k, "n7", "ln", d["ln3_g"], d["ln3_b"], out=out)


def load_rows(k, src, tile):
    loaded = k.sem("rows_loaded")
    with k.nc.Block() as block:
        @block.sync
        def _(sp):
            sp.dma_start(tile[:, :], rows(src)).then_inc(loaded, 16)
            sp.wait_ge(loaded, 16)



def chunked(w, width=CW):
    n = w.shape[1] // width
    return np.ascontiguousarray(w.reshape(KT, P, n, width).transpose(2, 1, 0, 3)).reshape(n, P, KT * width)


def row_chunked(w):
    return np.ascontiguousarray(w.reshape(-1, 2, P, D).transpose(0, 2, 1, 3)).reshape(-1, P, 2 * D)


def columns(b):
    return np.ascontiguousarray(b.reshape(-1, P).T)


def laid_out(i):
    i = {name: np.asarray(a) for name, a in i.items()}
    w = i["w_in"][0]
    q, kk, v, gq, gk, gv, gg, gf = np.split(w, np.cumsum([512, 512, 512, 256, 256, 512, 512]), axis=1)
    w2 = i["w_in_2"][0]
    cuts = np.cumsum([512, 128, 128, 512, 128, 512, 64])
    qa, ka, va, qb, cb, iq, ik, iw = np.split(w2, cuts, axis=1)
    bqa, bka, bva, bqb, bcb, biq, bik, biw = np.split(i["b_in_2"][0], cuts)
    up = i["w_up"][0].reshape(D, 2, NF1, P).transpose(0, 2, 1, 3).reshape(D, 2 * NF1 * P)
    conv = np.concatenate([i["w_conv"][0], i["b_conv"]], 0).reshape(4, 2, NF1, P)
    return {
        "x": i["x"][0], "c": columns(i["c"][0]), "w_ada": chunked(i["w_ada"][0]), "b_ada": i["b_ada"][0],
        "g_norm1": i["g_norm1"][0], "g_norm2": i["g_norm2"][0],
        "w_in_T": chunked(np.concatenate([q, kk, gq], 1)), "w_in_V": chunked(v),
        "w_in_G": chunked(np.concatenate([gk, gv, gg, gf], 1), GLA_IN // SB_HEADS), "w_fg2": i["w_fg2"][0], "b_fg2": i["b_fg2"][0],
        "g_gla_out": i["g_gla_out"][0], "w_out": chunked(i["w_out"][0]), "w_up": chunked(up),
        "conv": np.ascontiguousarray(conv.transpose(3, 2, 1, 0)), "w_down": row_chunked(i["w_down"][0]),
        "g_final": i["g_final"],
        "memT": np.ascontiguousarray(i["mem_2"][0].reshape(MEM, KT, P).transpose(2, 1, 0)).reshape(P, KT * MEM), "ln_emb_g": i["ln_emb_g_2"], "ln_emb_b": i["ln_emb_b_2"],
        "w_in2_T1": chunked(np.concatenate([iq, cb, ka], 1)), "b_in2_T1": columns(np.concatenate([biq, bcb, bka])),
        "w_in2_T2": chunked(np.concatenate([qa, qb], 1)), "b_in2_T2": columns(np.concatenate([bqa, bqb])),
        "w_in2_N": chunked(np.concatenate([va, ik, iw], 1), 200), "b_in2_N": np.concatenate([bva, bik, biw]),
        "sinks": i["swa_sinks_2"][0], "kv_g": i["dsa_kv_norm_g_2"][0], "ik_g": i["idx_k_ln_g_2"][0],
        "ik_b": i["idx_k_ln_b_2"][0], "w_ukT": np.ascontiguousarray(i["dsa_w_uk_2"][0].transpose(0, 2, 1)),
        "w_uv": i["dsa_w_uv_2"][0], "rel_bias": i["rel_bias_2"],
        "rel_last": np.ascontiguousarray(i["rel_bias_2"][BUCKETS - 1, SWA_HEADS:]),
        "buckets": np.stack([distance_buckets(P), distance_buckets(None)]),
        "w_o": chunked(i["w_o_2"][0]), "b_o": i["b_o_2"][0], "ln1_g": i["ln1_g_2"][0], "ln1_b": i["ln1_b_2"][0],
        "xa_wq": chunked(i["xa_wq_2"][0]), "xa_bq": columns(i["xa_bq_2"][0]), "xa_wkv": chunked(i["xa_wkv_2"][0]),
        "xa_bk": columns(i["xa_bkv_2"][0][:D]), "xa_bv": np.ascontiguousarray(i["xa_bkv_2"][0][D:]),
        "xa_wo": chunked(i["xa_wo_2"][0]), "xa_bo": i["xa_bo_2"][0], "ln2_g": i["ln2_g_2"][0],
        "ln2_b": i["ln2_b_2"][0], "w_up2": chunked(i["w_up_2"][0]), "b_up2": columns(i["b_up_2"][0]),
        "w_down2": row_chunked(i["w_down_2"][0]), "b_down2": i["b_down_2"][0], "ln3_g": i["ln3_g_2"][0],
        "ln3_b": i["ln3_b_2"][0],
    }


def kernel(**inputs):
    import concourse.bacc as bacc
    from concourse.bass_utils import run_bass_kernel_spmd

    nc = bacc.Bacc("TRN2", target_bir_lowering=False, num_devices=1)
    arrays = {name: np.ascontiguousarray(a) for name, a in laid_out(inputs).items()}
    dram = {name: nc.dram_tensor(f"in_{name}", a.shape, F, kind="ExternalInput").ap() for name, a in arrays.items()}
    out = nc.dram_tensor("out_0_dram", (S, D), F, kind="ExternalOutput").ap()
    build(nc, dram, out)
    result = run_bass_kernel_spmd(nc, [{f"in_{name}": a for name, a in arrays.items()}], core_ids=[0])
    return result.results[0]["out_0_dram"].reshape(1, S, D)
```
